# Optimizing a Trainium2 kernel written in Bass

```python
import jax
import jax.numpy as jnp
from jax import lax
import math
import jax, jax.numpy as jnp
import numpy as np

D_MODEL = 1024
BATCH = 1
SEQ = 512
DEPTH = 1

HEAD_DIM = 64
NSA_HEADS = 8
NSA_KV = 2
SWA_HEADS = 8
SWA_KV = 1
CMP_STRIDE = 16
CMP_LEN = 2 * CMP_STRIDE
CMP_HIDDEN = 256
SEL_LEN = 64
SEL_TOPN = 16
SEL_LOCAL = 2
NSA_WINDOW = 512
SWA_WINDOW = 128
Q_BLOCK = 128
D_FF = 2816
ROPE_THETA = 10000.0
RMS_EPS = 1e-6
FFN_HALF = 0.5
NEG_INF = -1e30
FORCE = 1e9

NSA_Q_W = NSA_HEADS * HEAD_DIM
NSA_KV_W = NSA_KV * HEAD_DIM
NSA_GATE_W = 3 * NSA_HEADS
SWA_Q_W = SWA_HEADS * HEAD_DIM
SWA_KV_W = SWA_KV * HEAD_DIM
IN_WIDTHS = (NSA_Q_W, NSA_KV_W, NSA_KV_W, NSA_KV_W, NSA_KV_W, NSA_KV_W, NSA_KV_W, NSA_GATE_W,
             SWA_Q_W, SWA_KV_W, SWA_KV_W, D_MODEL, D_MODEL)


def _split_points():
    pts, acc = [], 0
    for w in IN_WIDTHS[:-1]:
        acc += w
        pts.append(acc)
    return pts

def _rmsnorm(x, g):
    xf = x.astype(jnp.float32)
    y = xf * lax.rsqrt(jnp.mean(xf * xf, axis=-1, keepdims=True) + RMS_EPS)
    return (y * g.astype(jnp.float32)).astype(x.dtype)

def _swiglu(x, w_gate, w_up, w_down):
    return (jax.nn.silu(x @ w_gate) * (x @ w_up)) @ w_down

def _rope(x, pos):
    half = HEAD_DIM // 2
    inv_freq = ROPE_THETA ** (-jnp.arange(half, dtype=jnp.float32) / half)
    ang = pos.astype(jnp.float32)[..., None] * inv_freq
    cos = jnp.cos(ang)[:, :, None, :]
    sin = jnp.sin(ang)[:, :, None, :]
    xf = x.astype(jnp.float32)
    x1, x2 = xf[..., :half], xf[..., half:]
    return jnp.concatenate([x1 * cos - x2 * sin, x2 * cos + x1 * sin], axis=-1).astype(x.dtype)

def _banded_attention(q, k, v, window, sink):
    B, S, H, D = q.shape
    G = k.shape[2]
    R = H // G
    nb = S // Q_BLOCK
    pad = -(-window // Q_BLOCK) * Q_BLOCK
    L = pad + Q_BLOCK
    kp = jnp.pad(k, ((0, 0), (pad, 0), (0, 0), (0, 0)))
    vp = jnp.pad(v, ((0, 0), (pad, 0), (0, 0), (0, 0)))
    idx = jnp.arange(nb)[:, None] * Q_BLOCK + jnp.arange(L)[None, :]
    kb = kp[:, idx]
    vb = vp[:, idx]
    qb = q.reshape(B, nb, Q_BLOCK, G, R, D)
    s = jnp.einsum('bnqgrd,bnkgd->bngrqk', qb, kb).astype(jnp.float32) * (D ** -0.5)
    qpos = jnp.arange(nb)[:, None] * Q_BLOCK + jnp.arange(Q_BLOCK)[None, :]
    kpos = idx - pad
    diff = qpos[:, :, None] - kpos[:, None, :]
    mask = (diff >= 0) & (diff < window) & (kpos[:, None, :] >= 0)
    s = jnp.where(mask[None, :, None, None], s, NEG_INF)
    if sink is None:
        p = jax.nn.softmax(s, axis=-1)
    else:
        sk = sink.astype(jnp.float32).reshape(G, R)[None, None, :, :, None, None]
        m = jnp.maximum(jnp.max(s, axis=-1, keepdims=True), sk)
        e = jnp.exp(s - m)
        p = e / (jnp.sum(e, axis=-1, keepdims=True) + jnp.exp(sk - m))
    o = jnp.einsum('bngrqk,bnkgd->bnqgrd', p.astype(vb.dtype), vb)
    return o.reshape(B, S, H, D)

def _compress(kv, pe, w1, w2):
    B, S, G, D = kv.shape
    c = kv.reshape(B, S // CMP_STRIDE, CMP_STRIDE, G, D)
    blocks = jnp.concatenate([c[:, :-1], c[:, 1:]], axis=2)
    blocks = blocks + pe[None, None, :, None, :]
    n_cmp = blocks.shape[1]
    flat = blocks.transpose(0, 1, 3, 2, 4).reshape(B, n_cmp, G, CMP_LEN * D)
    return jax.nn.gelu(flat @ w1) @ w2

def _nsa(q, k_cmp, v_cmp, k_slc, v_slc, k_win, v_win, gates, pos, pe_k, wk1, wk2, pe_v, wv1, wv2):
    B, S, H, D = q.shape
    G = NSA_KV
    R = H // G
    scale = D ** -0.5
    n_sel = S // SEL_LEN
    n_top = min(SEL_TOPN, n_sel)
    nb = S // Q_BLOCK
    qg = q.reshape(B, S, G, R, D)
    t = jnp.arange(S)

    kc = _compress(k_cmp, pe_k, wk1, wk2)
    vc = _compress(v_cmp, pe_v, wv1, wv2)
    n_cmp = kc.shape[1]
    kc = _rope(kc, pos[:, CMP_LEN - 1::CMP_STRIDE])
    end = jnp.arange(n_cmp) * CMP_STRIDE + CMP_LEN - 1
    vis = end[None, :] <= t[:, None]
    s = jnp.einsum('bsgrd,bcgd->bgrsc', qg, kc).astype(jnp.float32) * scale
    s = jnp.where(vis, s, NEG_INF)
    p_cmp = jnp.where(vis, jax.nn.softmax(s, axis=-1), 0.0)
    o_cmp = jnp.einsum('bgrsc,bcgd->bsgrd', p_cmp.astype(vc.dtype), vc)

    cs = jnp.arange(n_cmp) * CMP_STRIDE
    ss = jnp.arange(n_sel) * SEL_LEN
    overlap = jnp.clip(jnp.minimum(cs[:, None] + CMP_LEN, ss[None, :] + SEL_LEN)
                       - jnp.maximum(cs[:, None], ss[None, :]), 0, None).astype(jnp.float32) / CMP_LEN
    imp = jnp.einsum('bgrsc,cj->bgsj', p_cmp, overlap)
    blk = jnp.arange(n_sel)[None, :]
    tb = (t // SEL_LEN)[:, None]
    forced = (blk == 0) | ((tb - blk >= 0) & (tb - blk < SEL_LOCAL))
    imp = jnp.where(forced, FORCE, jnp.where(blk > tb, -FORCE, imp))
    _, sel = lax.top_k(imp, n_top)

    kT = k_slc.transpose(0, 2, 1, 3)
    vT = v_slc.transpose(0, 2, 1, 3)
    offs = jnp.arange(SEL_LEN)
    gather = jax.vmap(jax.vmap(lambda a, i: a[i]))

    def one_block(args):
        qb, selb, tq = args
        idx = (selb[..., None] * SEL_LEN + offs).reshape(B, G, Q_BLOCK, n_top * SEL_LEN)
        kb = gather(kT, idx)
        vb = gather(vT, idx)
        sc = jnp.einsum('bqgrd,bgqtd->bgrqt', qb, kb).astype(jnp.float32) * scale
        m = (idx <= tq[None, None, :, None])[:, :, None]
        pr = jax.nn.softmax(jnp.where(m, sc, NEG_INF), axis=-1)
        return jnp.einsum('bgrqt,bgqtd->bqgrd', pr.astype(vb.dtype), vb)

    qs = qg.reshape(B, nb, Q_BLOCK, G, R, D).transpose(1, 0, 2, 3, 4, 5)
    sels = sel.reshape(B, G, nb, Q_BLOCK, n_top).transpose(2, 0, 1, 3, 4)
    tqs = t.reshape(nb, Q_BLOCK)
    o_slc = lax.map(one_block, (qs, sels, tqs))
    o_slc = o_slc.transpose(1, 0, 2, 3, 4, 5).reshape(B, S, G, R, D)

    o_win = _banded_attention(q, k_win, v_win, NSA_WINDOW, None).reshape(B, S, G, R, D)

    g = jax.nn.sigmoid(gates.astype(jnp.float32)).reshape(B, S, 3, G, R, 1)
    o = (g[:, :, 0] * o_cmp.astype(jnp.float32) + g[:, :, 1] * o_slc.astype(jnp.float32)
         + g[:, :, 2] * o_win.astype(jnp.float32))
    return o.astype(q.dtype).reshape(B, S, H * D)

def first_inputs(seed: int = 0) -> dict:
    key = jax.random.key(seed)
    ks = jax.random.split(key, 24)
    f32 = jnp.float32

    def w(k, shape, fan_in):
        return jax.random.normal(k, shape, f32) * fan_in ** -0.5

    def gain(k, shape):
        return 1.0 + 0.02 * jax.random.normal(k, shape, f32)

    w_in_width = sum(IN_WIDTHS)
    return {
        'x': jax.random.normal(ks[0], (BATCH, SEQ, D_MODEL), f32),
        'positions': jnp.broadcast_to(jnp.arange(SEQ, dtype=jnp.int32), (BATCH, SEQ)),
        'norm_ffn1': gain(ks[1], (DEPTH, D_MODEL)),
        'ffn1_gate': w(ks[2], (DEPTH, D_MODEL, D_FF), D_MODEL),
        'ffn1_up': w(ks[3], (DEPTH, D_MODEL, D_FF), D_MODEL),
        'ffn1_down': w(ks[4], (DEPTH, D_FF, D_MODEL), D_FF),
        'norm_mix': gain(ks[5], (DEPTH, D_MODEL)),
        'w_in': w(ks[6], (DEPTH, D_MODEL, w_in_width), D_MODEL),
        'cmp_pe_k': 0.1 * jax.random.normal(ks[7], (DEPTH, CMP_LEN, HEAD_DIM), f32),
        'cmp_k_w1': w(ks[8], (DEPTH, CMP_LEN * HEAD_DIM, CMP_HIDDEN), CMP_LEN * HEAD_DIM),
        'cmp_k_w2': w(ks[9], (DEPTH, CMP_HIDDEN, HEAD_DIM), CMP_HIDDEN),
        'cmp_pe_v': 0.1 * jax.random.normal(ks[10], (DEPTH, CMP_LEN, HEAD_DIM), f32),
        'cmp_v_w1': w(ks[11], (DEPTH, CMP_LEN * HEAD_DIM, CMP_HIDDEN), CMP_LEN * HEAD_DIM),
        'cmp_v_w2': w(ks[12], (DEPTH, CMP_HIDDEN, HEAD_DIM), CMP_HIDDEN),
        'swa_sinks': jax.random.normal(ks[13], (DEPTH, SWA_HEADS), f32),
        'w_branch_a': w(ks[14], (DEPTH, NSA_Q_W, D_MODEL), NSA_Q_W),
        'w_branch_b': w(ks[15], (DEPTH, SWA_Q_W, D_MODEL), SWA_Q_W),
        'w_out': w(ks[16], (DEPTH, D_MODEL, D_MODEL), D_MODEL),
        'norm_ffn2': gain(ks[17], (DEPTH, D_MODEL)),
        'ffn2_gate': w(ks[18], (DEPTH, D_MODEL, D_FF), D_MODEL),
        'ffn2_up': w(ks[19], (DEPTH, D_MODEL, D_FF), D_MODEL),
        'ffn2_down': w(ks[20], (DEPTH, D_FF, D_MODEL), D_FF),
        'norm_final': gain(ks[21], (D_MODEL,)),
    }

def first_block(x, positions, norm_ffn1, ffn1_gate, ffn1_up, ffn1_down, norm_mix, w_in,
              cmp_pe_k, cmp_k_w1, cmp_k_w2, cmp_pe_v, cmp_v_w1, cmp_v_w2, swa_sinks,
              w_branch_a, w_branch_b, w_out, norm_ffn2, ffn2_gate, ffn2_up, ffn2_down, norm_final):
    B, S, _ = x.shape
    pts = _split_points()
    h = x
    for i in range(DEPTH):
        h = h + FFN_HALF * _swiglu(_rmsnorm(h, norm_ffn1[i]), ffn1_gate[i], ffn1_up[i], ffn1_down[i])

        u = _rmsnorm(h, norm_mix[i])
        (nq, kc, vc, ksl, vsl, kwn, vwn, ng, sq, sk, sv, ga, gb) = jnp.split(u @ w_in[i], pts, axis=-1)
        nq = _rope(nq.reshape(B, S, NSA_HEADS, HEAD_DIM), positions)
        kc = kc.reshape(B, S, NSA_KV, HEAD_DIM)
        vc = vc.reshape(B, S, NSA_KV, HEAD_DIM)
        ksl = _rope(ksl.reshape(B, S, NSA_KV, HEAD_DIM), positions)
        vsl = vsl.reshape(B, S, NSA_KV, HEAD_DIM)
        kwn = _rope(kwn.reshape(B, S, NSA_KV, HEAD_DIM), positions)
        vwn = vwn.reshape(B, S, NSA_KV, HEAD_DIM)
        o_a = _nsa(nq, kc, vc, ksl, vsl, kwn, vwn, ng, positions,
                   cmp_pe_k[i], cmp_k_w1[i], cmp_k_w2[i], cmp_pe_v[i], cmp_v_w1[i], cmp_v_w2[i])

        sq = _rope(sq.reshape(B, S, SWA_HEADS, HEAD_DIM), positions)
        sk = _rope(sk.reshape(B, S, SWA_KV, HEAD_DIM), positions)
        sv = sv.reshape(B, S, SWA_KV, HEAD_DIM)
        o_b = _banded_attention(sq, sk, sv, SWA_WINDOW, swa_sinks[i]).reshape(B, S, SWA_Q_W)

        merged = jax.nn.sigmoid(ga) * (o_a @ w_branch_a[i]) + jax.nn.sigmoid(gb) * (o_b @ w_branch_b[i])
        h = h + merged @ w_out[i]

        h = h + FFN_HALF * _swiglu(_rmsnorm(h, norm_ffn2[i]), ffn2_gate[i], ffn2_up[i], ffn2_down[i])
    return _rmsnorm(h, norm_final)


MIX_WIDTH = D_MODEL
HG_WIDTH = MIX_WIDTH // 2
HG_HEADS = 4
HG_DK = HG_WIDTH // HG_HEADS
HG_CHUNK = 64
S5_WIDTH = MIX_WIDTH - HG_WIDTH
S5_GROUP = 16
S5_GROUPS = S5_WIDTH // S5_GROUP
S5_STATE = 64
IN_WIDTH = 4 * HG_WIDTH + S5_WIDTH
PEER_HEADS = 8
PEER_NKEYS = 128
PEER_EXPERTS = PEER_NKEYS * PEER_NKEYS
PEER_TOPK = 16
PEER_QDIM = 256
PEER_HALF = PEER_QDIM // 2
PEER_TOKEN_BLOCK = 128
EPS = 1e-6


def _rmsnorm_2(x, w):
    xf = x.astype(jnp.float32)
    y = xf * lax.rsqrt(jnp.mean(xf * xf, axis=-1, keepdims=True) + EPS)
    return (y * w.astype(jnp.float32)).astype(x.dtype)

def _hgrn2(q, f_logit, i, g, lb, gn_w):
    bsz, seq, _ = q.shape
    f32 = jnp.float32
    f = lb + (1.0 - lb) * jax.nn.sigmoid(f_logit.astype(f32))
    log_f = jnp.log(f)
    k = 1.0 - f
    qs = jax.nn.silu(q.astype(f32)) * (HG_DK ** -0.5)
    v = i.astype(f32)
    n_chunks = seq // HG_CHUNK

    def to_chunks(t):
        return t.reshape(bsz, n_chunks, HG_CHUNK, HG_HEADS, HG_DK).transpose(1, 0, 3, 2, 4)

    causal = jnp.tril(jnp.ones((HG_CHUNK, HG_CHUNK), dtype=bool))[:, :, None]

    def step(state, inp):
        qc, kc, vc, lc = inp
        bcum = jnp.cumsum(lc, axis=2)
        o_inter = jnp.einsum('bhtk,bhkv->bhtv', qc * jnp.exp(bcum), state)
        diff = bcum[:, :, :, None, :] - bcum[:, :, None, :, :]
        decay = jnp.exp(jnp.where(causal, diff, -jnp.inf))
        scores = jnp.einsum('bhtk,bhsk,bhtsk->bhts', qc, kc, decay)
        o_intra = jnp.einsum('bhts,bhsv->bhtv', scores, vc)
        b_last = bcum[:, :, -1:, :]
        new_state = (jnp.exp(b_last[:, :, 0, :])[..., None] * state
                     + jnp.einsum('bhsk,bhsv->bhkv', kc * jnp.exp(b_last - bcum), vc))
        return new_state, o_inter + o_intra

    s0 = jnp.zeros((bsz, HG_HEADS, HG_DK, HG_DK), f32)
    _, o = lax.scan(step, s0, (to_chunks(qs), to_chunks(k), to_chunks(v), to_chunks(log_f)))
    o = o.transpose(1, 0, 3, 2, 4).reshape(bsz, seq, HG_HEADS, HG_DK)
    gate = jax.nn.silu(g.astype(f32)).reshape(bsz, seq, HG_HEADS, HG_DK)
    o = _rmsnorm_2(o, gn_w) * gate
    return o.reshape(bsz, seq, HG_WIDTH)

def _s5(u, a_re, a_im, log_dt, b_re, b_im, c_re, c_im, d_skip, w_glu, b_glu):
    bsz, seq, _ = u.shape
    f32 = jnp.float32
    uf = u.astype(f32).reshape(bsz, seq, S5_GROUPS, S5_GROUP)
    ar = a_re.astype(f32)
    ai = a_im.astype(f32)
    dt = jnp.exp(log_dt.astype(f32))[:, None]
    mag = jnp.exp(ar * dt)
    abar_re = mag * jnp.cos(ai * dt)
    abar_im = mag * jnp.sin(ai * dt)
    den = ar * ar + ai * ai
    nr = abar_re - 1.0
    ni = abar_im
    coef_re = ((nr * ar + ni * ai) / den)[..., None]
    coef_im = ((ni * ar - nr * ai) / den)[..., None]
    br = b_re.astype(f32)
    bi = b_im.astype(f32)
    bb_re = coef_re * br - coef_im * bi
    bb_im = coef_re * bi + coef_im * br
    bu_re = jnp.einsum('bsgh,gph->bsgp', uf, bb_re)
    bu_im = jnp.einsum('bsgh,gph->bsgp', uf, bb_im)
    a_re_t = jnp.broadcast_to(abar_re, bu_re.shape)
    a_im_t = jnp.broadcast_to(abar_im, bu_im.shape)

    def combine(e1, e2):
        a1r, a1i, x1r, x1i = e1
        a2r, a2i, x2r, x2i = e2
        return (a2r * a1r - a2i * a1i,
                a2r * a1i + a2i * a1r,
                a2r * x1r - a2i * x1i + x2r,
                a2r * x1i + a2i * x1r + x2i)

    _, _, xr, xi = lax.associative_scan(combine, (a_re_t, a_im_t, bu_re, bu_im), axis=1)
    y = (jnp.einsum('bsgp,ghp->bsgh', xr, c_re.astype(f32))
         - jnp.einsum('bsgp,ghp->bsgh', xi, c_im.astype(f32)))
    y = y.reshape(bsz, seq, S5_WIDTH) + d_skip.astype(f32) * uf.reshape(bsz, seq, S5_WIDTH)
    y = jax.nn.gelu(y, approximate=False)
    y = y * jax.nn.sigmoid(y @ w_glu.astype(f32) + b_glu.astype(f32))
    return y.astype(u.dtype)

def _peer(h, w_q, keys1, keys2, u_tab, v_tab):
    bsz, seq, d = h.shape
    tb = PEER_TOKEN_BLOCK
    blocks = h.reshape(-1, tb, d)
    kk = PEER_TOPK * PEER_TOPK

    def block(hb):
        qh = (hb @ w_q).reshape(tb, PEER_HEADS, 2, PEER_HALF)
        s1 = jnp.einsum('thd,nd->thn', qh[:, :, 0], keys1)
        s2 = jnp.einsum('thd,nd->thn', qh[:, :, 1], keys2)
        v1, i1 = lax.top_k(s1, PEER_TOPK)
        v2, i2 = lax.top_k(s2, PEER_TOPK)
        cand = (v1[..., :, None] + v2[..., None, :]).reshape(tb, PEER_HEADS, kk)
        cidx = (i1[..., :, None] * PEER_NKEYS + i2[..., None, :]).reshape(tb, PEER_HEADS, kk)
        best, pos = lax.top_k(cand, PEER_TOPK)
        eidx = jnp.take_along_axis(cidx, pos, axis=-1)
        gates = jax.nn.softmax(best.astype(jnp.float32), axis=-1).astype(hb.dtype)
        act = jax.nn.gelu(jnp.einsum('td,thkd->thk', hb, u_tab[eidx]), approximate=False)
        return jnp.einsum('thk,thkd->td', gates * act, v_tab[eidx])

    return lax.map(block, blocks).reshape(bsz, seq, d)

def second_inputs(seed: int = 0) -> dict:
    key = jax.random.key(seed)
    ks = jax.random.split(key, 26)
    f32 = jnp.float32

    def nrm(k, shape, std):
        return std * jax.random.normal(k, shape, f32)

    L = DEPTH
    D = D_MODEL
    G = S5_GROUPS
    P = S5_STATE
    return {
        'x': nrm(ks[0], (BATCH, SEQ, D), 1.0),
        'c': nrm(ks[1], (BATCH, D), 1.0),
        'ada_w': nrm(ks[2], (L, D, 6 * D), 0.5 * D ** -0.5),
        'ada_b': nrm(ks[3], (L, 6 * D), 0.01),
        'norm_mix_w': 1.0 + nrm(ks[4], (L, D), 0.02),
        'norm_ffn_w': 1.0 + nrm(ks[5], (L, D), 0.02),
        'w_in': nrm(ks[6], (L, D, IN_WIDTH), D ** -0.5),
        'w_out': nrm(ks[7], (L, MIX_WIDTH, D), MIX_WIDTH ** -0.5),
        'hg_lower_bounds': nrm(ks[8], (L + 1, HG_WIDTH), 0.1),
        'hg_gnorm_w': 1.0 + nrm(ks[9], (L, HG_DK), 0.02),
        's5_a_re': -0.5 + nrm(ks[10], (L, G, P), 0.01),
        's5_a_im': math.pi * jnp.arange(P, dtype=f32) + nrm(ks[11], (L, G, P), 0.01),
        's5_log_dt': jax.random.uniform(ks[12], (L, G), f32, math.log(1e-3), math.log(1e-1)),
        's5_b_re': nrm(ks[13], (L, G, P, S5_GROUP), (2 * S5_GROUP) ** -0.5),
        's5_b_im': nrm(ks[14], (L, G, P, S5_GROUP), (2 * S5_GROUP) ** -0.5),
        's5_c_re': nrm(ks[15], (L, G, S5_GROUP, P), 0.25),
        's5_c_im': nrm(ks[16], (L, G, S5_GROUP, P), 0.25),
        's5_d': nrm(ks[17], (L, S5_WIDTH), 0.5),
        's5_glu_w': nrm(ks[18], (L, S5_WIDTH, S5_WIDTH), S5_WIDTH ** -0.5),
        's5_glu_b': nrm(ks[19], (L, S5_WIDTH), 0.01),
        'peer_wq': nrm(ks[20], (L, D, PEER_HEADS * PEER_QDIM), D ** -0.5),
        'peer_keys1': nrm(ks[21], (L, PEER_NKEYS, PEER_HALF), PEER_HALF ** -0.5),
        'peer_keys2': nrm(ks[22], (L, PEER_NKEYS, PEER_HALF), PEER_HALF ** -0.5),
        'peer_u': nrm(ks[23], (L, PEER_EXPERTS, D), D ** -0.5),
        'peer_v': nrm(ks[24], (L, PEER_EXPERTS, D), PEER_HEADS ** -0.5),
        'final_norm_w': 1.0 + nrm(ks[25], (D,), 0.02),
    }

def second_block(x, c, ada_w, ada_b, norm_mix_w, norm_ffn_w, w_in, w_out, hg_lower_bounds,
              hg_gnorm_w, s5_a_re, s5_a_im, s5_log_dt, s5_b_re, s5_b_im, s5_c_re, s5_c_im,
              s5_d, s5_glu_w, s5_glu_b, peer_wq, peer_keys1, peer_keys2, peer_u, peer_v,
              final_norm_w):
    cond = jax.nn.silu(c)
    lb_all = jnp.cumsum(jax.nn.softmax(hg_lower_bounds.astype(jnp.float32), axis=0), axis=0)
    for l in range(DEPTH):
        mod = (cond @ ada_w[l] + ada_b[l])[:, None, :]
        sh1, sc1, gt1, sh2, sc2, gt2 = jnp.split(mod, 6, axis=-1)
        h = _rmsnorm_2(x, norm_mix_w[l]) * (1.0 + sc1) + sh1
        proj = h @ w_in[l]
        q, f_logit, i, g, u = jnp.split(
            proj, [HG_WIDTH, 2 * HG_WIDTH, 3 * HG_WIDTH, 4 * HG_WIDTH], axis=-1)
        o_hg = _hgrn2(q, f_logit, i, g, lb_all[l], hg_gnorm_w[l]).astype(x.dtype)
        o_s5 = _s5(u, s5_a_re[l], s5_a_im[l], s5_log_dt[l], s5_b_re[l], s5_b_im[l],
                   s5_c_re[l], s5_c_im[l], s5_d[l], s5_glu_w[l], s5_glu_b[l])
        mixed = jnp.concatenate([o_hg, o_s5], axis=-1) @ w_out[l]
        x = x + gt1 * mixed
        h2 = _rmsnorm_2(x, norm_ffn_w[l]) * (1.0 + sc2) + sh2
        x = x + gt2 * _peer(h2, peer_wq[l], peer_keys1[l], peer_keys2[l], peer_u[l], peer_v[l])
    return _rmsnorm_2(x, final_norm_w)


def setup_inputs(seed=0):
    out = dict(first_inputs(seed))
    for name, value in second_inputs(seed + 1).items():
        if name != "x":
            out[name + "_2"] = value
    return out


def reference(
    x, positions, norm_ffn1, ffn1_gate, ffn1_up, ffn1_down, norm_mix, w_in, cmp_pe_k, cmp_k_w1,
    cmp_k_w2, cmp_pe_v, cmp_v_w1, cmp_v_w2, swa_sinks, w_branch_a, w_branch_b, w_out, norm_ffn2,
    ffn2_gate, ffn2_up, ffn2_down, norm_final, c_2, ada_w_2, ada_b_2, norm_mix_w_2,
    norm_ffn_w_2, w_in_2, w_out_2, hg_lower_bounds_2, hg_gnorm_w_2, s5_a_re_2, s5_a_im_2,
    s5_log_dt_2, s5_b_re_2, s5_b_im_2, s5_c_re_2, s5_c_im_2, s5_d_2, s5_glu_w_2, s5_glu_b_2,
    peer_wq_2, peer_keys1_2, peer_keys2_2, peer_u_2, peer_v_2, final_norm_w_2,
):
    x = first_block(
        x, positions, norm_ffn1, ffn1_gate, ffn1_up, ffn1_down, norm_mix, w_in, cmp_pe_k,
        cmp_k_w1, cmp_k_w2, cmp_pe_v, cmp_v_w1, cmp_v_w2, swa_sinks, w_branch_a, w_branch_b,
        w_out, norm_ffn2, ffn2_gate, ffn2_up, ffn2_down, norm_final,
    )
    return second_block(
        x, c_2, ada_w_2, ada_b_2, norm_mix_w_2, norm_ffn_w_2, w_in_2, w_out_2,
        hg_lower_bounds_2, hg_gnorm_w_2, s5_a_re_2, s5_a_im_2, s5_log_dt_2, s5_b_re_2,
        s5_b_im_2, s5_c_re_2, s5_c_im_2, s5_d_2, s5_glu_w_2, s5_glu_b_2, peer_wq_2,
        peer_keys1_2, peer_keys2_2, peer_u_2, peer_v_2, final_norm_w_2,
    )


_drawn_inputs = setup_inputs


def setup_inputs(seed=0):
    import zlib

    import numpy as np

    out = dict(_drawn_inputs(seed))
    spreads = {}
    factors = {'norm_ffn1': 5.092,
     'norm_mix': 8.0,
     'cmp_pe_k': 8.0,
     'cmp_pe_v': 10.223,
     'swa_sinks': 42.266,
     'norm_ffn2': 5.856,
     'ada_b_2': 5.795,
     'norm_mix_w_2': 8.0,
     'norm_ffn_w_2': 49.72,
     'hg_lower_bounds_2': 8.0,
     'hg_gnorm_w_2': 24.949,
     's5_a_re_2': 64.0,
     's5_a_im_2': 26.144,
     's5_log_dt_2': 31.584,
     's5_b_re_2': 35.992,
     's5_b_im_2': 34.72,
     's5_c_re_2': 37.264,
     's5_c_im_2': 32.512,
     's5_glu_w_2': 6.06,
     's5_glu_b_2': 64.0,
     'final_norm_w_2': 8.407}
    for name, (base, spread) in spreads.items():
        noise = np.random.default_rng([zlib.crc32(name.encode()), seed]).standard_normal(out[name].shape)
        drawn = base * np.exp(spread * noise) if base else spread * noise
        out[name] = jnp.asarray(drawn.astype(out[name].dtype))
    for name, factor in factors.items():
        out[name] = (out[name] * factor).astype(out[name].dtype)
    return out
```

```python
from contextlib import ExitStack

import numpy as np

import concourse.bass as bass
from concourse import mybir

F32 = mybir.dt.float32
I32 = mybir.dt.int32
U32 = mybir.dt.uint32
ALU = mybir.AluOpType
ACT = mybir.ActivationFunctionType
AX = mybir.AxisListType

P = 128
T = 512
D = 1024
KD = D // P
FF = 2816
KF = FF // P
HD = 64
QT = T // P
CMP = 31
EPS = 1e-6
NEG = -1e30
SLOTS = 4
BANKS = 8
SCALE = HD ** -0.5
TWO_PI = 2.0 * np.pi

Q0, KSL, KWN, SQ0, SK, KCA, KCB, VSL, VWN, SVG = 0, 4, 5, 6, 10, 11, 12, 13, 14, 15
ROPED = 11
PROJ = 16

VEC = {}
_at = 0
for _name, _n in (("norm_ffn1", 8), ("norm_mix", 8), ("norm_ffn2", 8), ("norm_final", 8),
                  ("norm_mix_w_2", 8), ("norm_ffn_w_2", 8), ("final_norm_w_2", 8), ("c_2", 8),
                  ("ada_b_2", 48), ("lb0", 4), ("lb1", 4), ("gn", 1), ("a_re", 16), ("a_im", 16),
                  ("log_dt", 16), ("d_skip", 4), ("glu_b", 4), ("sinks", 8), ("freq", 1)):
    VEC[_name] = (_at, _n)
    _at += _n
NVEC = _at


class Signal:

    def __init__(self, ctx, nc, name, base=0):
        self.sem = ctx.enter_context(nc.semaphore(name))
        self.base = base

    def at(self, n):
        return self.base + n

    def passed(self, n):
        self.base += n


class Steps:

    def __init__(self, ctx, nc, name):
        self.sem = ctx.enter_context(nc.semaphore(name))
        self.n = 0

    def then(self, eng, ins):
        self.n += 1
        ins.then_inc(self.sem, 1)
        eng.wait_ge(self.sem, self.n)


def one(ap, i):
    return ap[:, bass.ds(i, 1), :].rearrange("p a n -> p (a n)")


class Kernel:

    def __init__(self, nc, ctx, dram):
        self.nc, self.ctx, self.dram = nc, ctx, dram
        self.names = {}
        self.h = self.sbuf("h", [P, KD, T])
        self.u = self.sbuf("u", [P, KD, T])
        self.ring = self.sbuf("ring", [P, SLOTS, KD * P])
        self.vecs = self.sbuf("vecs", [P, NVEC])
        self.ident = self.sbuf("ident", [P, P])
        self.ones = self.sbuf("ones", [P, P])
        self.rs = self.sbuf("rs", [P, T])
        self.mod = self.sbuf("mod", [P, 6 * KD])
        self.ps = ctx.enter_context(nc.psum_tensor("ps", [P, BANKS, T], F32))
        self.dve_steps = Steps(ctx, nc, "dve_steps")
        self.act_steps = Steps(ctx, nc, "act_steps")
        self.pool_steps = Steps(ctx, nc, "pool_steps")
        self.loaded = [self.new_sem(f"slot{s}_loaded") for s in range(SLOTS)]
        self.used = [self.new_sem(f"slot{s}_used", 1) for s in range(SLOTS)]
        self.emptied = [self.new_sem(f"bank{b}_emptied", 1) for b in range(BANKS)]
        self.first_ready = self.new_sem("first_ready")
        self.squares_ready = self.new_sem("squares_ready")
        self.sumsq_ready = self.new_sem("sumsq_ready")
        self.mean_ready = self.new_sem("mean_ready")
        self.root_ready = self.new_sem("root_ready")

    def sbuf(self, name, shape, dtype=F32, ctx=None):
        self.names[name] = self.names.get(name, 0) + 1
        if self.names[name] > 1:
            name = f"{name}_{self.names[name]}"
        return (ctx or self.ctx).enter_context(self.nc.sbuf_tensor(name, shape, dtype))

    def new_sem(self, name, base=0):
        return Signal(self.ctx, self.nc, name, base)

    def vec(self, name):
        at, n = VEC[name]
        return self.vecs[:, at:at + n]


class Stream:

    def __init__(self, k, iters, chunks):
        self.k, self.iters, self.chunks = k, iters, chunks
        assert len(chunks) % SLOTS == 0
        self.turns = len(chunks) // SLOTS
        self.opened = [0] * BANKS
        for _, groups in chunks:
            for g in groups:
                self.opened[g[0]] += g[3]

    def load(self, sp):
        k = self.k
        with sp.Fori(0, self.iters) as i:
            for j, (source, _) in enumerate(self.chunks):
                s, n = j % SLOTS, j // SLOTS
                src = source(i)
                sp.wait_ge(k.used[s].sem, i * self.turns + k.used[s].at(n))
                sp.dma_start(k.ring[:, s, 0:src.shape[-1]], src).then_inc(k.loaded[s].sem, 16)

    def multiply(self, pe):
        k = self.k
        with pe.Fori(0, self.iters) as i:
            seen = [0] * BANKS
            for j, (_, groups) in enumerate(self.chunks):
                s, n = j % SLOTS, j // SLOTS
                pe.wait_ge(k.loaded[s].sem, i * (16 * self.turns) + k.loaded[s].at(16 * (n + 1)))
                for bank, out, parts, opens, closes, before in groups:
                    if opens:
                        pe.wait_ge(k.emptied[bank].sem, i * self.opened[bank] + k.emptied[bank].at(seen[bank]))
                        seen[bank] += 1
                    if before is not None:
                        before(pe, i)
                    for m, (tile, moving) in enumerate(parts):
                        last = pe.matmul(out, k.ring[:, s, tile * P:(tile + 1) * P], moving,
                                         start=opens and m == 0, stop=closes and m == len(parts) - 1)
                last.then_inc(k.used[s].sem, 1)

    def wait_products(self, eng, i, j):
        s, n = j % SLOTS, j // SLOTS
        eng.wait_ge(self.k.used[s].sem, i * self.turns + self.k.used[s].at(n + 1))

    def finish(self):
        for s in range(SLOTS):
            self.k.loaded[s].passed(16 * self.turns * self.iters)
            self.k.used[s].passed(self.turns * self.iters)
        for b in range(BANKS):
            self.k.emptied[b].passed(self.opened[b] * self.iters)


def chunk_of(weights, per_iter, j):
    return lambda i: weights[bass.ds(i * per_iter + j, 1), :, :].rearrange("a p n -> p (a n)")


def plain_stream(k, weights, tiles, unroll, kin, moving):
    per = -(-kin // KD)
    chunks = []
    for t in range(unroll):
        for c in range(per):
            tiles_here = range(c * KD, min(kin, (c + 1) * KD))
            parts = [(x - c * KD, moving(x)) for x in tiles_here]
            first = moving(0)
            out = k.ps[:, t, 0:first.shape[-1]]
            chunks.append((chunk_of(weights, unroll * per, t * per + c),
                           [(t, out, parts, c == 0, c == per - 1, None)]))
    return Stream(k, tiles // unroll, chunks)


def setup(k):
    nc = k.nc
    h_in = k.dram["x"]
    with nc.Block() as block:
        @block.sync
        def _(sp):
            sp.dma_start(k.h[:], h_in).then_inc(k.first_ready.sem, 16)
            sp.dma_start(k.vecs[:], k.dram["vecs"]).then_inc(k.first_ready.sem, 16)
            sp.wait_ge(k.first_ready.sem, 32)

        @block.tensor
        def _(pe):
            for s in range(SLOTS):
                pe.sem_inc(k.used[s].sem, 1)

        @block.vector
        def _(dve):
            dve.memset(k.ones[:], 1.0)
            for b in range(BANKS):
                dve.sem_inc(k.emptied[b].sem, 1)

        @block.gpsimd
        def _(pool):
            k.pool_steps.then(pool, pool.memset(k.ident[:], 0.0))
            k.pool_steps.then(pool, pool.affine_select(out=k.ident[:], in_=k.ident[:], compare_op=ALU.not_equal,
                                                       fill=1.0, base=0, pattern=[[-1, P]], channel_multiplier=1))


def norm(k, gain, out, shift=None):
    nc = k.nc
    with nc.Block() as block:
        @block.scalar
        def _(act):
            for t in range(KD):
                act.activation(out[:, t], k.h[:, t], ACT.Square).then_inc(k.squares_ready.sem, 1)
            act.wait_ge(k.mean_ready.sem, k.mean_ready.at(1))
            act.activation(k.rs[:], k.rs[:], ACT.Sqrt).then_inc(k.root_ready.sem, 1)

        @block.tensor
        def _(pe):
            for t in range(KD):
                pe.wait_ge(k.squares_ready.sem, k.squares_ready.at(t + 1))
                mm = pe.matmul(k.ps[:, 0], k.ones[:], out[:, t], start=t == 0, stop=t == KD - 1)
            mm.then_inc(k.sumsq_ready.sem, 1)

        @block.vector
        def _(dve):
            dve.wait_ge(k.sumsq_ready.sem, k.sumsq_ready.at(1))
            dve.tensor_scalar(k.rs[:], k.ps[:, 0], 1.0 / D, EPS, ALU.mult, ALU.add).then_inc(k.mean_ready.sem, 1)
            dve.wait_ge(k.root_ready.sem, k.root_ready.at(1))
            k.dve_steps.then(dve, dve.reciprocal(k.rs[:], k.rs[:]))
            for t in range(KD):
                ins = dve.scalar_tensor_tensor(out[:, t], k.h[:, t], gain[:, t:t + 1], k.rs[:], ALU.mult, ALU.mult)
                if shift is not None:
                    k.dve_steps.then(dve, ins)
                    dve.tensor_scalar(out[:, t], out[:, t], shift[:, t:t + 1], None, ALU.add)
    k.squares_ready.passed(KD)
    for s in (k.sumsq_ready, k.mean_ready, k.root_ready):
        s.passed(1)


def residual(k, weights, kin, moving, scale):
    stream = plain_stream(k, weights, KD, 4, kin, moving)
    per = -(-kin // KD)
    with k.nc.Block() as block:
        @block.sync
        def _(sp):
            stream.load(sp)

        @block.tensor
        def _(pe):
            stream.multiply(pe)

        @block.vector
        def _(dve):
            with dve.Fori(0, stream.iters) as i:
                for t in range(4):
                    stream.wait_products(dve, i, t * per + per - 1)
                    by = scale if isinstance(scale, float) else scale[:, bass.ds(i * 4 + t, 1)]
                    dve.scalar_tensor_tensor(one(k.h, i * 4 + t), k.ps[:, t], by, one(k.h, i * 4 + t),
                                             ALU.mult, ALU.add).then_inc(k.emptied[t].sem, 1)
    stream.finish()


def ffn(k, name, gain, sig):
    nc = k.nc
    norm(k, gain, k.u)
    with ExitStack() as ctx:
        hid = k.sbuf(f"{name}_hid", [P, KF, T], ctx=ctx)
        gated = k.sbuf(f"{name}_gated", [P, 2, T], ctx=ctx)
        gated_ready, gated_used = sig
        stream = plain_stream(k, k.dram[f"{name}_gu"], 2 * KF, 4, KD, lambda x: k.u[:, x])
        with nc.Block() as block:
            @block.sync
            def _(sp):
                stream.load(sp)

            @block.tensor
            def _(pe):
                stream.multiply(pe)

            @block.scalar
            def _(act):
                with act.Fori(0, stream.iters) as i:
                    for t in range(2):
                        stream.wait_products(act, i, 2 * t)
                        act.wait_ge(gated_used[t].sem, i + gated_used[t].at(0))
                        act.activation(gated[:, t], k.ps[:, 2 * t], ACT.Silu).then_inc(gated_ready[t].sem, 1)

            @block.vector
            def _(dve):
                with dve.Fori(0, stream.iters) as i:
                    for t in range(2):
                        stream.wait_products(dve, i, 2 * t + 1)
                        dve.wait_ge(gated_ready[t].sem, i + gated_ready[t].at(1))
                        dve.sem_inc(k.emptied[2 * t].sem, 1)
                        dve.tensor_tensor(one(hid, i * 2 + t), gated[:, t], k.ps[:, 2 * t + 1], ALU.mult)\
                           .then_inc(gated_used[t].sem, 1)
                        dve.wait_ge(gated_used[t].sem, i + gated_used[t].at(1))
                        dve.sem_inc(k.emptied[2 * t + 1].sem, 1)
        stream.finish()
        for t in range(2):
            gated_ready[t].passed(stream.iters)
            gated_used[t].passed(stream.iters)
        residual(k, k.dram[f"{name}_down"], KF, lambda x: hid[:, x], 0.5)


def reduce_angle(k, dve, angle, turns, sine, cosine):
    magic = 1.5 * 2.0 ** 23
    c1 = 6.28125
    c2 = float(np.float32(TWO_PI - c1))
    c3 = float(np.float32(TWO_PI - c1 - c2))
    edge = 3.1415925
    step = lambda ins: k.dve_steps.then(dve, ins)
    step(dve.tensor_scalar(turns, angle, 1.0 / TWO_PI, None, ALU.mult))
    step(dve.tensor_scalar(turns, turns, magic, None, ALU.add))
    step(dve.tensor_scalar(turns, turns, magic, None, ALU.subtract))
    step(dve.scalar_tensor_tensor(sine, turns, -c1, angle, ALU.mult, ALU.add))
    step(dve.scalar_tensor_tensor(sine, turns, -c2, sine, ALU.mult, ALU.add))
    step(dve.scalar_tensor_tensor(sine, turns, -c3, sine, ALU.mult, ALU.add))
    step(dve.tensor_scalar(cosine, sine, np.pi / 2, None, ALU.add))
    step(dve.tensor_scalar(turns, cosine, edge, None, ALU.is_gt))
    step(dve.scalar_tensor_tensor(cosine, turns, -TWO_PI, cosine, ALU.mult, ALU.add))
    step(dve.tensor_scalar(cosine, cosine, edge, -edge, ALU.min, ALU.max))
    step(dve.tensor_scalar(sine, sine, edge, -edge, ALU.min, ALU.max))


def project(k, weights, proj, gates):
    stream = plain_stream(k, weights, 2 * PROJ, 4, KD, lambda x: k.u[:, x])
    half = PROJ // 4
    with k.nc.Block() as block:
        @block.sync
        def _(sp):
            stream.load(sp)

        @block.tensor
        def _(pe):
            stream.multiply(pe)

        @block.scalar
        def _(act):
            with act.Fori(half, 2 * half) as i:
                for t in range(4):
                    stream.wait_products(act, i, t)
                    act.activation(one(gates, i * 4 + (t - PROJ)), k.ps[:, t], ACT.Sigmoid)\
                       .then_inc(k.emptied[t].sem, 1)

        @block.vector
        def _(dve):
            with dve.Fori(0, half) as i:
                for t in range(4):
                    stream.wait_products(dve, i, t)
                    dve.tensor_copy(one(proj, i * 4 + t), k.ps[:, t]).then_inc(k.emptied[t].sem, 1)
    stream.finish()


def copy_tiles(k, weights, tiles, dst, moving):
    stream = plain_stream(k, weights, tiles, 4, KD, moving)
    with k.nc.Block() as block:
        @block.sync
        def _(sp):
            stream.load(sp)

        @block.tensor
        def _(pe):
            stream.multiply(pe)

        @block.scalar
        def _(act):
            with act.Fori(0, stream.iters) as i:
                for t in (1, 3):
                    stream.wait_products(act, i, t)
                    act.activation(one(dst, i * 4 + t), k.ps[:, t], ACT.Copy).then_inc(k.emptied[t].sem, 1)

        @block.vector
        def _(dve):
            with dve.Fori(0, stream.iters) as i:
                for t in (0, 2):
                    stream.wait_products(dve, i, t)
                    dve.tensor_copy(one(dst, i * 4 + t), k.ps[:, t]).then_inc(k.emptied[t].sem, 1)
    stream.finish()


def rope_tables(k, c, ctx):
    nc = k.nc
    with ExitStack() as tmp:
        raw = k.sbuf("pos_raw", [P, T], I32, tmp)
        turns = k.sbuf("turns", [P, T], ctx=tmp)
        posf = k.sbuf("posf", [P, T], ctx=tmp)
        loads = Signal(tmp, nc, "pos_loaded")
        reduced = Signal(tmp, nc, "angles_reduced")
        with nc.Block() as block:
            @block.sync
            def _(sp):
                sp.dma_start(raw[:], k.dram["positions"].to_broadcast((P, T))).then_inc(loads.sem, 16)

            @block.vector
            def _(dve):
                dve.wait_ge(loads.sem, 16)
                k.dve_steps.then(dve, dve.tensor_copy(posf[:], raw[:]))
                k.dve_steps.then(dve, dve.tensor_scalar(posf[:], posf[:], k.vec("freq"), None, ALU.mult))
                reduce_angle(k, dve, posf[:], turns[:], c.sin[:], c.cos[:])
                dve.sem_inc(reduced.sem, 1)

            @block.scalar
            def _(act):
                act.wait_ge(reduced.sem, 1)
                act.activation(c.sin[:], c.sin[:], ACT.Sin)
                act.activation(c.cos[:], c.cos[:], ACT.Sin)

            @block.gpsimd
            def _(pool):
                step = lambda ins: k.pool_steps.then(pool, ins)
                step(pool.memset(c.rot[:], 0.0))
                for b, fill in ((0, -1.0), (1, 1.0)):
                    view = c.rot[:].rearrange("p (a b c) -> p b a c", a=2, b=2)[:, b]
                    step(pool.affine_select(out=view, in_=view, compare_op=ALU.not_equal, fill=fill,
                                            base=-32 if b == 0 else 0, pattern=[[-64, 2], [-1, 32]],
                                            channel_multiplier=1))
                step(pool.memset(c.causal[:], 0.0))
                step(pool.memset(c.before[:], 0.0))
                step(pool.memset(c.seen[:], 0.0))
                step(pool.memset(c.some[:], 1.0))
                pool.affine_select(out=c.causal[:], in_=c.causal[:], compare_op=ALU.is_ge, fill=NEG, base=0,
                                   pattern=[[-1, P]], channel_multiplier=1)
                pool.affine_select(out=c.before[:], in_=c.before[:], compare_op=ALU.is_ge, fill=NEG, base=-1,
                                   pattern=[[1, P]], channel_multiplier=-1)
                pool.affine_select(out=c.seen[:], in_=c.seen[:], compare_op=ALU.is_ge, fill=NEG, base=-31,
                                   pattern=[[P, QT], [-16, CMP]], channel_multiplier=1)
                pool.affine_select(out=c.some[:], in_=c.some[:], compare_op=ALU.is_ge, fill=0.0, base=-31,
                                   pattern=[[P, QT]], channel_multiplier=1)


def rope(k, c, proj):
    nc = k.nc
    with ExitStack() as tmp:
        part = k.sbuf("rope_part", [P, 2, T], ctx=tmp)
        turned = Signal(tmp, nc, "halves_turned")
        roped = Signal(tmp, nc, "tile_roped")
        with nc.Block() as block:
            @block.tensor
            def _(pe):
                for t in range(ROPED):
                    if t >= 2:
                        pe.wait_ge(roped.sem, t - 1)
                    pe.matmul(k.ps[:, t % 2], c.rot[:], proj[:, t], start=True, stop=True).then_inc(turned.sem, 1)

            @block.vector
            def _(dve):
                for t in range(ROPED):
                    dve.wait_ge(turned.sem, t + 1)
                    dve.tensor_tensor(part[:, 0], k.ps[:, t % 2], c.sin[:], ALU.mult)
                    k.dve_steps.then(dve, dve.tensor_tensor(part[:, 1], proj[:, t], c.cos[:], ALU.mult))
                    dve.tensor_tensor(proj[:, t], part[:, 0], part[:, 1], ALU.add).then_inc(roped.sem, 1)
                    dve.wait_ge(roped.sem, t + 1)


def compress(k, c, proj):
    nc = k.nc
    with ExitStack() as tmp:
        w1 = k.sbuf("cmp_w1", [P, 32, 256], ctx=tmp)
        w2 = k.sbuf("cmp_w2", [P, 2, 192], ctx=tmp)
        pe_k = k.sbuf("cmp_pe", [P, 32], ctx=tmp)
        blocks = k.sbuf("cmp_blocks", [P, 32, 2, CMP], ctx=tmp)
        hid = k.sbuf("cmp_hid", [P, 2, 2, 2 * CMP], ctx=tmp)
        part = k.sbuf("cmp_part", [P, 2, CMP], ctx=tmp)
        loads = Signal(tmp, nc, "cmp_loaded")
        made = Signal(tmp, nc, "cmp_blocks_made")
        first = Signal(tmp, nc, "cmp_first_done")
        act_done = Signal(tmp, nc, "cmp_hid_ready")
        second = Signal(tmp, nc, "cmp_second_done")
        copied = Signal(tmp, nc, "cmp_keys_copied")
        turned = Signal(tmp, nc, "cmp_keys_turned")
        with nc.Block() as block:
            @block.sync
            def _(sp):
                sp.dma_start(pe_k[:], k.dram["cmp_pe"]).then_inc(loads.sem, 16)
                sp.dma_start(w2[:], k.dram["cmp_w2"]).then_inc(loads.sem, 16)
                sp.dma_start(w1[:], k.dram["cmp_w1"]).then_inc(loads.sem, 16)

            @block.tensor
            def _(pe):
                pe.wait_ge(loads.sem, 48)
                pe.wait_ge(made.sem, 4)
                for kv in range(2):
                    rows = slice(HD * kv, HD * (kv + 1))
                    for t in range(2):
                        for l in range(32):
                            mm = pe.matmul(k.ps[:, 2 * kv + t, 0:2 * CMP], w1[rows, l, t * P:(t + 1) * P],
                                           blocks[rows, l].rearrange("p g c -> p (g c)"),
                                           start=l == 0, stop=l == 31)
                        mm.then_inc(first.sem, 1)
                pe.wait_ge(act_done.sem, 4)
                for t in range(2):
                    mm = pe.matmul(k.ps[:, 4, 0:2 * CMP], w2[:, t, 0:P], hid[:, 0, t], start=t == 0, stop=t == 1)
                mm.then_inc(second.sem, 1)
                for g in range(2):
                    for t in range(2):
                        mm = pe.matmul(k.ps[0:CMP, 5, g * HD:(g + 1) * HD], hid[:, 1, t, g * CMP:(g + 1) * CMP],
                                       w2[:, t, P:P + HD], start=t == 0, stop=t == 1)
                mm.then_inc(second.sem, 1)
                pe.wait_ge(copied.sem, 2)
                pe.matmul(k.ps[:, 6, 0:CMP], c.rot[:], c.kcmp[:], start=True, stop=True).then_inc(turned.sem, 1)

            @block.scalar
            def _(act):
                for n in range(4):
                    act.wait_ge(first.sem, n + 1)
                    act.activation(hid[:, n // 2, n % 2], k.ps[:, n, 0:2 * CMP], ACT.Gelu_apprx_tanh)\
                       .then_inc(act_done.sem, 1)

            @block.vector
            def _(dve):
                dve.wait_ge(loads.sem, 48)
                for g in range(2):
                    strides = proj[:, KCA + g].rearrange("p (c l) -> p l c", l=16)
                    for half in range(2):
                        pos = pe_k[:, half * 16:(half + 1) * 16].unsqueeze(2).to_broadcast((P, 16, CMP))
                        dve.tensor_tensor(blocks[:, half * 16:(half + 1) * 16, g], strides[:, :, half:half + CMP],
                                          pos, ALU.add).then_inc(made.sem, 1)
                dve.wait_ge(second.sem, 2)
                for g in range(2):
                    rows = slice(HD * g, HD * (g + 1))
                    dve.tensor_copy(c.kcmp[rows], k.ps[rows, 4, g * CMP:(g + 1) * CMP]).then_inc(copied.sem, 1)
                dve.tensor_copy(c.vcmp[0:CMP], k.ps[0:CMP, 5, 0:P])
                dve.wait_ge(turned.sem, 1)
                last = slice(31, T, 16)
                dve.tensor_tensor(part[:, 0], k.ps[:, 6, 0:CMP], c.sin[:, last], ALU.mult)
                k.dve_steps.then(dve, dve.tensor_tensor(part[:, 1], c.kcmp[:], c.cos[:, last], ALU.mult))
                dve.tensor_tensor(c.kcmp[:], part[:, 0], part[:, 1], ALU.add)


def token_major(k, name, sources, dst):
    nc = k.nc
    n_banks = -(-len(sources) // 4)
    with ExitStack() as tmp:
        turned = Signal(tmp, nc, f"{name}_turned")
        copied = Signal(tmp, nc, f"{name}_copied")
        with nc.Block() as block:
            @block.tensor
            def _(pe):
                for b in range(n_banks):
                    if b >= BANKS:
                        pe.wait_ge(copied.sem, b - BANKS + 1)
                    for n in range(4 * b, min(4 * b + 4, len(sources))):
                        tr = pe.transpose(k.ps[:, b % BANKS, (n % 4) * P:(n % 4 + 1) * P], sources[n], k.ident[:])
                    tr.then_inc(turned.sem, 1)

            @block.vector
            def _(dve):
                for b in range(n_banks):
                    dve.wait_ge(turned.sem, b + 1)
                    for n in range(4 * b, min(4 * b + 4, len(sources))):
                        ins = dve.tensor_copy(dst[n], k.ps[:, b % BANKS, (n % 4) * P:(n % 4 + 1) * P])
                    ins.then_inc(copied.sem, 1)


def nsa(k, c, proj, vtok, o):
    nc = k.nc
    units = [(qt, j, g) for qt in range(QT) for j in range(4) for g in range(2)]
    with ExitStack() as tmp:
        probs = k.sbuf("nsa_probs", [P, 2, 3, T], ctx=tmp)
        keyed = k.sbuf("nsa_keyed", [P, 2, 9, P], ctx=tmp)
        peak = k.sbuf("nsa_peak", [P, 2, 3], ctx=tmp)
        sums = k.sbuf("nsa_sums", [P, 2, 3], ctx=tmp)
        share = k.sbuf("nsa_share", [P, 3], ctx=tmp)
        sigm = k.sbuf("nsa_gates", [P, QT, 24], ctx=tmp)
        gates_ready = Signal(tmp, nc, "nsa_gates_ready")
        scored = Signal(tmp, nc, "nsa_scored")
        peaked = Signal(tmp, nc, "nsa_peaked")
        exped = Signal(tmp, nc, "nsa_exped")
        turned = Signal(tmp, nc, "nsa_turned")
        copied_a = Signal(tmp, nc, "nsa_copied_by_act")
        copied_v = Signal(tmp, nc, "nsa_copied_by_dve")
        mixed = Signal(tmp, nc, "nsa_mixed")
        summed = Signal(tmp, nc, "nsa_summed")
        with nc.Block() as block:
            @block.tensor
            def _(pe):
                def score(n):
                    qt, j, g = units[n]
                    rows, keys = slice(HD * g, HD * (g + 1)), (qt + 1) * P
                    q = proj[rows, Q0 + j, qt * P:(qt + 1) * P]
                    if n >= 1:
                        pe.wait_ge(exped.sem, n)
                    pe.matmul(k.ps[:, 0, 0:keys], q, proj[rows, KSL, 0:keys], start=True, stop=True)
                    pe.matmul(k.ps[:, 1, 0:keys], q, proj[rows, KWN, 0:keys], start=True, stop=True)
                    pe.matmul(k.ps[:, 2, 0:CMP], q, c.kcmp[rows], start=True, stop=True).then_inc(scored.sem, 1)

                score(0)
                for n, (qt, j, g) in enumerate(units):
                    b = n % 2
                    pe.wait_ge(exped.sem, n + 1)
                    if n >= 1:
                        pe.wait_ge(copied_a.sem, n)
                        pe.wait_ge(copied_v.sem, n)
                    for kind in range(2):
                        for kb in range(qt + 1):
                            pe.transpose(k.ps[:, 3 + kind, kb * P:(kb + 1) * P],
                                         probs[:, b, kind, kb * P:(kb + 1) * P], k.ident[:])
                    pe.transpose(k.ps[0:CMP, 5, 0:P], probs[:, b, 2, 0:CMP], k.ident[:]).then_inc(turned.sem, 1)
                    if n + 1 < len(units):
                        score(n + 1)
                    pe.wait_ge(copied_a.sem, n + 1)
                    pe.wait_ge(copied_v.sem, n + 1)
                    if n >= 2:
                        pe.wait_ge(summed.sem, n - 1)
                    for kind in range(2):
                        for kb in range(qt + 1):
                            pe.matmul(k.ps[:, 6 + b, kind * HD:(kind + 1) * HD], keyed[:, b, 4 * kind + kb],
                                      vtok[:, kind, kb, HD * g:HD * (g + 1)], start=kb == 0, stop=kb == qt)
                    pe.matmul(k.ps[:, 6 + b, 2 * HD:3 * HD], keyed[0:CMP, b, 8], c.vcmp[0:CMP, HD * g:HD * (g + 1)],
                              start=True, stop=True).then_inc(mixed.sem, 1)

            @block.scalar
            def _(act):
                act.activation(sigm[:], vtok[:, 2, :, HD:HD + 24], ACT.Sigmoid).then_inc(gates_ready.sem, 1)
                for n, (qt, j, g) in enumerate(units):
                    b, keys = n % 2, (qt + 1) * P
                    act.wait_ge(peaked.sem, n + 1)
                    if n >= 2:
                        act.wait_ge(turned.sem, n - 1)
                    if n >= 2:
                        act.wait_ge(summed.sem, n - 1)
                    for kind, width in ((0, keys), (1, keys), (2, CMP)):
                        ins = act.activation(probs[:, b, kind, 0:width], k.ps[:, kind, 0:width], ACT.Exp,
                                             bias=peak[:, b, kind:kind + 1], scale=SCALE,
                                             accum_out=sums[:, b, kind:kind + 1])
                    ins.then_inc(exped.sem, 1)
                    act.wait_ge(turned.sem, n + 1)
                    if n >= 2:
                        act.wait_ge(mixed.sem, n - 1)
                    act.activation(keyed[:, b, 0:qt + 1], k.ps[:, 3, 0:keys].rearrange("p (a n) -> p a n", n=P),
                                   ACT.Copy)
                    act.activation(keyed[0:CMP, b, 8], k.ps[0:CMP, 5, 0:P], ACT.Copy).then_inc(copied_a.sem, 1)

            @block.vector
            def _(dve):
                def peaks(n):
                    qt, b = units[n][0], n % 2
                    own, keys = slice(qt * P, (qt + 1) * P), (qt + 1) * P
                    dve.wait_ge(scored.sem, n + 1)
                    dve.tensor_tensor(k.ps[:, 0, own], k.ps[:, 0, own], c.causal[:], ALU.add)
                    dve.tensor_tensor(k.ps[:, 1, own], k.ps[:, 1, own], c.causal[:], ALU.add)
                    k.dve_steps.then(dve, dve.tensor_tensor(k.ps[:, 2, 0:CMP], k.ps[:, 2, 0:CMP], c.seen[:, qt],
                                                            ALU.add))
                    if n >= 2:
                        dve.wait_ge(exped.sem, n - 1)
                    for kind, width in ((0, keys), (1, keys), (2, CMP)):
                        ins = dve.tensor_reduce(peak[:, b, kind:kind + 1], k.ps[:, kind, 0:width], AX.X, ALU.max)
                    k.dve_steps.then(dve, ins)
                    dve.tensor_scalar(peak[:, b], peak[:, b], -SCALE, None, ALU.mult).then_inc(peaked.sem, 1)

                peaks(0)
                dve.wait_ge(gates_ready.sem, 1)
                for n, (qt, j, g) in enumerate(units):
                    b, head = n % 2, 4 * g + j
                    dve.wait_ge(turned.sem, n + 1)
                    if n >= 2:
                        dve.wait_ge(mixed.sem, n - 1)
                    dve.tensor_copy(keyed[:, b, 4:5 + qt], k.ps[:, 4, 0:(qt + 1) * P].rearrange("p (a n) -> p a n", n=P))\
                       .then_inc(copied_v.sem, 1)
                    if n + 1 < len(units):
                        peaks(n + 1)
                    k.dve_steps.then(dve, dve.reciprocal(share[:], sums[:, b]))
                    gate = sigm[:, qt].rearrange("p (b h) -> p b h", b=3)
                    k.dve_steps.then(dve, dve.tensor_tensor(share[:, 0:2], share[:, 0:2], gate[:, 1:3, head], ALU.mult))
                    k.dve_steps.then(dve, dve.scalar_tensor_tensor(share[:, 2:3], share[:, 2:3], c.some[:, qt:qt + 1],
                                                                   gate[:, 0:1, head], ALU.mult, ALU.mult))
                    dve.wait_ge(mixed.sem, n + 1)
                    mine = o[:, qt, HD * head:HD * (head + 1)]
                    k.dve_steps.then(dve, dve.tensor_scalar(mine, k.ps[:, 6 + b, 0:HD], share[:, 0:1], None, ALU.mult))
                    k.dve_steps.then(dve, dve.scalar_tensor_tensor(mine, k.ps[:, 6 + b, HD:2 * HD], share[:, 1:2], mine,
                                                                   ALU.mult, ALU.add))
                    dve.scalar_tensor_tensor(mine, k.ps[:, 6 + b, 2 * HD:3 * HD], share[:, 2:3], mine,
                                             ALU.mult, ALU.add).then_inc(summed.sem, 1)
                    dve.wait_ge(summed.sem, n + 1)


def swa(k, c, proj, vtok, o):
    nc = k.nc
    units = [(qt, j, g) for qt in range(QT) for j in range(4) for g in range(2)]
    with ExitStack() as tmp:
        probs = k.sbuf("swa_probs", [P, 2, 2 * P], ctx=tmp)
        keyed = k.sbuf("swa_keyed", [P, 2, 2, P], ctx=tmp)
        peak = k.sbuf("swa_peak", [P, 2], ctx=tmp)
        sums = k.sbuf("swa_sums", [P, 2, 2], ctx=tmp)
        share = k.sbuf("swa_share", [P, 1], ctx=tmp)
        scored = Signal(tmp, nc, "swa_scored")
        peaked = Signal(tmp, nc, "swa_peaked")
        exped = Signal(tmp, nc, "swa_exped")
        turned = Signal(tmp, nc, "swa_turned")
        copied = Signal(tmp, nc, "swa_copied")
        mixed = Signal(tmp, nc, "swa_mixed")
        summed = Signal(tmp, nc, "swa_summed")
        with nc.Block() as block:
            @block.tensor
            def _(pe):
                def score(n):
                    qt, j, g = units[n]
                    rows, lo = slice(HD * g, HD * (g + 1)), max(qt - 1, 0) * P
                    if n >= 2:
                        pe.wait_ge(exped.sem, n - 1)
                    pe.matmul(k.ps[:, n % 2, 0:(qt + 1) * P - lo], proj[rows, SQ0 + j, qt * P:(qt + 1) * P],
                              proj[rows, SK, lo:(qt + 1) * P], start=True, stop=True).then_inc(scored.sem, 1)

                score(0)
                for n, (qt, j, g) in enumerate(units):
                    b, blocks = n % 2, min(qt, 1) + 1
                    if n + 1 < len(units):
                        score(n + 1)
                    pe.wait_ge(exped.sem, n + 1)
                    if n >= 2:
                        pe.wait_ge(copied.sem, n - 1)
                    for m in range(blocks):
                        tr = pe.transpose(k.ps[:, 2 + b, m * P:(m + 1) * P], probs[:, b, m * P:(m + 1) * P], k.ident[:])
                    tr.then_inc(turned.sem, 1)
                    pe.wait_ge(copied.sem, n + 1)
                    if n >= 2:
                        pe.wait_ge(summed.sem, n - 1)
                    for m in range(blocks):
                        mm = pe.matmul(k.ps[:, 4 + b, 0:HD], keyed[:, b, m], vtok[:, 2, qt - blocks + 1 + m, 0:HD],
                                       start=m == 0, stop=m == blocks - 1)
                    mm.then_inc(mixed.sem, 1)

            @block.scalar
            def _(act):
                for n, (qt, j, g) in enumerate(units):
                    b, head, width = n % 2, 4 * g + j, (min(qt, 1) + 1) * P
                    act.wait_ge(peaked.sem, n + 1)
                    if n >= 2:
                        act.wait_ge(turned.sem, n - 1)
                        act.wait_ge(summed.sem, n - 1)
                    act.activation(probs[:, b, 0:width], k.ps[:, b, 0:width], ACT.Exp, bias=peak[:, b:b + 1],
                                   scale=SCALE, accum_out=sums[:, b, 0:1])
                    act.activation(sums[:, b, 1:2], k.vec("sinks")[:, head:head + 1], ACT.Exp,
                                   bias=peak[:, b:b + 1]).then_inc(exped.sem, 1)
                    act.wait_ge(turned.sem, n + 1)
                    if n >= 2:
                        act.wait_ge(mixed.sem, n - 1)
                    act.activation(keyed[:, b, 0:width // P], k.ps[:, 2 + b, 0:width].rearrange("p (a n) -> p a n", n=P),
                                   ACT.Copy).then_inc(copied.sem, 1)

            @block.vector
            def _(dve):
                def peaks(n):
                    qt, j, g = units[n]
                    b, head, blocks = n % 2, 4 * g + j, min(qt, 1) + 1
                    dve.wait_ge(scored.sem, n + 1)
                    if blocks == 2:
                        dve.tensor_tensor(k.ps[:, b, 0:P], k.ps[:, b, 0:P], c.before[:], ALU.add)
                    own = k.ps[:, b, (blocks - 1) * P:blocks * P]
                    k.dve_steps.then(dve, dve.tensor_tensor(own, own, c.causal[:], ALU.add))
                    if n >= 2:
                        dve.wait_ge(exped.sem, n - 1)
                    k.dve_steps.then(dve, dve.tensor_reduce(peak[:, b:b + 1], k.ps[:, b, 0:blocks * P], AX.X, ALU.max))
                    k.dve_steps.then(dve, dve.scalar_tensor_tensor(peak[:, b:b + 1], peak[:, b:b + 1], SCALE,
                                                                   k.vec("sinks")[:, head:head + 1], ALU.mult, ALU.max))
                    dve.tensor_scalar(peak[:, b:b + 1], peak[:, b:b + 1], -1.0, None, ALU.mult)\
                       .then_inc(peaked.sem, 1)

                peaks(0)
                for n, (qt, j, g) in enumerate(units):
                    b, head = n % 2, 4 * g + j
                    if n + 1 < len(units):
                        peaks(n + 1)
                    dve.wait_ge(mixed.sem, n + 1)
                    k.dve_steps.then(dve, dve.tensor_tensor(share[:], sums[:, b, 0:1], sums[:, b, 1:2], ALU.add))
                    k.dve_steps.then(dve, dve.reciprocal(share[:], share[:]))
                    dve.tensor_scalar(o[:, qt, HD * head:HD * (head + 1)], k.ps[:, 4 + b, 0:HD], share[:], None,
                                      ALU.mult).then_inc(summed.sem, 1)
                    dve.wait_ge(summed.sem, n + 1)


def branches(k, weights, gates, oa, ob, merged):
    nc = k.nc
    chunks = []
    for t in range(4):
        groups = [(t, k.ps[:, t], [(x, oa[:, x]) for x in range(4)], True, True, None),
                  (4 + t, k.ps[:, 4 + t], [(4 + x, ob[:, x]) for x in range(4)], True, True, None)]
        chunks.append((chunk_of(weights, 4, t), groups))
    stream = Stream(k, KD // 4, chunks)
    with ExitStack() as tmp:
        part = k.sbuf("branch_part", [P, 2, T], ctx=tmp)
        product = Signal(tmp, nc, "branch_product")
        added = Signal(tmp, nc, "branch_added")
        with nc.Block() as block:
            @block.sync
            def _(sp):
                stream.load(sp)

            @block.tensor
            def _(pe):
                stream.multiply(pe)

            @block.vector
            def _(dve):
                with dve.Fori(0, stream.iters) as i:
                    for t in range(4):
                        stream.wait_products(dve, i, t)
                        dve.tensor_tensor(part[:, 0], one(gates, i * 4 + t), k.ps[:, t], ALU.mult)\
                           .then_inc(k.emptied[t].sem, 1)
                        dve.tensor_tensor(part[:, 1], one(gates, i * 4 + (KD + t)), k.ps[:, 4 + t], ALU.mult)\
                           .then_inc(k.emptied[4 + t].sem, 1)
                        dve.wait_ge(k.emptied[t].sem, i + k.emptied[t].at(1))
                        dve.wait_ge(k.emptied[4 + t].sem, i + k.emptied[4 + t].at(1))
                        dve.tensor_tensor(one(merged, i * 4 + t), part[:, 0], part[:, 1], ALU.add)\
                           .then_inc(added.sem, 1)
                        dve.wait_ge(added.sem, i * 4 + (t + 1))
        stream.finish()


class Mixer1:
    pass


def mixer1(k):
    nc = k.nc
    norm(k, k.vec("norm_mix"), k.u)
    with ExitStack() as ctx:
        c = Mixer1()
        oa_t = k.sbuf("oa_t", [P, 4, T], ctx=ctx)
        ob_t = k.sbuf("ob_t", [P, 4, T], ctx=ctx)
        gates = k.sbuf("branch_gates", [P, 2 * KD, T], ctx=ctx)
        with ExitStack() as inner:
            proj = k.sbuf("proj", [P, PROJ, T], ctx=inner)
            c.cos = k.sbuf("cos", [P, T], ctx=inner)
            c.sin = k.sbuf("sin", [P, T], ctx=inner)
            c.rot = k.sbuf("rot", [P, P], ctx=inner)
            c.causal = k.sbuf("causal", [P, P], ctx=inner)
            c.before = k.sbuf("before", [P, P], ctx=inner)
            c.seen = k.sbuf("seen", [P, QT, CMP], ctx=inner)
            c.some = k.sbuf("some", [P, QT], ctx=inner)
            c.kcmp = k.sbuf("kcmp", [P, CMP], ctx=inner)
            c.vcmp = k.sbuf("vcmp", [P, P], ctx=inner)
            project(k, k.dram["w_in"], proj, gates)
            rope_tables(k, c, inner)
            rope(k, c, proj)
            compress(k, c, proj)
            vtok = k.sbuf("vtok", [P, 3, QT, P], ctx=inner)
            token_major(k, "values", [proj[:, t, b * P:(b + 1) * P] for t in (VSL, VWN, SVG) for b in range(QT)],
                        [vtok[:, n, b] for n in range(3) for b in range(QT)])
            with ExitStack() as deep:
                oa = k.sbuf("oa", [P, QT, 512], ctx=deep)
                ob = k.sbuf("ob", [P, QT, 512], ctx=deep)
                nsa(k, c, proj, vtok, oa)
                swa(k, c, proj, vtok, ob)
                token_major(k, "outputs",
                            [s[:, q, f * P:(f + 1) * P] for s in (oa, ob) for f in range(4) for q in range(QT)],
                            [d[:, f, q * P:(q + 1) * P] for d in (oa_t, ob_t) for f in range(4) for q in range(QT)])
        merged = k.sbuf("merged", [P, KD, T], ctx=ctx)
        branches(k, k.dram["w_branch"], gates, oa_t, ob_t, merged)
        residual(k, k.dram["w_out"], KD, lambda x: merged[:, x], 1.0)


CHUNK = 16
NCH = T // CHUNK
HEADS2 = 4
LANES = HEADS2 * NCH
S5T = 16


def modulation(k):
    nc = k.nc
    with ExitStack() as tmp:
        cond = k.sbuf("cond", [P, KD], ctx=tmp)
        ready = Signal(tmp, nc, "cond_ready")
        stream = plain_stream(k, k.dram["ada_w"], 6 * KD, 4, KD, lambda x: cond[:, x:x + 1])
        with nc.Block() as block:
            @block.sync
            def _(sp):
                stream.load(sp)

            @block.scalar
            def _(act):
                act.activation(cond[:], k.vec("c_2"), ACT.Silu).then_inc(ready.sem, 1)

            @block.tensor
            def _(pe):
                pe.wait_ge(ready.sem, 1)
                stream.multiply(pe)

            @block.vector
            def _(dve):
                with dve.Fori(0, stream.iters) as i:
                    for t in range(4):
                        stream.wait_products(dve, i, t)
                        dve.tensor_tensor(k.mod[:, bass.ds(i * 4 + t, 1)], k.ps[:, t, 0:1],
                                          k.vec("ada_b_2")[:, bass.ds(i * 4 + t, 1)], ALU.add)\
                           .then_inc(k.emptied[t].sem, 1)
        stream.finish()


def scaled_gain(k, name, scale, out):
    with k.nc.Block() as block:
        @block.vector
        def _(dve):
            dve.scalar_tensor_tensor(out, scale, 1.0, k.vec(name), ALU.add, ALU.mult)


def hgrn(k, proj, out):
    nc = k.nc
    Q, F, V, G = 0, 4, 8, 12
    lanes = lambda ap: ap.rearrange("p h (c j) -> p (h c) j", j=CHUNK)
    heads = lambda ap: ap.rearrange("p h (c j) -> p h c j", j=CHUNK)
    with ExitStack() as outer:
        f = k.sbuf("hg_f", [P, HEADS2, T], ctx=outer)
        key = k.sbuf("hg_key", [P, HEADS2, T], ctx=outer)
        start = k.sbuf("hg_start", [P, HEADS2, T], ctx=outer)
        q = proj[:, Q:Q + 4]
        with ExitStack() as tmp:
            lb = k.sbuf("hg_lb", [P, 3, HEADS2], ctx=tmp)
            lb_ready = Signal(tmp, nc, "hg_lb_ready")
            sig_ready = Signal(tmp, nc, "hg_sigmoid_ready")
            with nc.Block() as block:
                @block.scalar
                def _(act):
                    act.activation(q, q, ACT.Silu).then_inc(sig_ready.sem, 1)
                    act.activation(proj[:, G:G + 4], proj[:, G:G + 4], ACT.Silu).then_inc(sig_ready.sem, 1)
                    act.activation(f[:], proj[:, F:F + 4], ACT.Sigmoid).then_inc(sig_ready.sem, 1)
                    act.wait_ge(lb_ready.sem, 1)
                    act.activation(lb[:, 0:2], lb[:, 0:2], ACT.Exp).then_inc(sig_ready.sem, 1)

                @block.vector
                def _(dve):
                    step = lambda ins: k.dve_steps.then(dve, ins)
                    step(dve.tensor_tensor(lb[:, 2], k.vec("lb0"), k.vec("lb1"), ALU.max))
                    step(dve.tensor_tensor(lb[:, 0], k.vec("lb0"), lb[:, 2], ALU.subtract))
                    dve.tensor_tensor(lb[:, 1], k.vec("lb1"), lb[:, 2], ALU.subtract).then_inc(lb_ready.sem, 1)
                    dve.wait_ge(sig_ready.sem, 4)
                    step(dve.tensor_tensor(lb[:, 1], lb[:, 0], lb[:, 1], ALU.add))
                    step(dve.reciprocal(lb[:, 1], lb[:, 1]))
                    step(dve.tensor_tensor(lb[:, 0], lb[:, 0], lb[:, 1], ALU.mult))
                    step(dve.tensor_scalar(lb[:, 1], lb[:, 0], -1.0, 1.0, ALU.mult, ALU.add))
                    for h in range(HEADS2):
                        ins = dve.tensor_scalar(f[:, h], f[:, h], lb[:, 1, h:h + 1], lb[:, 0, h:h + 1],
                                                ALU.mult, ALU.add)
                    step(ins)
                    step(dve.tensor_scalar(key[:], f[:], -1.0, 1.0, ALU.mult, ALU.add))
                    step(dve.tensor_scalar(q, q, float(P) ** -0.5, None, ALU.mult))
                    sl, fl = lanes(start), lanes(f)
                    step(dve.tensor_copy(sl[:, :, 0:1], fl[:, :, 0:1]))
                    for j in range(1, CHUNK):
                        step(dve.tensor_tensor(sl[:, :, j:j + 1], sl[:, :, j - 1:j], fl[:, :, j:j + 1], ALU.mult))
        hgrn_within(k, lanes, heads, q, f, key, proj[:, V:V + 4], out)
        hgrn_across(k, lanes, q, f, key, start, proj[:, V:V + 4], out)
    hgrn_finish(k, proj[:, G:G + 4], out)


def hgrn_within(k, lanes, heads, q, f, key, v, out):
    nc = k.nc
    with ExitStack() as tmp:
        qf = k.sbuf("hg_qf", [P, LANES, CHUNK], ctx=tmp)
        qk = k.sbuf("hg_qk", [P, 2, LANES * CHUNK], ctx=tmp)
        sv = k.sbuf("hg_sv", [P, HEADS2 * NCH * CHUNK], ctx=tmp)
        decayed = Signal(tmp, nc, "hg_query_decayed")
        paired = Signal(tmp, nc, "hg_pairs_ready")
        scored = Signal(tmp, nc, "hg_lag_scored")
        with nc.Block() as block:
            @block.gpsimd
            def _(pool):
                fl = lanes(f)
                for lag in range(1, CHUNK):
                    if lag == 1:
                        ins = pool.tensor_tensor(qf[:, :, 1:], lanes(q)[:, :, 1:], fl[:, :, 1:], ALU.mult)
                    else:
                        pool.wait_ge(decayed.sem, lag - 1)
                        pool.wait_ge(paired.sem, lag)
                        ins = pool.tensor_tensor(qf[:, :, lag:], qf[:, :, lag:], fl[:, :, 1:CHUNK - lag + 1], ALU.mult)
                    ins.then_inc(decayed.sem, 1)

            @block.tensor
            def _(pe):
                for lag in range(CHUNK):
                    w = (CHUNK - lag) * NCH
                    pe.wait_ge(paired.sem, lag + 1)
                    for h in range(HEADS2):
                        mm = pe.matmul(k.ps[:, 4 * (lag % 2) + h, 0:w], k.ones[:],
                                       qk[:, lag % 2, h * w:(h + 1) * w], start=True, stop=True)
                    mm.then_inc(scored.sem, 1)

            @block.vector
            def _(dve):
                kl = lanes(key)

                def pairs(lag):
                    w = CHUNK - lag
                    dst = qk[:, lag % 2, 0:LANES * w].rearrange("p (l j) -> p l j", j=w)
                    if lag >= 1:
                        dve.wait_ge(decayed.sem, lag)
                    if lag >= 2:
                        dve.wait_ge(scored.sem, lag - 1)
                    source = lanes(q) if lag == 0 else qf[:, :, lag:]
                    dve.tensor_tensor(dst, source, kl[:, :, 0:w], ALU.mult).then_inc(paired.sem, 1)

                pairs(0)
                for lag in range(CHUNK):
                    w = CHUNK - lag
                    if lag + 1 < CHUNK:
                        pairs(lag + 1)
                    dve.wait_ge(scored.sem, lag + 1)
                    score = k.ps[:, 4 * (lag % 2):4 * (lag % 2) + 4, 0:NCH * w].rearrange("p h (c j) -> p h c j", j=w)
                    if lag == 0:
                        k.dve_steps.then(dve, dve.tensor_tensor(heads(out), score, heads(v), ALU.mult))
                        continue
                    part = sv[:, 0:HEADS2 * NCH * w].rearrange("p (h c j) -> p h c j", h=HEADS2, j=w)
                    k.dve_steps.then(dve, dve.tensor_tensor(part, score, heads(v)[:, :, :, 0:w], ALU.mult))
                    flat = sv[:, 0:LANES * w].rearrange("p (l j) -> p l j", j=w)
                    k.dve_steps.then(dve, dve.tensor_tensor(lanes(out)[:, :, lag:], lanes(out)[:, :, lag:], flat, ALU.add))


def hgrn_across(k, lanes, q, f, key, start, v, out):
    nc = k.nc
    per = T // (HEADS2 * CHUNK)
    with ExitStack() as tmp:
        rest = k.sbuf("hg_rest", [P, HEADS2, T], ctx=tmp)
        ktok = k.sbuf("hg_ktok", [CHUNK, 2, HEADS2 * P], ctx=tmp)
        vtok = k.sbuf("hg_vtok", [CHUNK, 2, HEADS2 * P], ctx=tmp)
        state = k.sbuf("hg_state", [P, 2, HEADS2, P], ctx=tmp)
        prepared = Signal(tmp, nc, "hg_prepared")
        turned = Signal(tmp, nc, "hg_turned")
        copied = Signal(tmp, nc, "hg_copied")
        multiplied = Signal(tmp, nc, "hg_outer_ready")
        stated = Signal(tmp, nc, "hg_state_ready")
        read = Signal(tmp, nc, "hg_state_read")
        gathered = Signal(tmp, nc, "hg_gathered")
        with nc.Block() as block:
            @block.tensor
            def _(pe):
                def turn(c):
                    if c >= 2:
                        pe.wait_ge(copied.sem, c - 1)
                    own = slice(c * CHUNK, (c + 1) * CHUNK)
                    for h in range(HEADS2):
                        pe.transpose(k.ps[0:CHUNK, c % 2, h * P:(h + 1) * P], key[:, h, own], k.ident[:])
                        tr = pe.transpose(k.ps[0:CHUNK, 2 + c % 2, h * P:(h + 1) * P], v[:, h, own], k.ident[:])
                    tr.then_inc(turned.sem, 1)

                pe.wait_ge(prepared.sem, 1)
                turn(0)
                for c in range(NCH - 1):
                    if c + 1 < NCH - 1:
                        turn(c + 1)
                    pe.wait_ge(copied.sem, c + 1)
                    if c >= 2:
                        pe.wait_ge(stated.sem, c - 1)
                    for h in range(HEADS2):
                        mm = pe.matmul(k.ps[:, 4 + c % 2, h * P:(h + 1) * P], ktok[:, c % 2, h * P:(h + 1) * P],
                                       vtok[:, c % 2, h * P:(h + 1) * P], start=True, stop=True)
                    mm.then_inc(multiplied.sem, 1)
                    n = c + 1
                    pe.wait_ge(stated.sem, n)
                    if n // per >= 2 and n % per == 0:
                        pe.wait_ge(gathered.sem, n // per - 1)
                    for h in range(HEADS2):
                        at = (h * per + n % per) * CHUNK
                        mm = pe.matmul(k.ps[:, 6 + (n // per) % 2, at:at + CHUNK], state[:, c % 2, h],
                                       q[:, h, n * CHUNK:(n + 1) * CHUNK], start=True, stop=True)
                    mm.then_inc(read.sem, 1)

            @block.scalar
            def _(act):
                for c in range(NCH - 1):
                    act.wait_ge(turned.sem, c + 1)
                    if c >= 2:
                        act.wait_ge(multiplied.sem, c - 1)
                    act.activation(ktok[:, c % 2], k.ps[0:CHUNK, c % 2], ACT.Copy)
                    act.activation(vtok[:, c % 2], k.ps[0:CHUNK, 2 + c % 2], ACT.Copy).then_inc(copied.sem, 1)

            @block.vector
            def _(dve):
                step = lambda ins: k.dve_steps.then(dve, ins)
                rl, fl = lanes(rest), lanes(f)
                step(dve.memset(rl[:, :, CHUNK - 1:], 1.0))
                for j in range(CHUNK - 2, -1, -1):
                    step(dve.tensor_tensor(rl[:, :, j:j + 1], rl[:, :, j + 1:j + 2], fl[:, :, j + 1:j + 2], ALU.mult))
                step(dve.tensor_tensor(key[:], key[:], rest[:], ALU.mult))
                dve.tensor_tensor(q, q, start[:], ALU.mult).then_inc(prepared.sem, 1)
                for c in range(NCH):
                    if c < NCH - 1:
                        dve.wait_ge(multiplied.sem, c + 1)
                        if c >= 2:
                            dve.wait_ge(read.sem, c - 1)
                        if c == 0:
                            ins = dve.tensor_copy(state[:, 0], k.ps[:, 4].rearrange("p (h n) -> p h n", h=HEADS2))
                        else:
                            for h in range(HEADS2):
                                last = (c + 1) * CHUNK - 1
                                ins = dve.scalar_tensor_tensor(state[:, c % 2, h], state[:, (c - 1) % 2, h],
                                                               start[:, h, last:last + 1],
                                                               k.ps[:, 4 + c % 2, h * P:(h + 1) * P], ALU.mult, ALU.add)
                        ins.then_inc(stated.sem, 1)
                        dve.wait_ge(stated.sem, c + 1)
                    if c % per == per - 1:
                        b = c // per
                        lo = 1 if b == 0 else 0
                        dve.wait_ge(read.sem, c)
                        mine = out[:, :, (b * per + lo) * CHUNK:(b + 1) * per * CHUNK]
                        got = k.ps[:, 6 + b % 2].rearrange("p (h n) -> p h n", h=HEADS2)[:, :, lo * CHUNK:]
                        dve.tensor_tensor(mine, mine, got, ALU.add).then_inc(gathered.sem, 1)


def hgrn_finish(k, gate, out):
    nc = k.nc
    with ExitStack() as tmp:
        sq = k.sbuf("hg_sq", [P, HEADS2, T], ctx=tmp)
        squared = Signal(tmp, nc, "hg_squared")
        summed = Signal(tmp, nc, "hg_squares_summed")
        mean = Signal(tmp, nc, "hg_mean_ready")
        root = Signal(tmp, nc, "hg_root_ready")
        with nc.Block() as block:
            @block.scalar
            def _(act):
                act.activation(sq[:], out, ACT.Square).then_inc(squared.sem, 1)
                act.wait_ge(mean.sem, 1)
                act.activation(sq[:], sq[:], ACT.Sqrt).then_inc(root.sem, 1)

            @block.tensor
            def _(pe):
                pe.wait_ge(squared.sem, 1)
                for h in range(HEADS2):
                    mm = pe.matmul(k.ps[:, h], k.ones[:], sq[:, h], start=True, stop=True)
                mm.then_inc(summed.sem, 1)

            @block.vector
            def _(dve):
                step = lambda ins: k.dve_steps.then(dve, ins)
                dve.wait_ge(summed.sem, 1)
                dve.tensor_scalar(sq[:], k.ps[:, 0:HEADS2], 1.0 / P, EPS, ALU.mult, ALU.add).then_inc(mean.sem, 1)
                dve.wait_ge(root.sem, 1)
                step(dve.reciprocal(sq[:], sq[:]))
                step(dve.tensor_tensor(sq[:], sq[:], gate, ALU.mult))
                step(dve.tensor_scalar(sq[:], sq[:], k.vec("gn"), None, ALU.mult))
                step(dve.tensor_tensor(out, out, sq[:], ALU.mult))


def spread(dve, src, dst, scale):
    to = dst.rearrange("p (a r) n -> p a r n", r=4)
    of = src.rearrange("p (a r) n -> p a r n", r=4)
    for r in range(4):
        for s in range(2):
            rows = slice(64 * s, 64 * (s + 1))
            at = 32 * r + 16 * s
            ins = dve.tensor_scalar(to[rows, :, r, at:at + 16], of[rows, :, r, :], scale, None, ALU.mult)
    return ins


def s5(k, u, out):
    nc = k.nc
    HALF = S5T // 2
    with ExitStack() as ctx:
        b_t = k.sbuf("s5_b_t", [P, 2, S5T, P], ctx=ctx)
        c_x = k.sbuf("s5_c_x", [P, 2, S5T, P], ctx=ctx)
        mag = k.sbuf("s5_mag", [P, S5T], ctx=ctx)
        unit = k.sbuf("s5_unit", [P, 2, S5T], ctx=ctx)
        with ExitStack() as tmp:
            load = k.sbuf("s5_load", [P, 4, S5T, 16], ctx=tmp)
            bb = k.sbuf("s5_bb", [P, 3, S5T, 16], ctx=tmp)
            s = k.sbuf("s5_small", [P, 10, S5T], ctx=tmp)
            loads = Signal(tmp, nc, "s5_loaded")
            handed = Signal(tmp, nc, "s5_to_act")
            acted = Signal(tmp, nc, "s5_act_done")
            with nc.Block() as block:
                @block.sync
                def _(sp):
                    for n, name in enumerate(("b_re", "b_im", "c_re", "c_im")):
                        sp.dma_start(load[:, n], k.dram["s5_" + name]).then_inc(loads.sem, 16)

                @block.scalar
                def _(act):
                    act.activation(s[:, 0], k.vec("log_dt"), ACT.Exp).then_inc(acted.sem, 1)
                    act.wait_ge(handed.sem, 1)
                    act.activation(mag[:], s[:, 1], ACT.Exp).then_inc(acted.sem, 1)
                    act.wait_ge(handed.sem, 2)
                    act.activation(unit[:, 0], s[:, 5], ACT.Sin).then_inc(acted.sem, 1)
                    act.activation(unit[:, 1], s[:, 4], ACT.Sin).then_inc(acted.sem, 1)

                @block.vector
                def _(dve):
                    step = lambda ins: k.dve_steps.then(dve, ins)
                    tt = lambda o, a, b, op: step(dve.tensor_tensor(o, a, b, op))
                    ar, ai = k.vec("a_re"), k.vec("a_im")
                    step(dve.memset(b_t[:], 0.0))
                    step(dve.memset(c_x[:], 0.0))
                    dve.wait_ge(acted.sem, 1)
                    dve.tensor_tensor(s[:, 1], ar, s[:, 0], ALU.mult).then_inc(handed.sem, 1)
                    tt(s[:, 2], ai, s[:, 0], ALU.mult)
                    reduce_angle(k, dve, s[:, 2], s[:, 3], s[:, 4], s[:, 5])
                    dve.sem_inc(handed.sem, 1)
                    dve.wait_ge(acted.sem, 4)
                    tt(s[:, 0], mag[:], unit[:, 0], ALU.mult)
                    step(dve.tensor_scalar(s[:, 0], s[:, 0], -1.0, None, ALU.add))
                    tt(s[:, 1], mag[:], unit[:, 1], ALU.mult)
                    tt(s[:, 2], ar, ar, ALU.mult)
                    tt(s[:, 3], ai, ai, ALU.mult)
                    tt(s[:, 2], s[:, 2], s[:, 3], ALU.add)
                    step(dve.reciprocal(s[:, 2], s[:, 2]))
                    tt(s[:, 3], s[:, 0], ar, ALU.mult)
                    tt(s[:, 4], s[:, 1], ai, ALU.mult)
                    tt(s[:, 3], s[:, 3], s[:, 4], ALU.add)
                    tt(s[:, 6], s[:, 3], s[:, 2], ALU.mult)
                    tt(s[:, 3], s[:, 1], ar, ALU.mult)
                    tt(s[:, 4], s[:, 0], ai, ALU.mult)
                    tt(s[:, 3], s[:, 3], s[:, 4], ALU.subtract)
                    tt(s[:, 7], s[:, 3], s[:, 2], ALU.mult)
                    dve.wait_ge(loads.sem, 64)
                    wide = lambda n: s[:, n].unsqueeze(2).to_broadcast((P, S5T, 16))
                    tt(bb[:, 0], load[:, 0], wide(6), ALU.mult)
                    tt(bb[:, 2], load[:, 1], wide(7), ALU.mult)
                    tt(bb[:, 0], bb[:, 0], bb[:, 2], ALU.subtract)
                    tt(bb[:, 1], load[:, 1], wide(6), ALU.mult)
                    tt(bb[:, 2], load[:, 0], wide(7), ALU.mult)
                    tt(bb[:, 1], bb[:, 1], bb[:, 2], ALU.add)
                    for n in range(2):
                        step(spread(dve, bb[:, n], b_t[:, n], 1.0))
                        step(spread(dve, load[:, 2 + n], c_x[:, n], 1.0 if n == 0 else -1.0))
        squares = [b_t[:, n, t] for n in range(2) for t in range(S5T)]
        token_major(k, "s5_b", squares, squares)
        y = k.sbuf("s5_y", [P, 4, T], ctx=ctx)
        with ExitStack() as tmp:
            turn = k.sbuf("s5_turn", [P, 2, HALF, T], ctx=tmp)
            s5_scan(k, u, y, turn, unit, mag, b_t, c_x)
        s5_glu(k, y, out)


def s5_scan(k, u, y, turn, unit, mag, b_t, c_x):
    nc = k.nc
    HALF = S5T // 2
    with ExitStack() as tmp:
        part = k.sbuf("s5_part", [P, 2, T], ctx=tmp)
        w = k.sbuf("s5_w", [P, 2, 2, T], ctx=tmp)
        x = k.sbuf("s5_x", [P, 2, 2, T], ctx=tmp)
        ppart = k.sbuf("s5_pool_part", [P, T], ctx=tmp)
        dbl = k.sbuf("s5_double", [P, 2, 2, S5T], ctx=tmp)
        fed = Signal(tmp, nc, "s5_inputs_ready")
        rotated = Signal(tmp, nc, "s5_inputs_read")
        scanned = Signal(tmp, nc, "s5_scanned")
        real = Signal(tmp, nc, "s5_real_ready")
        imag = Signal(tmp, nc, "s5_imag_ready")
        done = Signal(tmp, nc, "s5_tile_multiplied")
        skipped = Signal(tmp, nc, "s5_skip_added")
        with nc.Block() as block:
            @block.tensor
            def _(pe):
                def feed(t):
                    if t >= 2:
                        pe.wait_ge(rotated.sem, t - 1)
                    for n in range(2):
                        mm = pe.matmul(k.ps[:, 2 * (t % 2) + n], b_t[:, n, t], u[:, t // 4], start=True, stop=True)
                    mm.then_inc(fed.sem, 1)

                feed(0)
                for t in range(S5T):
                    if t + 1 < S5T:
                        feed(t + 1)
                    bank = 4 + (t // 4) % 2
                    if t % 4 == 0 and t >= 8:
                        pe.wait_ge(skipped.sem, t // 4 - 1)
                    pe.wait_ge(real.sem, t + 1)
                    pe.matmul(k.ps[:, bank], c_x[:, 0, t], x[:, t % 2, 0], start=t % 4 == 0, stop=False)
                    pe.wait_ge(imag.sem, t + 1)
                    pe.matmul(k.ps[:, bank], c_x[:, 1, t], x[:, t % 2, 1], start=False, stop=t % 4 == 3)\
                      .then_inc(done.sem, 1)

            @block.gpsimd
            def _(pool):
                for t in range(S5T):
                    cos, sin = turn[:, 0, t % HALF], turn[:, 1, t % HALF]
                    pool.wait_ge(scanned.sem, t + 1)
                    if t >= 2:
                        pool.wait_ge(done.sem, t - 1)
                    pool.tensor_tensor(ppart[:], sin, w[:, t % 2, 1], ALU.mult)
                    k.pool_steps.then(pool, pool.tensor_tensor(x[:, t % 2, 0], cos, w[:, t % 2, 0], ALU.mult))
                    pool.tensor_tensor(x[:, t % 2, 0], x[:, t % 2, 0], ppart[:], ALU.subtract).then_inc(real.sem, 1)
                    pool.wait_ge(real.sem, t + 1)

            @block.vector
            def _(dve):
                step = lambda ins: k.dve_steps.then(dve, ins)
                tt = lambda o, a, b, op: step(dve.tensor_tensor(o, a, b, op))

                def tables(half):
                    own = slice(half * HALF, (half + 1) * HALF)
                    c, s = turn[:, 0], turn[:, 1]
                    dve.memset(c[:, :, 0:1], 1.0)
                    step(dve.memset(s[:, :, 0:1], 0.0))
                    step(dve.tensor_copy(dbl[:, 0, :, 0:HALF], unit[:, :, own]))
                    n, m = 1, 0
                    while n < T:
                        ca, sa = dbl[:, m, 0, 0:HALF], dbl[:, m, 1, 0:HALF]
                        cw, sw = (a.unsqueeze(2).to_broadcast((P, HALF, n)) for a in (ca, sa))
                        lo, hi = slice(0, n), slice(n, 2 * n)
                        cols = part[:].rearrange("p a t -> p (a t)")
                        done_ = 0
                        fit = min(HALF, 2 * T // n)
                        while done_ < HALF:
                            g = slice(done_, done_ + fit)
                            tmp_ = cols[:, 0:fit * n].rearrange("p (g t) -> p g t", t=n)
                            tt(tmp_, s[:, g, lo], sw[:, g], ALU.mult)
                            tt(c[:, g, hi], c[:, g, lo], cw[:, g], ALU.mult)
                            tt(c[:, g, hi], c[:, g, hi], tmp_, ALU.subtract)
                            tt(tmp_, c[:, g, lo], sw[:, g], ALU.mult)
                            tt(s[:, g, hi], s[:, g, lo], cw[:, g], ALU.mult)
                            tt(s[:, g, hi], s[:, g, hi], tmp_, ALU.add)
                            done_ += fit
                        c2, s2 = dbl[:, 1 - m, 0, 0:HALF], dbl[:, 1 - m, 1, 0:HALF]
                        tt(c2, ca, ca, ALU.mult)
                        tt(s2, sa, sa, ALU.mult)
                        tt(c2, c2, s2, ALU.subtract)
                        tt(s2, ca, sa, ALU.mult)
                        step(dve.tensor_scalar(s2, s2, 2.0, None, ALU.mult))
                        n, m = 2 * n, 1 - m

                for t in range(S5T):
                    if t % HALF == 0:
                        if t:
                            dve.wait_ge(real.sem, t)
                        tables(t // HALF)
                    cos, sin = turn[:, 0, t % HALF], turn[:, 1, t % HALF]
                    br, bi = k.ps[:, 2 * (t % 2)], k.ps[:, 2 * (t % 2) + 1]
                    wr, wi = w[:, t % 2, 0], w[:, t % 2, 1]
                    dve.wait_ge(fed.sem, t + 1)
                    if t >= 2:
                        dve.wait_ge(real.sem, t - 1)
                    dve.tensor_tensor(part[:, 0], br, cos, ALU.mult)
                    tt(part[:, 1], bi, sin, ALU.mult)
                    tt(wr, part[:, 0], part[:, 1], ALU.add)
                    dve.tensor_tensor(part[:, 0], bi, cos, ALU.mult)
                    dve.tensor_tensor(part[:, 1], br, sin, ALU.mult).then_inc(rotated.sem, 1)
                    dve.wait_ge(rotated.sem, t + 1)
                    tt(wi, part[:, 0], part[:, 1], ALU.subtract)
                    decay = mag[:, t:t + 1].to_broadcast((P, T))
                    dve.tensor_tensor_scan(wr, decay, wr, 0.0, ALU.mult, ALU.add)
                    dve.tensor_tensor_scan(wi, decay, wi, 0.0, ALU.mult, ALU.add).then_inc(scanned.sem, 1)
                    dve.wait_ge(scanned.sem, t + 1)
                    if t >= 2:
                        dve.wait_ge(done.sem, t - 1)
                    dve.tensor_tensor(part[:, 0], wi, cos, ALU.mult)
                    tt(part[:, 1], wr, sin, ALU.mult)
                    dve.tensor_tensor(x[:, t % 2, 1], part[:, 0], part[:, 1], ALU.add).then_inc(imag.sem, 1)
                    dve.wait_ge(imag.sem, t + 1)
                    if t % 4 == 3:
                        m = t // 4
                        dve.wait_ge(done.sem, t + 1)
                        dve.scalar_tensor_tensor(y[:, m], u[:, m], k.vec("d_skip")[:, m:m + 1], k.ps[:, 4 + m % 2],
                                                 ALU.mult, ALU.add).then_inc(skipped.sem, 1)


def s5_glu(k, y, out):
    nc = k.nc
    with ExitStack() as tmp:
        w = k.sbuf("glu_w", [P, 4, 512], ctx=tmp)
        loads = Signal(tmp, nc, "glu_loaded")
        acted = Signal(tmp, nc, "glu_gelu_ready")
        gated = Signal(tmp, nc, "glu_gate_ready")
        product = Signal(tmp, nc, "glu_product_ready")
        with nc.Block() as block:
            @block.sync
            def _(sp):
                sp.dma_start(w[:], k.dram["glu_w"]).then_inc(loads.sem, 16)

            @block.scalar
            def _(act):
                for m in range(4):
                    act.activation(y[:, m], y[:, m], ACT.Gelu).then_inc(acted.sem, 1)
                for m in range(4):
                    act.wait_ge(product.sem, m + 1)
                    act.activation(out[:, m], k.ps[:, m], ACT.Sigmoid, bias=k.vec("glu_b")[:, m:m + 1])\
                       .then_inc(gated.sem, 1)

            @block.tensor
            def _(pe):
                pe.wait_ge(loads.sem, 16)
                pe.wait_ge(acted.sem, 4)
                for m in range(4):
                    for x in range(4):
                        mm = pe.matmul(k.ps[:, m], w[:, x, m * P:(m + 1) * P], y[:, x], start=x == 0, stop=x == 3)
                    mm.then_inc(product.sem, 1)

            @block.vector
            def _(dve):
                for m in range(4):
                    dve.wait_ge(gated.sem, m + 1)
                    dve.tensor_tensor(out[:, m], out[:, m], y[:, m], ALU.mult)


def mixer2(k, gain):
    scaled_gain(k, "norm_mix_w_2", k.mod[:, KD:2 * KD], gain[:, 0])
    norm(k, gain[:, 0], k.u, k.mod[:, 0:KD])
    with ExitStack() as ctx:
        proj = k.sbuf("proj2", [P, 20, T], ctx=ctx)
        copy_tiles(k, k.dram["w_in_2"], 20, proj, lambda x: k.u[:, x])
        hgrn(k, proj, k.u[:, 0:4])
        s5(k, proj[:, 16:20], k.u[:, 4:8])
    residual(k, k.dram["w_out_2"], KD, lambda x: k.u[:, x], k.mod[:, 2 * KD:3 * KD])


PH = 8
TOPK = 16
ROUNDS = 2
I1 = P // ROUNDS
LOW = -3.0e38


def top16(k, dve, src, work, values, index):
    step = lambda ins: k.dve_steps.then(dve, ins)
    step(dve.max(values[:, 0:8], src))
    dve.max_index(index[:, 0:8], values[:, 0:8], src)
    step(dve.match_replace(work, values[:, 0:8], src, LOW))
    step(dve.max(values[:, 8:16], work))
    return dve.max_index(index[:, 8:16], values[:, 8:16], work)


def route(k, by_choice):
    nc = k.nc
    with ExitStack() as ctx:
        q = k.sbuf("peer_q", [P, 2 * PH, T], ctx=ctx)
        keys = k.sbuf("peer_keys", [P, 2, P], ctx=ctx)
        copy_tiles(k, k.dram["peer_wq"], 2 * PH, q, lambda x: k.u[:, x])
        work = k.sbuf("peer_work", [P, 2 * P], ctx=ctx)
        best = k.sbuf("peer_best", [P, PH, 2, TOPK], ctx=ctx)
        which = k.sbuf("peer_which", [P, PH, 2, TOPK], U32, ctx)
        whichf = k.sbuf("peer_whichf", [P, PH, 2, TOPK], ctx=ctx)
        cand = k.sbuf("peer_cand", [P, PH, TOPK, TOPK], ctx=ctx)
        top = k.sbuf("peer_top", [P, PH, TOPK], ctx=ctx)
        place = k.sbuf("peer_place", [P, PH, TOPK], U32, ctx)
        part = k.sbuf("peer_part", [P, 2, PH, TOPK], U32, ctx)
        partf = k.sbuf("peer_partf", [P, 2, PH * TOPK], ctx=ctx)
        hot = k.sbuf("peer_hot", [P, PH * TOPK, TOPK], ctx=ctx)
        chosen = k.sbuf("peer_chosen", [P, QT, 3, PH * TOPK], ctx=ctx)
        count = k.sbuf("peer_count", [P, TOPK], ctx=ctx)
        total = k.sbuf("peer_total", [P, PH], ctx=ctx)
        loads = Signal(ctx, nc, "peer_keys_loaded")
        counted = Signal(ctx, nc, "peer_count_ready")
        scored = Signal(ctx, nc, "peer_scored")
        ranked = Signal(ctx, nc, "peer_ranked")
        shifted = Signal(ctx, nc, "peer_shifted")
        exped = Signal(ctx, nc, "peer_exped")
        with nc.Block() as block:
            @block.sync
            def _(sp):
                sp.dma_start(keys[:], k.dram["peer_keys"]).then_inc(loads.sem, 16)

            @block.gpsimd
            def _(pool):
                pool.iota(count[:], pattern=[[1, TOPK]], base=0, channel_multiplier=0,
                          allow_small_or_imprecise_dtypes=True).then_inc(counted.sem, 1)

            @block.tensor
            def _(pe):
                pe.wait_ge(loads.sem, 16)
                for n in range(QT * 4):
                    qt, quad = n // 4, n % 4
                    if n >= BANKS:
                        pe.wait_ge(ranked.sem, n - BANKS + 1)
                    for m in range(4):
                        t = 4 * quad + m
                        mm = pe.matmul(k.ps[:, n % BANKS, m * P:(m + 1) * P], q[:, t, qt * P:(qt + 1) * P],
                                       keys[:, t % 2], start=True, stop=True)
                    mm.then_inc(scored.sem, 1)

            @block.scalar
            def _(act):
                for qt in range(QT):
                    act.wait_ge(shifted.sem, qt + 1)
                    gate = chosen[:, qt, 2]
                    act.activation(gate, gate, ACT.Exp).then_inc(exped.sem, 1)

            @block.vector
            def _(dve):
                step = lambda ins: k.dve_steps.then(dve, ins)
                tt = lambda o, a, b, op: step(dve.tensor_tensor(o, a, b, op))
                dve.wait_ge(counted.sem, 1)
                for qt in range(QT):
                    for quad in range(4):
                        n = qt * 4 + quad
                        dve.wait_ge(scored.sem, n + 1)
                        for m in range(4):
                            t = 4 * quad + m
                            ins = top16(k, dve, k.ps[:, n % BANKS, m * P:(m + 1) * P], work[:, 0:P],
                                        best[:, t // 2, t % 2], which[:, t // 2, t % 2])
                            step(ins)
                        dve.sem_inc(ranked.sem, 1)
                    step(dve.tensor_copy(whichf[:], which[:]))
                    first = best[:, :, 0].unsqueeze(3).to_broadcast((P, PH, TOPK, TOPK))
                    second = best[:, :, 1].unsqueeze(2).to_broadcast((P, PH, TOPK, TOPK))
                    tt(cand[:], first, second, ALU.add)
                    for h in range(PH):
                        step(top16(k, dve, cand[:, h].rearrange("p a b -> p (a b)"), work[:], top[:, h], place[:, h]))
                    gate = chosen[:, qt, 2].rearrange("p (h c) -> p h c", h=PH)
                    dve.tensor_tensor(gate, top[:], top[:, :, 0:1].to_broadcast((P, PH, TOPK)), ALU.subtract)\
                       .then_inc(shifted.sem, 1)
                    dve.tensor_scalar(part[:, 0], place[:], 4, None, ALU.logical_shift_right)
                    step(dve.tensor_scalar(part[:, 1], place[:], 15, None, ALU.bitwise_and))
                    step(dve.tensor_copy(partf[:], part[:].rearrange("p s h c -> p s (h c)")))
                    for s in range(2):
                        at = partf[:, s].unsqueeze(2).to_broadcast((P, PH * TOPK, TOPK))
                        tt(hot[:], at, count[:].unsqueeze(1).to_broadcast((P, PH * TOPK, TOPK)), ALU.is_equal)
                        names = whichf[:, :, s].unsqueeze(2).to_broadcast((P, PH, TOPK, TOPK))
                        view = hot[:].rearrange("p (h c) a -> p h c a", h=PH)
                        tt(view, view, names, ALU.mult)
                        step(dve.tensor_reduce(chosen[:, qt, s], hot[:], AX.X, ALU.add))
                    dve.wait_ge(exped.sem, qt + 1)
                    step(dve.tensor_reduce(total[:], gate, AX.X, ALU.add))
                    step(dve.reciprocal(total[:], total[:]))
                    tt(gate, gate, total[:].unsqueeze(2).to_broadcast((P, PH, TOPK)), ALU.mult)
        token_major(k, "choices", [chosen[:, qt, s] for s in range(3) for qt in range(QT)],
                    [by_choice[:, s, qt * P:(qt + 1) * P] for s in range(3) for qt in range(QT)])


TOK = 8


def expert_weights(k, r, by_choice, weight, sig):
    nc = k.nc
    counted, rows_ready, cols_ready, product, copied = sig
    iters = T // (2 * TOK)
    with ExitStack() as tmp:
        rows = k.sbuf("hot_i2", [P, 2, TOK, P], ctx=tmp)
        cols = k.sbuf("hot_i1", [P, 2, TOK, I1], ctx=tmp)
        count = k.sbuf("hot_count", [P, P], ctx=tmp)
        with nc.Block() as block:
            @block.gpsimd
            def _(pool):
                pool.iota(count[:], pattern=[[1, P]], base=0, channel_multiplier=0,
                          allow_small_or_imprecise_dtypes=True).then_inc(counted.sem, 1)
                with pool.Fori(0, iters) as i:
                    for b in range(2):
                        gates = by_choice[:, 2, bass.ds(i * (2 * TOK) + b * TOK, TOK)]
                        pool.wait_ge(cols_ready[b].sem, i * 2 + cols_ready[b].at(1))
                        pool.tensor_tensor(cols[:, b], cols[:, b], gates.unsqueeze(2).to_broadcast((P, TOK, I1)),
                                           ALU.mult).then_inc(cols_ready[b].sem, 1)

            @block.vector
            def _(dve):
                dve.wait_ge(counted.sem, counted.at(1))
                with dve.Fori(0, iters) as i:
                    for b in range(2):
                        dve.wait_ge(product[b].sem, i + product[b].at(0))
                        mine = by_choice[:, 0:2, bass.ds(i * (2 * TOK) + b * TOK, TOK)]
                        names = count[:, r * I1:(r + 1) * I1].unsqueeze(1).to_broadcast((P, TOK, I1))
                        dve.tensor_tensor(cols[:, b], mine[:, 0].unsqueeze(2).to_broadcast((P, TOK, I1)), names,
                                          ALU.is_equal).then_inc(cols_ready[b].sem, 1)
                        dve.tensor_tensor(rows[:, b], mine[:, 1].unsqueeze(2).to_broadcast((P, TOK, P)),
                                          count[:].unsqueeze(1).to_broadcast((P, TOK, P)), ALU.is_equal)\
                           .then_inc(rows_ready[b].sem, 1)

            @block.tensor
            def _(pe):
                with pe.Fori(0, iters) as i:
                    for b in range(2):
                        pe.wait_ge(rows_ready[b].sem, i + rows_ready[b].at(1))
                        pe.wait_ge(cols_ready[b].sem, i * 2 + cols_ready[b].at(2))
                        pe.wait_ge(copied[b].sem, i + copied[b].at(0))
                        for t in range(TOK):
                            mm = pe.matmul(k.ps[:, b, t * I1:(t + 1) * I1], rows[:, b, t], cols[:, b, t],
                                           start=True, stop=True)
                        mm.then_inc(product[b].sem, 1)

            @block.scalar
            def _(act):
                with act.Fori(0, iters) as i:
                    for b in range(2):
                        act.wait_ge(product[b].sem, i + product[b].at(1))
                        act.activation(weight[:, :, bass.ds(i * (2 * TOK) + b * TOK, TOK)].rearrange("p e t -> p t e"),
                                       k.ps[:, b].rearrange("p (t e) -> p t e", t=TOK), ACT.Copy)\
                           .then_inc(copied[b].sem, 1)
    counted.passed(1)
    for b in range(2):
        rows_ready[b].passed(iters)
        cols_ready[b].passed(2 * iters)
        product[b].passed(iters)
        copied[b].passed(iters)


def experts(k, r, weight, gate, sig):
    nc = k.nc
    gelu_ready, gelu_used, coef_ready = sig
    with ExitStack() as tmp:
        acted = k.sbuf("expert_act", [P, 2, T], ctx=tmp)
        coef = k.sbuf("expert_coef", [P, 8, T], ctx=tmp)
        iters = I1 // 8
        base = r * I1

        def source(name, j):
            return lambda i: k.dram[name][bass.ds(i * 8 + (base + j), 1), :, :].rearrange("a p n -> p (a n)")

        def coef_is_ready(pe, i):
            pe.wait_ge(coef_ready.sem, i * 8 + coef_ready.at(8))

        chunks = [(source("peer_u", e), [(e % 4, k.ps[:, e % 4], [(x, k.u[:, x]) for x in range(KD)], True, True, None)])
                  for e in range(8)]
        chunks += [(source("peer_v", d), [(4 + d % 4, k.ps[:, 4 + d % 4], [(x, coef[:, x]) for x in range(8)],
                                           True, True, coef_is_ready if d == 0 else None)]) for d in range(KD)]
        stream = Stream(k, iters, chunks)
        with nc.Block() as block:
            @block.sync
            def _(sp):
                stream.load(sp)

            @block.tensor
            def _(pe):
                stream.multiply(pe)

            @block.scalar
            def _(act):
                with act.Fori(0, iters) as i:
                    for e in range(8):
                        stream.wait_products(act, i, e)
                        act.wait_ge(gelu_used[e % 2].sem, i * 4 + gelu_used[e % 2].at(e // 2))
                        act.activation(acted[:, e % 2], k.ps[:, e % 4], ACT.Gelu).then_inc(gelu_ready.sem, 1)

            @block.vector
            def _(dve):
                with dve.Fori(0, iters) as i:
                    for e in range(8):
                        dve.wait_ge(gelu_ready.sem, i * 8 + gelu_ready.at(e + 1))
                        dve.sem_inc(k.emptied[e % 4].sem, 1)
                        dve.tensor_tensor(coef[:, e], acted[:, e % 2], one(weight, i * 8 + e), ALU.mult)\
                           .then_inc(coef_ready.sem, 1)
                        dve.wait_ge(coef_ready.sem, i * 8 + coef_ready.at(e + 1))
                        dve.sem_inc(gelu_used[e % 2].sem, 1)
                    for d in range(KD):
                        stream.wait_products(dve, i, 8 + d)
                        dve.scalar_tensor_tensor(k.h[:, d], k.ps[:, 4 + d % 4], gate[:, d:d + 1], k.h[:, d],
                                                 ALU.mult, ALU.add).then_inc(k.emptied[4 + d % 4].sem, 1)
        stream.finish()
    gelu_ready.passed(8 * iters)
    coef_ready.passed(8 * iters)
    for b in range(2):
        gelu_used[b].passed(4 * iters)


def peer(k, gain):
    nc = k.nc
    scaled_gain(k, "norm_ffn_w_2", k.mod[:, 4 * KD:5 * KD], gain[:, 1])
    norm(k, gain[:, 1], k.u, k.mod[:, 3 * KD:4 * KD])
    with ExitStack() as ctx:
        by_choice = k.sbuf("by_choice", [P, 3, T], ctx=ctx)
        route(k, by_choice)
        weight = k.sbuf("expert_weight", [P, I1, T], ctx=ctx)
        for r in range(ROUNDS):
            expert_weights(k, r, by_choice, weight, k.weight_signals)
            experts(k, r, weight, k.mod[:, 5 * KD:6 * KD], k.expert_signals)


def signals_of_loops(k):
    pair = lambda name, base=0: [k.new_sem(f"{name}{b}", base) for b in range(2)]
    k.ffn_signals = (pair("gated_ready"), pair("gated_used", 1))
    k.weight_signals = (k.new_sem("count_ready"), pair("rows_ready"), pair("cols_ready"),
                        pair("weights_ready", 1), pair("weights_copied", 1))
    k.expert_signals = (k.new_sem("gelu_ready"), pair("gelu_used", 1), k.new_sem("coef_ready"))
    with k.nc.Block() as block:
        @block.vector
        def _(dve):
            for b in range(2):
                dve.sem_inc(k.ffn_signals[1][b].sem, 1)
                dve.sem_inc(k.weight_signals[3][b].sem, 1)
                dve.sem_inc(k.weight_signals[4][b].sem, 1)
                dve.sem_inc(k.expert_signals[1][b].sem, 1)


def store(k):
    stored = k.new_sem("stored")
    with k.nc.Block() as block:
        @block.sync
        def _(sp):
            sp.dma_start(k.dram["y"], k.u[:]).then_inc(stored.sem, 16)
            sp.wait_ge(stored.sem, 16)


def build(nc, dram):
    with ExitStack() as ctx:
        k = Kernel(nc, ctx, dram)
        gain = k.sbuf("gain", [P, 2, KD])
        setup(k)
        signals_of_loops(k)
        ffn(k, "ffn1", k.vec("norm_ffn1"), k.ffn_signals)
        mixer1(k)
        ffn(k, "ffn2", k.vec("norm_ffn2"), k.ffn_signals)
        norm(k, k.vec("norm_final"), k.u)
        restart(k)
        modulation(k)
        mixer2(k, gain)
        peer(k, gain)
        norm(k, k.vec("final_norm_w_2"), k.u)
        store(k)


def restart(k):
    with k.nc.Block() as block:
        @block.vector
        def _(dve):
            dve.tensor_copy(k.h[:, 0:4], k.u[:, 0:4])

        @block.scalar
        def _(act):
            act.activation(k.h[:, 4:8], k.u[:, 4:8], ACT.Copy)



def tiles8(w):
    kin, n = w.shape
    return w.reshape(kin // P, P, n // P, P).transpose(2, 1, 0, 3).reshape(n // P, P, kin)


def down_chunks(w):
    c = np.zeros((KD, P, 3 * KD, P), w.dtype)
    c[:, :, :KF] = w.reshape(KF, P, KD, P).transpose(2, 1, 0, 3)
    return c.reshape(KD, P, 3, KD * P).transpose(0, 2, 1, 3).reshape(3 * KD, P, KD * P)


def features(v):
    return v.reshape(-1, P).T


def projection_columns():
    nq, kc, vc, ksl, vsl, kwn, vwn, ng, sq, sk, sv, ga, gb = np.cumsum(
        [0, 512, 128, 128, 128, 128, 128, 128, 24, 512, 64, 64, 1024])
    r = np.arange
    head = lambda base, a: r(base + HD * a, base + HD * (a + 1))
    tiles = [np.r_[head(nq, j), head(nq, 4 + j)] for j in range(4)]
    tiles += [r(ksl, ksl + P), r(kwn, kwn + P)]
    tiles += [np.r_[head(sq, j), head(sq, 4 + j)] for j in range(4)]
    tiles += [np.r_[head(sk, 0), head(sk, 0)]]
    tiles += [np.r_[head(kc, g), head(vc, g)] for g in range(2)]
    tiles += [r(vsl, vsl + P), r(vwn, vwn + P)]
    tiles += [np.r_[head(sv, 0), r(ng, ng + 24), np.full(P - HD - 24, -1)]]
    return np.concatenate(tiles + [r(ga, ga + D), r(gb, gb + D)])


def lay_out(a):
    g = {n: np.asarray(v) for n, v in a.items()}
    first = lambda n: g[n][0]
    out = {"x": g["x"][0].T.reshape(KD, P, T).transpose(1, 0, 2)}
    for n in (1, 2):
        gate, up = tiles8(first(f"ffn{n}_gate")), tiles8(first(f"ffn{n}_up"))
        out[f"ffn{n}_gu"] = np.stack([gate, up], 1).reshape(2 * KF, P, D)
        out[f"ffn{n}_down"] = down_chunks(first(f"ffn{n}_down"))
    w = first("w_in")
    w = np.concatenate([w, np.zeros((D, 1), w.dtype)], 1)[:, projection_columns()]
    out["w_in"] = tiles8(w)
    out["positions"] = g["positions"].astype(np.int32).reshape(1, T)
    w1 = np.concatenate([first(f"cmp_{n}_w1").reshape(32, HD, 256).transpose(1, 0, 2) for n in "kv"])
    out["cmp_w1"] = w1
    w2k, w2v = (first(f"cmp_{n}_w2").reshape(2, P, HD).transpose(1, 0, 2) for n in "kv")
    out["cmp_w2"] = np.concatenate([w2k, w2k, w2v], 2)
    out["cmp_pe"] = np.concatenate([first("cmp_pe_k").T, first("cmp_pe_v").T])
    ab = [first(n).reshape(4, P, KD, P).transpose(2, 1, 0, 3) for n in ("w_branch_a", "w_branch_b")]
    out["w_branch"] = np.concatenate(ab, 2).reshape(KD, P, D)
    out["w_out"] = tiles8(first("w_out"))
    out["ada_w"] = tiles8(first("ada_w_2"))
    out["w_in_2"] = tiles8(first("w_in_2"))
    out["w_out_2"] = tiles8(first("w_out_2"))
    out["peer_wq"] = tiles8(first("peer_wq_2"))
    out["peer_keys"] = np.stack([first("peer_keys1_2").T, first("peer_keys2_2").T], 1)
    out["peer_u"] = first("peer_u_2").reshape(P, P, KD, P).transpose(0, 3, 2, 1).reshape(P, P, D)
    out["peer_v"] = first("peer_v_2").reshape(P // 8, 8, P, KD, P).transpose(0, 3, 2, 1, 4).reshape(P, P, D)
    for n in ("b_re", "b_im"):
        out["s5_" + n] = first(f"s5_{n}_2").reshape(16, P, 16).transpose(1, 0, 2)
    for n in ("c_re", "c_im"):
        out["s5_" + n] = first(f"s5_{n}_2").transpose(0, 2, 1).reshape(16, P, 16).transpose(1, 0, 2)
    out["glu_w"] = first("s5_glu_w_2").reshape(4, P, 512).transpose(1, 0, 2)
    half = HD // 2
    freq = (np.float32(10000.0) ** (-np.arange(half, dtype=np.float32) / np.float32(half))).astype(np.float32)
    vecs = {n: features(g[n].reshape(-1)) for n in
            ("norm_ffn1", "norm_mix", "norm_ffn2", "norm_final", "norm_mix_w_2", "norm_ffn_w_2",
             "final_norm_w_2", "c_2", "ada_b_2")}
    vecs["lb0"], vecs["lb1"] = (features(g["hg_lower_bounds_2"][i]) for i in range(2))
    vecs["gn"] = features(first("hg_gnorm_w_2"))
    vecs["a_re"], vecs["a_im"] = features(first("s5_a_re_2").reshape(-1)), features(first("s5_a_im_2").reshape(-1))
    vecs["log_dt"] = features(np.repeat(first("s5_log_dt_2"), 64))
    vecs["d_skip"], vecs["glu_b"] = features(first("s5_d_2")), features(first("s5_glu_b_2"))
    vecs["sinks"] = np.broadcast_to(first("swa_sinks"), (P, 8))
    vecs["freq"] = np.tile(freq, P // half).reshape(P, 1)
    out["vecs"] = np.concatenate([vecs[n] for n in VEC], 1)
    return {n: np.ascontiguousarray(v) for n, v in out.items()}


def kernel(**inputs):
    import concourse.bacc as bacc
    from concourse.bass_utils import run_bass_kernel_spmd

    nc = bacc.Bacc("TRN2", target_bir_lowering=False, num_devices=1)
    arrays = lay_out(inputs)
    dram = {n: nc.dram_tensor(f"in_{n}", a.shape, mybir.dt.from_np(a.dtype), kind="ExternalInput").ap()
            for n, a in arrays.items()}
    dram["y"] = nc.dram_tensor("out_y", (P, KD, T), F32, kind="ExternalOutput").ap()
    build(nc, dram)
    r = run_bass_kernel_spmd(nc, [{f"in_{n}": a for n, a in arrays.items()}], core_ids=[0])
    y = r.results[0]["out_y"]
    return np.ascontiguousarray(y.transpose(1, 0, 2).reshape(D, T).T).reshape(1, T, D)
```

```python
from contextlib import ExitStack

import numpy as np

import concourse.bass as bass
from concourse import mybir

F32 = mybir.dt.float32
F32R = mybir.dt.float32r
I32 = mybir.dt.int32
BF16 = mybir.dt.bfloat16
U32 = mybir.dt.uint32
ALU = mybir.AluOpType
ACT = mybir.ActivationFunctionType
AX = mybir.AxisListType

P = 128
T = 512
D = 1024
KD = D // P
FF = 2816
KF = FF // P
HD = 64
QT = T // P
CMP = 31
EPS = 1e-6
NEG = -1e30
SLOTS = 4
PARTS = 2
BANKS = 8
SCALE = HD ** -0.5
TWO_PI = 2.0 * np.pi

Q0, KSL, KWN, SQ0, SK, KCA, KCB, VSL, VWN, SVG = 0, 4, 5, 6, 10, 11, 12, 13, 14, 15
ROPED = 11
PROJ = 16

VEC = {}
_at = 0
for _name, _n in (("norm_ffn1", 8), ("norm_mix", 8), ("norm_ffn2", 8), ("norm_final", 8),
                  ("norm_mix_w_2", 8), ("norm_ffn_w_2", 8), ("final_norm_w_2", 8), ("c_2", 8),
                  ("ada_b_2", 48), ("lb0", 4), ("lb1", 4), ("gn", 1), ("a_re", 16), ("a_im", 16),
                  ("log_dt", 16), ("d_skip", 4), ("glu_b", 4), ("sinks", 8), ("freq", 1)):
    VEC[_name] = (_at, _n)
    _at += _n
NVEC = _at


class Signal:

    def __init__(self, ctx, nc, name, base=0):
        self.sem = ctx.enter_context(nc.semaphore(name))
        self.base = base

    def at(self, n):
        return self.base + n

    def passed(self, n):
        self.base += n


class Steps:

    def __init__(self, ctx, nc, name):
        self.sem = ctx.enter_context(nc.semaphore(name))
        self.n = 0

    def then(self, eng, ins):
        self.n += 1
        ins.then_inc(self.sem, 1)
        eng.wait_ge(self.sem, self.n)


def one(ap, i):
    return ap[:, bass.ds(i, 1), :].rearrange("p a n -> p (a n)")


class Kernel:

    def __init__(self, nc, ctx, dram):
        self.nc, self.ctx, self.dram = nc, ctx, dram
        self.names = {}
        self.h = self.sbuf("h", [P, KD, T])
        self.u = Split(self, ctx, "u", KD)
        self.ring = self.sbuf("ring", [P, SLOTS, KD * P])
        self.high = self.sbuf("ring_high", [P, PARTS, KD * P], F32R)
        self.low = self.sbuf("ring_low", [P, PARTS, KD * P], F32R)
        self.vecs = self.sbuf("vecs", [P, NVEC])
        self.ident = self.sbuf("ident", [P, P])
        self.ones = self.sbuf("ones", [P, P])
        self.rs = self.sbuf("rs", [P, T])
        self.mod = self.sbuf("mod", [P, 6 * KD])
        self.ps = ctx.enter_context(nc.psum_tensor("ps", [P, BANKS, T], F32))
        self.dve_steps = Steps(ctx, nc, "dve_steps")
        self.act_steps = Steps(ctx, nc, "act_steps")
        self.pool_steps = Steps(ctx, nc, "pool_steps")
        self.loaded = [self.new_sem(f"slot{s}_loaded") for s in range(SLOTS)]
        self.high_ready = [self.new_sem(f"high{p}_ready") for p in range(PARTS)]
        self.low_ready = [self.new_sem(f"low{p}_ready", 2) for p in range(PARTS)]
        self.used = [self.new_sem(f"split{p}_used", 1) for p in range(PARTS)]
        self.emptied = [self.new_sem(f"bank{b}_emptied", 1) for b in range(BANKS)]
        self.first_ready = self.new_sem("first_ready")
        self.squares_ready = self.new_sem("squares_ready")
        self.sumsq_ready = self.new_sem("sumsq_ready")
        self.mean_ready = self.new_sem("mean_ready")
        self.root_ready = self.new_sem("root_ready")
        self.scaled_ready = self.new_sem("scaled_ready")
        self.rounded_ready = self.new_sem("rounded_ready")

    def sbuf(self, name, shape, dtype=F32, ctx=None):
        self.names[name] = self.names.get(name, 0) + 1
        if self.names[name] > 1:
            name = f"{name}_{self.names[name]}"
        return (ctx or self.ctx).enter_context(self.nc.sbuf_tensor(name, shape, dtype))

    def new_sem(self, name, base=0):
        return Signal(self.ctx, self.nc, name, base)

    def vec(self, name):
        at, n = VEC[name]
        return self.vecs[:, at:at + n]


class Split:

    def __init__(self, k, ctx, name, tiles):
        self.high = k.sbuf(f"{name}_high", [P, tiles, T], F32R, ctx)
        self.low = k.sbuf(f"{name}_low", [P, tiles, T], F32R, ctx)


class Stream:

    def __init__(self, k, iters, chunks):
        self.k, self.iters, self.chunks = k, iters, chunks
        assert len(chunks) % SLOTS == 0
        self.n = len(chunks)
        self.opened = [0] * BANKS
        for _, groups in chunks:
            for g in groups:
                self.opened[g[0]] += g[3]

    def load(self, sp):
        k = self.k
        with sp.Fori(0, self.iters) as i:
            for j, (source, _) in enumerate(self.chunks):
                s, p = j % SLOTS, j % PARTS
                src = source(i)
                sp.wait_ge(k.low_ready[p].sem, i * (self.n // PARTS) + k.low_ready[p].at(j // PARTS - 1))
                sp.dma_start(k.ring[:, s, 0:src.shape[-1]], src).then_inc(k.loaded[s].sem, 16)

    def split_high(self, act, i, j):
        k = self.k
        s, p = j % SLOTS, j % PARTS
        act.wait_ge(k.loaded[s].sem, i * (16 * self.n // SLOTS) + k.loaded[s].at(16 * (j // SLOTS + 1)))
        act.wait_ge(k.used[p].sem, i * (self.n // PARTS) + k.used[p].at(j // PARTS))
        act.activation(k.high[:, p], k.ring[:, s], ACT.Copy).then_inc(k.high_ready[p].sem, 1)

    def scalar(self, act, epilogue=None, after=None):
        def turn(i, j, ahead):
            if epilogue is not None:
                epilogue(i, j)
            if ahead:
                if j + PARTS < self.n:
                    self.split_high(act, i, j + PARTS)
                else:
                    self.split_high(act, i + 1, j + PARTS - self.n)
            if after is not None:
                after(i, j)

        for j in range(PARTS):
            self.split_high(act, 0, j)
        if self.iters > 1:
            with act.Fori(0, self.iters - 1) as i:
                for j in range(self.n):
                    turn(i, j, True)
        for j in range(self.n):
            turn(self.iters - 1, j, j + PARTS < self.n)

    def split_low(self, pool):
        k = self.k
        with pool.Fori(0, self.iters) as i:
            for j in range(self.n):
                s, p = j % SLOTS, j % PARTS
                pool.wait_ge(k.high_ready[p].sem, i * (self.n // PARTS) + k.high_ready[p].at(j // PARTS + 1))
                pool.tensor_tensor(k.low[:, p], k.ring[:, s], k.high[:, p].bitcast(F32), ALU.subtract)\
                    .then_inc(k.low_ready[p].sem, 1)

    def multiply(self, pe):
        k = self.k
        with pe.Fori(0, self.iters) as i:
            seen = [0] * BANKS
            for j, (_, groups) in enumerate(self.chunks):
                p = j % PARTS
                pe.wait_ge(k.low_ready[p].sem, i * (self.n // PARTS) + k.low_ready[p].at(j // PARTS + 1))
                for bank, out, parts, opens, closes, before in groups:
                    if opens:
                        pe.wait_ge(k.emptied[bank].sem, i * self.opened[bank] + k.emptied[bank].at(seen[bank]))
                        seen[bank] += 1
                    if before is not None:
                        before(pe, i)
                    for m, (tile, high, low) in enumerate(parts):
                        w = slice(tile * P, (tile + 1) * P)
                        first, final = opens and m == 0, closes and m == len(parts) - 1
                        pe.matmul(out, k.high[:, p, w], high, start=first, stop=False)
                        pe.matmul(out, k.high[:, p, w], low, start=False, stop=False)
                        last = pe.matmul(out, k.low[:, p, w], high, start=False, stop=final)
                last.then_inc(k.used[p].sem, 1)

    def wait_products(self, eng, i, j):
        p = j % PARTS
        eng.wait_ge(self.k.used[p].sem, i * (self.n // PARTS) + self.k.used[p].at(j // PARTS + 1))

    def finish(self):
        for s in range(SLOTS):
            self.k.loaded[s].passed(16 * self.n // SLOTS * self.iters)
        for p in range(PARTS):
            for sem in (self.k.high_ready, self.k.low_ready, self.k.used):
                sem[p].passed(self.n // PARTS * self.iters)
        for b in range(BANKS):
            self.k.emptied[b].passed(self.opened[b] * self.iters)


def chunk_of(weights, per_iter, j):
    return lambda i: weights[bass.ds(i * per_iter + j, 1), :, :].rearrange("a p n -> p (a n)")


def plain_stream(k, weights, tiles, unroll, kin, moving):
    per = -(-kin // KD)
    chunks = []
    for t in range(unroll):
        for c in range(per):
            parts = [(x - c * KD, moving.high[:, x], moving.low[:, x]) for x in range(c * KD, min(kin, (c + 1) * KD))]
            chunks.append((chunk_of(weights, unroll * per, t * per + c),
                           [(t, k.ps[:, t], parts, c == 0, c == per - 1, None)]))
    return Stream(k, tiles // unroll, chunks)


def split_tiles(k, name, source, to, at=0):
    nc = k.nc
    tiles = source.shape[1]
    with ExitStack() as tmp:
        rounded = Signal(tmp, nc, f"{name}_rounded")
        with nc.Block() as block:
            @block.scalar
            def _(act):
                for t in range(tiles):
                    act.activation(to.high[:, at + t], source[:, t], ACT.Copy).then_inc(rounded.sem, 1)

            @block.vector
            def _(dve):
                for t in range(tiles):
                    dve.wait_ge(rounded.sem, t + 1)
                    dve.tensor_tensor(to.low[:, at + t], source[:, t], to.high[:, at + t].bitcast(F32), ALU.subtract)


def setup(k):
    nc = k.nc
    h_in = k.dram["x"]
    with nc.Block() as block:
        @block.sync
        def _(sp):
            sp.dma_start(k.h[:], h_in).then_inc(k.first_ready.sem, 16)
            sp.dma_start(k.vecs[:], k.dram["vecs"]).then_inc(k.first_ready.sem, 16)
            sp.wait_ge(k.first_ready.sem, 32)

        @block.tensor
        def _(pe):
            for p in range(PARTS):
                pe.sem_inc(k.used[p].sem, 1)

        @block.vector
        def _(dve):
            dve.memset(k.ones[:], 1.0)
            for b in range(BANKS):
                dve.sem_inc(k.emptied[b].sem, 1)

        @block.gpsimd
        def _(pool):
            for p in range(PARTS):
                pool.sem_inc(k.low_ready[p].sem, 2)
            k.pool_steps.then(pool, pool.memset(k.ident[:], 0.0))
            k.pool_steps.then(pool, pool.affine_select(out=k.ident[:], in_=k.ident[:], compare_op=ALU.not_equal,
                                                       fill=1.0, base=0, pattern=[[-1, P]], channel_multiplier=1))


def norm(k, gain, out, shift=None, plain=None):
    nc = k.nc
    with ExitStack() as tmp:
        sq = k.sbuf("norm_squares", [P, KD, T], ctx=tmp)
        scaled = sq if plain is None else plain
        with nc.Block() as block:
            @block.scalar
            def _(act):
                for t in range(KD):
                    act.activation(sq[:, t], k.h[:, t], ACT.Square).then_inc(k.squares_ready.sem, 1)
                act.wait_ge(k.mean_ready.sem, k.mean_ready.at(1))
                act.activation(k.rs[:], k.rs[:], ACT.Sqrt).then_inc(k.root_ready.sem, 1)
                if plain is None:
                    for t in range(KD):
                        act.wait_ge(k.scaled_ready.sem, k.scaled_ready.at(t + 1))
                        act.activation(out.high[:, t], sq[:, t], ACT.Copy).then_inc(k.rounded_ready.sem, 1)

            @block.tensor
            def _(pe):
                for t in range(KD):
                    pe.wait_ge(k.squares_ready.sem, k.squares_ready.at(t + 1))
                    mm = pe.matmul(k.ps[:, 0], k.ones[:], sq[:, t], start=t == 0, stop=t == KD - 1)
                mm.then_inc(k.sumsq_ready.sem, 1)

            @block.vector
            def _(dve):
                dve.wait_ge(k.sumsq_ready.sem, k.sumsq_ready.at(1))
                dve.tensor_scalar(k.rs[:], k.ps[:, 0], 1.0 / D, EPS, ALU.mult, ALU.add).then_inc(k.mean_ready.sem, 1)
                dve.wait_ge(k.root_ready.sem, k.root_ready.at(1))
                k.dve_steps.then(dve, dve.reciprocal(k.rs[:], k.rs[:]))

                def rest(t):
                    dve.wait_ge(k.rounded_ready.sem, k.rounded_ready.at(t + 1))
                    dve.tensor_tensor(out.low[:, t], sq[:, t], out.high[:, t].bitcast(F32), ALU.subtract)

                for t in range(KD):
                    ins = dve.scalar_tensor_tensor(scaled[:, t], k.h[:, t], gain[:, t:t + 1], k.rs[:],
                                                   ALU.mult, ALU.mult)
                    if shift is not None:
                        k.dve_steps.then(dve, ins)
                        ins = dve.tensor_scalar(scaled[:, t], scaled[:, t], shift[:, t:t + 1], None, ALU.add)
                    ins.then_inc(k.scaled_ready.sem, 1)
                    if plain is None and t >= 1:
                        rest(t - 1)
                if plain is None:
                    rest(KD - 1)
    k.squares_ready.passed(KD)
    k.scaled_ready.passed(KD)
    if plain is None:
        k.rounded_ready.passed(KD)
    for s in (k.sumsq_ready, k.mean_ready, k.root_ready):
        s.passed(1)


def residual(k, weights, kin, moving, scale):
    stream = plain_stream(k, weights, KD, 4, kin, moving)
    per = -(-kin // KD)
    with k.nc.Block() as block:
        @block.sync
        def _(sp):
            stream.load(sp)

        @block.gpsimd
        def _(pool):
            stream.split_low(pool)

        @block.scalar
        def _(act):
            stream.scalar(act)

        @block.tensor
        def _(pe):
            stream.multiply(pe)

        @block.vector
        def _(dve):
            with dve.Fori(0, stream.iters) as i:
                for t in range(4):
                    stream.wait_products(dve, i, t * per + per - 1)
                    by = scale if isinstance(scale, float) else scale[:, bass.ds(i * 4 + t, 1)]
                    dve.scalar_tensor_tensor(one(k.h, i * 4 + t), k.ps[:, t], by, one(k.h, i * 4 + t),
                                             ALU.mult, ALU.add).then_inc(k.emptied[t].sem, 1)
    stream.finish()


def ffn(k, name, gain, sig):
    nc = k.nc
    norm(k, gain, k.u)
    with ExitStack() as ctx:
        hid = Split(k, ctx, f"{name}_hid", KF)
        gated = k.sbuf(f"{name}_gated", [P, 2, T], ctx=ctx)
        product = k.sbuf(f"{name}_product", [P, 2, T], ctx=ctx)
        gated_ready, product_ready, high_ready, low_ready = sig
        stream = plain_stream(k, k.dram[f"{name}_gu"], 2 * KF, 4, KD, k.u)
        with nc.Block() as block:
            @block.sync
            def _(sp):
                stream.load(sp)

            @block.gpsimd
            def _(pool):
                stream.split_low(pool)

            @block.tensor
            def _(pe):
                stream.multiply(pe)

            @block.scalar
            def _(act):
                def epilogue(i, j):
                    if j % 2 == 0:
                        t = j // 2
                        stream.wait_products(act, i, j)
                        act.wait_ge(product_ready[t].sem, i + product_ready[t].at(0))
                        act.activation(gated[:, t], k.ps[:, j], ACT.Silu).then_inc(gated_ready[t].sem, 1)

                def after(i, j):
                    if j % 2 == 1:
                        t = j // 2
                        act.wait_ge(product_ready[t].sem, i + product_ready[t].at(1))
                        act.activation(one(hid.high, i * 2 + t), product[:, t], ACT.Copy)\
                           .then_inc(high_ready[t].sem, 1)

                stream.scalar(act, epilogue, after)

            @block.vector
            def _(dve):
                with dve.Fori(0, stream.iters) as i:
                    for t in range(2):
                        stream.wait_products(dve, i, 2 * t + 1)
                        dve.wait_ge(gated_ready[t].sem, i + gated_ready[t].at(1))
                        dve.wait_ge(low_ready[t].sem, i + low_ready[t].at(0))
                        dve.tensor_tensor(product[:, t], gated[:, t], k.ps[:, 2 * t + 1], ALU.mult)\
                           .then_inc(product_ready[t].sem, 1)
                        dve.wait_ge(product_ready[t].sem, i + product_ready[t].at(1))
                        dve.sem_inc(k.emptied[2 * t].sem, 1)
                        dve.sem_inc(k.emptied[2 * t + 1].sem, 1)
                        dve.wait_ge(high_ready[t].sem, i + high_ready[t].at(1))
                        dve.tensor_tensor(one(hid.low, i * 2 + t), product[:, t], one(hid.high, i * 2 + t).bitcast(F32),
                                          ALU.subtract).then_inc(low_ready[t].sem, 1)
        stream.finish()
        for t in range(2):
            for s in (gated_ready, product_ready, high_ready, low_ready):
                s[t].passed(stream.iters)
        residual(k, k.dram[f"{name}_down"], KF, hid, 0.5)


def reduce_angle(k, dve, angle, turns, sine, cosine):
    magic = 1.5 * 2.0 ** 23
    c1 = 6.28125
    c2 = float(np.float32(TWO_PI - c1))
    c3 = float(np.float32(TWO_PI - c1 - c2))
    edge = 3.1415925
    step = lambda ins: k.dve_steps.then(dve, ins)
    step(dve.tensor_scalar(turns, angle, 1.0 / TWO_PI, None, ALU.mult))
    step(dve.tensor_scalar(turns, turns, magic, None, ALU.add))
    step(dve.tensor_scalar(turns, turns, magic, None, ALU.subtract))
    step(dve.scalar_tensor_tensor(sine, turns, -c1, angle, ALU.mult, ALU.add))
    step(dve.scalar_tensor_tensor(sine, turns, -c2, sine, ALU.mult, ALU.add))
    step(dve.scalar_tensor_tensor(sine, turns, -c3, sine, ALU.mult, ALU.add))
    step(dve.tensor_scalar(cosine, sine, np.pi / 2, None, ALU.add))
    step(dve.tensor_scalar(turns, cosine, edge, None, ALU.is_gt))
    step(dve.scalar_tensor_tensor(cosine, turns, -TWO_PI, cosine, ALU.mult, ALU.add))
    step(dve.tensor_scalar(cosine, cosine, edge, -edge, ALU.min, ALU.max))
    step(dve.tensor_scalar(sine, sine, edge, -edge, ALU.min, ALU.max))


def copy_tiles(k, weights, tiles, dst, moving, sigmoid=False):
    stream = plain_stream(k, weights, tiles, 4, KD, moving)
    with k.nc.Block() as block:
        @block.sync
        def _(sp):
            stream.load(sp)

        @block.gpsimd
        def _(pool):
            stream.split_low(pool)

        @block.tensor
        def _(pe):
            stream.multiply(pe)

        if sigmoid:
            @block.scalar
            def _(act):
                def epilogue(i, j):
                    stream.wait_products(act, i, j)
                    act.activation(one(dst, i * 4 + j), k.ps[:, j], ACT.Sigmoid).then_inc(k.emptied[j].sem, 1)

                stream.scalar(act, epilogue)
        else:
            @block.scalar
            def _(act):
                stream.scalar(act)

            @block.vector
            def _(dve):
                with dve.Fori(0, stream.iters) as i:
                    for t in range(4):
                        stream.wait_products(dve, i, t)
                        dve.tensor_copy(one(dst, i * 4 + t), k.ps[:, t]).then_inc(k.emptied[t].sem, 1)
    stream.finish()


def rope_tables(k, c, ctx):
    nc = k.nc
    with ExitStack() as tmp:
        raw = k.sbuf("pos_raw", [P, T], I32, tmp)
        turns = k.sbuf("turns", [P, T], ctx=tmp)
        posf = k.sbuf("posf", [P, T], ctx=tmp)
        loads = Signal(tmp, nc, "pos_loaded")
        reduced = Signal(tmp, nc, "angles_reduced")
        with nc.Block() as block:
            @block.sync
            def _(sp):
                sp.dma_start(raw[:], k.dram["positions"].to_broadcast((P, T))).then_inc(loads.sem, 16)

            @block.vector
            def _(dve):
                dve.wait_ge(loads.sem, 16)
                k.dve_steps.then(dve, dve.tensor_copy(posf[:], raw[:]))
                k.dve_steps.then(dve, dve.tensor_scalar(posf[:], posf[:], k.vec("freq"), None, ALU.mult))
                reduce_angle(k, dve, posf[:], turns[:], c.sin[:], c.cos[:])
                dve.sem_inc(reduced.sem, 1)

            @block.scalar
            def _(act):
                act.wait_ge(reduced.sem, 1)
                act.activation(c.sin[:], c.sin[:], ACT.Sin)
                act.activation(c.cos[:], c.cos[:], ACT.Sin)

            @block.gpsimd
            def _(pool):
                step = lambda ins: k.pool_steps.then(pool, ins)
                step(pool.memset(c.rot[:], 0.0))
                for b, fill in ((0, -1.0), (1, 1.0)):
                    view = c.rot[:].rearrange("p (a b c) -> p b a c", a=2, b=2)[:, b]
                    step(pool.affine_select(out=view, in_=view, compare_op=ALU.not_equal, fill=fill,
                                            base=-32 if b == 0 else 0, pattern=[[-64, 2], [-1, 32]],
                                            channel_multiplier=1))
                step(pool.memset(c.causal[:], 0.0))
                step(pool.memset(c.before[:], 0.0))
                step(pool.memset(c.seen[:], 0.0))
                step(pool.memset(c.some[:], 1.0))
                pool.affine_select(out=c.causal[:], in_=c.causal[:], compare_op=ALU.is_ge, fill=NEG, base=0,
                                   pattern=[[-1, P]], channel_multiplier=1)
                pool.affine_select(out=c.before[:], in_=c.before[:], compare_op=ALU.is_ge, fill=NEG, base=-1,
                                   pattern=[[1, P]], channel_multiplier=-1)
                pool.affine_select(out=c.seen[:], in_=c.seen[:], compare_op=ALU.is_ge, fill=NEG, base=-31,
                                   pattern=[[P, QT], [-16, CMP]], channel_multiplier=1)
                pool.affine_select(out=c.some[:], in_=c.some[:], compare_op=ALU.is_ge, fill=0.0, base=-31,
                                   pattern=[[P, QT]], channel_multiplier=1)


def rope(k, c, proj):
    nc = k.nc
    with ExitStack() as tmp:
        part = k.sbuf("rope_part", [P, 2, T], ctx=tmp)
        turned = Signal(tmp, nc, "halves_turned")
        roped = Signal(tmp, nc, "tile_roped")
        with nc.Block() as block:
            @block.tensor
            def _(pe):
                for t in range(ROPED):
                    if t >= 2:
                        pe.wait_ge(roped.sem, t - 1)
                    pe.matmul(k.ps[:, t % 2], c.rot[:], proj[:, t], start=True, stop=True).then_inc(turned.sem, 1)

            @block.vector
            def _(dve):
                for t in range(ROPED):
                    dve.wait_ge(turned.sem, t + 1)
                    dve.tensor_tensor(part[:, 0], k.ps[:, t % 2], c.sin[:], ALU.mult)
                    k.dve_steps.then(dve, dve.tensor_tensor(part[:, 1], proj[:, t], c.cos[:], ALU.mult))
                    dve.tensor_tensor(proj[:, t], part[:, 0], part[:, 1], ALU.add).then_inc(roped.sem, 1)
                    dve.wait_ge(roped.sem, t + 1)


def compress(k, c, proj):
    nc = k.nc
    with ExitStack() as tmp:
        w1 = k.sbuf("cmp_w1", [P, 32, 256], ctx=tmp)
        w2 = k.sbuf("cmp_w2", [P, 2, 192], ctx=tmp)
        pe_k = k.sbuf("cmp_pe", [P, 32], ctx=tmp)
        blocks = k.sbuf("cmp_blocks", [P, 32, 2, CMP], ctx=tmp)
        hid = k.sbuf("cmp_hid", [P, 2, 2, 2 * CMP], ctx=tmp)
        part = k.sbuf("cmp_part", [P, 2, CMP], ctx=tmp)
        loads = Signal(tmp, nc, "cmp_loaded")
        made = Signal(tmp, nc, "cmp_blocks_made")
        first = Signal(tmp, nc, "cmp_first_done")
        act_done = Signal(tmp, nc, "cmp_hid_ready")
        second = Signal(tmp, nc, "cmp_second_done")
        copied = Signal(tmp, nc, "cmp_keys_copied")
        turned = Signal(tmp, nc, "cmp_keys_turned")
        with nc.Block() as block:
            @block.sync
            def _(sp):
                sp.dma_start(pe_k[:], k.dram["cmp_pe"]).then_inc(loads.sem, 16)
                sp.dma_start(w2[:], k.dram["cmp_w2"]).then_inc(loads.sem, 16)
                sp.dma_start(w1[:], k.dram["cmp_w1"]).then_inc(loads.sem, 16)

            @block.tensor
            def _(pe):
                pe.wait_ge(loads.sem, 48)
                pe.wait_ge(made.sem, 4)
                for kv in range(2):
                    rows = slice(HD * kv, HD * (kv + 1))
                    for t in range(2):
                        for l in range(32):
                            mm = pe.matmul(k.ps[:, 2 * kv + t, 0:2 * CMP], w1[rows, l, t * P:(t + 1) * P],
                                           blocks[rows, l].rearrange("p g c -> p (g c)"),
                                           start=l == 0, stop=l == 31)
                        mm.then_inc(first.sem, 1)
                pe.wait_ge(act_done.sem, 4)
                for t in range(2):
                    mm = pe.matmul(k.ps[:, 4, 0:2 * CMP], w2[:, t, 0:P], hid[:, 0, t], start=t == 0, stop=t == 1)
                mm.then_inc(second.sem, 1)
                for g in range(2):
                    for t in range(2):
                        mm = pe.matmul(k.ps[0:CMP, 5, g * HD:(g + 1) * HD], hid[:, 1, t, g * CMP:(g + 1) * CMP],
                                       w2[:, t, P:P + HD], start=t == 0, stop=t == 1)
                mm.then_inc(second.sem, 1)
                pe.wait_ge(copied.sem, 2)
                pe.matmul(k.ps[:, 6, 0:CMP], c.rot[:], c.kcmp[:], start=True, stop=True).then_inc(turned.sem, 1)

            @block.scalar
            def _(act):
                for n in range(4):
                    act.wait_ge(first.sem, n + 1)
                    act.activation(hid[:, n // 2, n % 2], k.ps[:, n, 0:2 * CMP], ACT.Gelu_apprx_tanh)\
                       .then_inc(act_done.sem, 1)

            @block.vector
            def _(dve):
                dve.wait_ge(loads.sem, 48)
                for g in range(2):
                    strides = proj[:, KCA + g].rearrange("p (c l) -> p l c", l=16)
                    for half in range(2):
                        pos = pe_k[:, half * 16:(half + 1) * 16].unsqueeze(2).to_broadcast((P, 16, CMP))
                        dve.tensor_tensor(blocks[:, half * 16:(half + 1) * 16, g], strides[:, :, half:half + CMP],
                                          pos, ALU.add).then_inc(made.sem, 1)
                dve.wait_ge(second.sem, 2)
                for g in range(2):
                    rows = slice(HD * g, HD * (g + 1))
                    dve.tensor_copy(c.kcmp[rows], k.ps[rows, 4, g * CMP:(g + 1) * CMP]).then_inc(copied.sem, 1)
                dve.tensor_copy(c.vcmp[0:CMP], k.ps[0:CMP, 5, 0:P])
                dve.wait_ge(turned.sem, 1)
                last = slice(31, T, 16)
                dve.tensor_tensor(part[:, 0], k.ps[:, 6, 0:CMP], c.sin[:, last], ALU.mult)
                k.dve_steps.then(dve, dve.tensor_tensor(part[:, 1], c.kcmp[:], c.cos[:, last], ALU.mult))
                dve.tensor_tensor(c.kcmp[:], part[:, 0], part[:, 1], ALU.add)


def token_major(k, name, sources, dst):
    nc = k.nc
    n_banks = -(-len(sources) // 4)
    with ExitStack() as tmp:
        turned = Signal(tmp, nc, f"{name}_turned")
        copied = Signal(tmp, nc, f"{name}_copied")
        with nc.Block() as block:
            @block.tensor
            def _(pe):
                for b in range(n_banks):
                    if b >= BANKS:
                        pe.wait_ge(copied.sem, b - BANKS + 1)
                    for n in range(4 * b, min(4 * b + 4, len(sources))):
                        tr = pe.transpose(k.ps[:, b % BANKS, (n % 4) * P:(n % 4 + 1) * P], sources[n], k.ident[:])
                    tr.then_inc(turned.sem, 1)

            @block.vector
            def _(dve):
                for b in range(n_banks):
                    dve.wait_ge(turned.sem, b + 1)
                    for n in range(4 * b, min(4 * b + 4, len(sources))):
                        ins = dve.tensor_copy(dst[n], k.ps[:, b % BANKS, (n % 4) * P:(n % 4 + 1) * P])
                    ins.then_inc(copied.sem, 1)


def nsa(k, c, proj, vtok, o):
    nc = k.nc
    units = [(qt, j, g) for qt in range(QT) for j in range(4) for g in range(2)]
    with ExitStack() as tmp:
        probs = k.sbuf("nsa_probs", [P, 2, 3, T], ctx=tmp)
        keyed = k.sbuf("nsa_keyed", [P, 2, 9, P], ctx=tmp)
        peak = k.sbuf("nsa_peak", [P, 2, 3], ctx=tmp)
        sums = k.sbuf("nsa_sums", [P, 2, 3], ctx=tmp)
        share = k.sbuf("nsa_share", [P, 3], ctx=tmp)
        sigm = k.sbuf("nsa_gates", [P, QT, 24], ctx=tmp)
        gates_ready = Signal(tmp, nc, "nsa_gates_ready")
        scored = Signal(tmp, nc, "nsa_scored")
        peaked = Signal(tmp, nc, "nsa_peaked")
        exped = Signal(tmp, nc, "nsa_exped")
        turned = Signal(tmp, nc, "nsa_turned")
        copied_a = Signal(tmp, nc, "nsa_copied_by_act")
        copied_v = Signal(tmp, nc, "nsa_copied_by_dve")
        mixed = Signal(tmp, nc, "nsa_mixed")
        summed = Signal(tmp, nc, "nsa_summed")
        cmp_scores = lambda b: k.ps[:, 6 + b, 3 * HD:3 * HD + CMP]
        cmp_turned = lambda b: k.ps[0:CMP, 6 + b, 2 * P:3 * P]
        with nc.Block() as block:
            @block.tensor
            def _(pe):
                def score(n):
                    qt, j, g = units[n]
                    rows, keys = slice(HD * g, HD * (g + 1)), (qt + 1) * P
                    q = proj[rows, Q0 + j, qt * P:(qt + 1) * P]
                    b = n % 2
                    if n >= 2:
                        pe.wait_ge(exped.sem, n - 1)
                        pe.wait_ge(summed.sem, n - 1)
                    pe.matmul(k.ps[:, 2 * b, 0:keys], q, proj[rows, KSL, 0:keys], start=True, stop=True)
                    pe.matmul(k.ps[:, 2 * b + 1, 0:keys], q, proj[rows, KWN, 0:keys], start=True, stop=True)
                    pe.matmul(cmp_scores(b), q, c.kcmp[rows], start=True, stop=True).then_inc(scored.sem, 1)

                score(0)
                for n, (qt, j, g) in enumerate(units):
                    b = n % 2
                    if n + 1 < len(units):
                        score(n + 1)
                    pe.wait_ge(exped.sem, n + 1)
                    if n >= 1:
                        pe.wait_ge(copied_a.sem, n)
                        pe.wait_ge(copied_v.sem, n)
                    for kind in range(2):
                        for kb in range(qt + 1):
                            pe.transpose(k.ps[:, 4 + kind, kb * P:(kb + 1) * P],
                                         probs[:, b, kind, kb * P:(kb + 1) * P], k.ident[:])
                    pe.transpose(cmp_turned(b), probs[:, b, 2, 0:CMP], k.ident[:]).then_inc(turned.sem, 1)
                    pe.wait_ge(copied_a.sem, n + 1)
                    pe.wait_ge(copied_v.sem, n + 1)
                    for kind in range(2):
                        for kb in range(qt + 1):
                            pe.matmul(k.ps[:, 6 + b, kind * HD:(kind + 1) * HD], keyed[:, b, 4 * kind + kb],
                                      vtok[:, kind, kb, HD * g:HD * (g + 1)], start=kb == 0, stop=kb == qt)
                    pe.matmul(k.ps[:, 6 + b, 2 * HD:3 * HD], keyed[0:CMP, b, 8], c.vcmp[0:CMP, HD * g:HD * (g + 1)],
                              start=True, stop=True).then_inc(mixed.sem, 1)

            @block.scalar
            def _(act):
                act.activation(sigm[:], vtok[:, 2, :, HD:HD + 24], ACT.Sigmoid).then_inc(gates_ready.sem, 1)
                def weigh(n):
                    b, keys = n % 2, (units[n][0] + 1) * P
                    act.wait_ge(peaked.sem, n + 1)
                    if n >= 2:
                        act.wait_ge(turned.sem, n - 1)
                        act.wait_ge(summed.sem, n - 1)
                    for kind, scores in ((0, k.ps[:, 2 * b, 0:keys]), (1, k.ps[:, 2 * b + 1, 0:keys]), (2, cmp_scores(b))):
                        ins = act.activation(probs[:, b, kind, 0:scores.shape[1]], scores, ACT.Exp,
                                             bias=peak[:, b, kind:kind + 1], scale=SCALE,
                                             accum_out=sums[:, b, kind:kind + 1])
                    ins.then_inc(exped.sem, 1)

                weigh(0)
                for n, (qt, j, g) in enumerate(units):
                    b, keys = n % 2, (qt + 1) * P
                    if n + 1 < len(units):
                        weigh(n + 1)
                    act.wait_ge(turned.sem, n + 1)
                    if n >= 2:
                        act.wait_ge(mixed.sem, n - 1)
                    act.activation(keyed[:, b, 0:qt + 1], k.ps[:, 4, 0:keys].rearrange("p (a n) -> p a n", n=P),
                                   ACT.Copy)
                    act.activation(keyed[0:CMP, b, 8], cmp_turned(b), ACT.Copy).then_inc(copied_a.sem, 1)

            @block.vector
            def _(dve):
                def peaks(n):
                    qt, b = units[n][0], n % 2
                    own, keys = slice(qt * P, (qt + 1) * P), (qt + 1) * P
                    dve.wait_ge(scored.sem, n + 1)
                    both = k.ps[:, 2 * b:2 * b + 2, own]
                    dve.tensor_tensor(both, both, c.causal[:].unsqueeze(1).to_broadcast((P, 2, P)), ALU.add)
                    k.dve_steps.then(dve, dve.tensor_tensor(cmp_scores(b), cmp_scores(b), c.seen[:, qt], ALU.add))
                    if n >= 2:
                        dve.wait_ge(exped.sem, n - 1)
                    dve.tensor_reduce(peak[:, b, 0:2], k.ps[:, 2 * b:2 * b + 2, 0:keys], AX.X, ALU.max)
                    k.dve_steps.then(dve, dve.tensor_reduce(peak[:, b, 2:3], cmp_scores(b), AX.X, ALU.max))
                    dve.tensor_scalar(peak[:, b], peak[:, b], -SCALE, None, ALU.mult).then_inc(peaked.sem, 1)

                peaks(0)
                dve.wait_ge(gates_ready.sem, 1)
                for n, (qt, j, g) in enumerate(units):
                    b, head = n % 2, 4 * g + j
                    if n + 1 < len(units):
                        peaks(n + 1)
                    dve.wait_ge(turned.sem, n + 1)
                    if n >= 2:
                        dve.wait_ge(mixed.sem, n - 1)
                    dve.tensor_copy(keyed[:, b, 4:5 + qt], k.ps[:, 5, 0:(qt + 1) * P].rearrange("p (a n) -> p a n", n=P))\
                       .then_inc(copied_v.sem, 1)
                    k.dve_steps.then(dve, dve.reciprocal(share[:], sums[:, b]))
                    gate = sigm[:, qt].rearrange("p (b h) -> p b h", b=3)
                    k.dve_steps.then(dve, dve.tensor_tensor(share[:, 0:2], share[:, 0:2], gate[:, 1:3, head], ALU.mult))
                    k.dve_steps.then(dve, dve.scalar_tensor_tensor(share[:, 2:3], share[:, 2:3], c.some[:, qt:qt + 1],
                                                                   gate[:, 0:1, head], ALU.mult, ALU.mult))
                    dve.wait_ge(mixed.sem, n + 1)
                    mine = o[:, qt, HD * head:HD * (head + 1)]
                    k.dve_steps.then(dve, dve.tensor_scalar(mine, k.ps[:, 6 + b, 0:HD], share[:, 0:1], None, ALU.mult))
                    k.dve_steps.then(dve, dve.scalar_tensor_tensor(mine, k.ps[:, 6 + b, HD:2 * HD], share[:, 1:2], mine,
                                                                   ALU.mult, ALU.add))
                    dve.scalar_tensor_tensor(mine, k.ps[:, 6 + b, 2 * HD:3 * HD], share[:, 2:3], mine,
                                             ALU.mult, ALU.add).then_inc(summed.sem, 1)
                    dve.wait_ge(summed.sem, n + 1)


def swa(k, c, proj, vtok, o):
    nc = k.nc
    units = [(qt, j, g) for qt in range(QT) for j in range(4) for g in range(2)]
    with ExitStack() as tmp:
        probs = k.sbuf("swa_probs", [P, 2, 2 * P], ctx=tmp)
        keyed = k.sbuf("swa_keyed", [P, 2, 2, P], ctx=tmp)
        peak = k.sbuf("swa_peak", [P, 2], ctx=tmp)
        sums = k.sbuf("swa_sums", [P, 2, 2], ctx=tmp)
        share = k.sbuf("swa_share", [P, 1], ctx=tmp)
        scored = Signal(tmp, nc, "swa_scored")
        peaked = Signal(tmp, nc, "swa_peaked")
        exped = Signal(tmp, nc, "swa_exped")
        turned = Signal(tmp, nc, "swa_turned")
        copied = Signal(tmp, nc, "swa_copied")
        mixed = Signal(tmp, nc, "swa_mixed")
        summed = Signal(tmp, nc, "swa_summed")
        with nc.Block() as block:
            @block.tensor
            def _(pe):
                def score(n):
                    qt, j, g = units[n]
                    rows, lo = slice(HD * g, HD * (g + 1)), max(qt - 1, 0) * P
                    if n >= 2:
                        pe.wait_ge(exped.sem, n - 1)
                    pe.matmul(k.ps[:, n % 2, 0:(qt + 1) * P - lo], proj[rows, SQ0 + j, qt * P:(qt + 1) * P],
                              proj[rows, SK, lo:(qt + 1) * P], start=True, stop=True).then_inc(scored.sem, 1)

                score(0)
                for n, (qt, j, g) in enumerate(units):
                    b, blocks = n % 2, min(qt, 1) + 1
                    if n + 1 < len(units):
                        score(n + 1)
                    pe.wait_ge(exped.sem, n + 1)
                    if n >= 2:
                        pe.wait_ge(copied.sem, n - 1)
                    for m in range(blocks):
                        tr = pe.transpose(k.ps[:, 2 + b, m * P:(m + 1) * P], probs[:, b, m * P:(m + 1) * P], k.ident[:])
                    tr.then_inc(turned.sem, 1)
                    pe.wait_ge(copied.sem, n + 1)
                    if n >= 2:
                        pe.wait_ge(summed.sem, n - 1)
                    for m in range(blocks):
                        mm = pe.matmul(k.ps[:, 4 + b, 0:HD], keyed[:, b, m], vtok[:, 2, qt - blocks + 1 + m, 0:HD],
                                       start=m == 0, stop=m == blocks - 1)
                    mm.then_inc(mixed.sem, 1)

            @block.scalar
            def _(act):
                for n, (qt, j, g) in enumerate(units):
                    b, head, width = n % 2, 4 * g + j, (min(qt, 1) + 1) * P
                    act.wait_ge(peaked.sem, n + 1)
                    if n >= 2:
                        act.wait_ge(turned.sem, n - 1)
                        act.wait_ge(summed.sem, n - 1)
                    act.activation(probs[:, b, 0:width], k.ps[:, b, 0:width], ACT.Exp, bias=peak[:, b:b + 1],
                                   scale=SCALE, accum_out=sums[:, b, 0:1])
                    act.activation(sums[:, b, 1:2], k.vec("sinks")[:, head:head + 1], ACT.Exp,
                                   bias=peak[:, b:b + 1]).then_inc(exped.sem, 1)
                    act.wait_ge(turned.sem, n + 1)
                    if n >= 2:
                        act.wait_ge(mixed.sem, n - 1)
                    act.activation(keyed[:, b, 0:width // P], k.ps[:, 2 + b, 0:width].rearrange("p (a n) -> p a n", n=P),
                                   ACT.Copy).then_inc(copied.sem, 1)

            @block.vector
            def _(dve):
                def peaks(n):
                    qt, j, g = units[n]
                    b, head, blocks = n % 2, 4 * g + j, min(qt, 1) + 1
                    dve.wait_ge(scored.sem, n + 1)
                    if blocks == 2:
                        dve.tensor_tensor(k.ps[:, b, 0:P], k.ps[:, b, 0:P], c.before[:], ALU.add)
                    own = k.ps[:, b, (blocks - 1) * P:blocks * P]
                    k.dve_steps.then(dve, dve.tensor_tensor(own, own, c.causal[:], ALU.add))
                    if n >= 2:
                        dve.wait_ge(exped.sem, n - 1)
                    k.dve_steps.then(dve, dve.tensor_reduce(peak[:, b:b + 1], k.ps[:, b, 0:blocks * P], AX.X, ALU.max))
                    k.dve_steps.then(dve, dve.scalar_tensor_tensor(peak[:, b:b + 1], peak[:, b:b + 1], SCALE,
                                                                   k.vec("sinks")[:, head:head + 1], ALU.mult, ALU.max))
                    dve.tensor_scalar(peak[:, b:b + 1], peak[:, b:b + 1], -1.0, None, ALU.mult)\
                       .then_inc(peaked.sem, 1)

                peaks(0)
                for n, (qt, j, g) in enumerate(units):
                    b, head = n % 2, 4 * g + j
                    if n + 1 < len(units):
                        peaks(n + 1)
                    dve.wait_ge(mixed.sem, n + 1)
                    k.dve_steps.then(dve, dve.tensor_tensor(share[:], sums[:, b, 0:1], sums[:, b, 1:2], ALU.add))
                    k.dve_steps.then(dve, dve.reciprocal(share[:], share[:]))
                    dve.tensor_scalar(o[:, qt, HD * head:HD * (head + 1)], k.ps[:, 4 + b, 0:HD], share[:], None,
                                      ALU.mult).then_inc(summed.sem, 1)
                    dve.wait_ge(summed.sem, n + 1)


def branches(k, weights, gates, o, merged):
    nc = k.nc
    chunks = []
    for t in range(4):
        groups = [(t, k.ps[:, t], [(x, o.high[:, x], o.low[:, x]) for x in range(4)], True, True, None),
                  (4 + t, k.ps[:, 4 + t], [(x, o.high[:, x], o.low[:, x]) for x in range(4, 8)], True, True, None)]
        chunks.append((chunk_of(weights, 4, t), groups))
    stream = Stream(k, KD // 4, chunks)
    with ExitStack() as tmp:
        part = k.sbuf("branch_part", [P, 2, T], ctx=tmp)
        added = Signal(tmp, nc, "branch_added")
        with nc.Block() as block:
            @block.sync
            def _(sp):
                stream.load(sp)

            @block.gpsimd
            def _(pool):
                stream.split_low(pool)

            @block.tensor
            def _(pe):
                stream.multiply(pe)

            @block.scalar
            def _(act):
                stream.scalar(act)

            @block.vector
            def _(dve):
                with dve.Fori(0, stream.iters) as i:
                    for t in range(4):
                        stream.wait_products(dve, i, t)
                        dve.tensor_tensor(part[:, 0], one(gates, i * 4 + t), k.ps[:, t], ALU.mult)\
                           .then_inc(k.emptied[t].sem, 1)
                        dve.tensor_tensor(part[:, 1], one(gates, i * 4 + (KD + t)), k.ps[:, 4 + t], ALU.mult)\
                           .then_inc(k.emptied[4 + t].sem, 1)
                        dve.wait_ge(k.emptied[t].sem, i + k.emptied[t].at(1))
                        dve.wait_ge(k.emptied[4 + t].sem, i + k.emptied[4 + t].at(1))
                        dve.tensor_tensor(one(merged, i * 4 + t), part[:, 0], part[:, 1], ALU.add)\
                           .then_inc(added.sem, 1)
                        dve.wait_ge(added.sem, i * 4 + (t + 1))
        stream.finish()


class Mixer1:
    pass


def mixer1(k):
    nc = k.nc
    norm(k, k.vec("norm_mix"), k.u)
    with ExitStack() as ctx:
        c = Mixer1()
        o_t = k.sbuf("o_t", [P, KD, T], ctx=ctx)
        with ExitStack() as inner:
            proj = k.sbuf("proj", [P, PROJ, T], ctx=inner)
            c.cos = k.sbuf("cos", [P, T], ctx=inner)
            c.sin = k.sbuf("sin", [P, T], ctx=inner)
            c.rot = k.sbuf("rot", [P, P], ctx=inner)
            c.causal = k.sbuf("causal", [P, P], ctx=inner)
            c.before = k.sbuf("before", [P, P], ctx=inner)
            c.seen = k.sbuf("seen", [P, QT, CMP], ctx=inner)
            c.some = k.sbuf("some", [P, QT], ctx=inner)
            c.kcmp = k.sbuf("kcmp", [P, CMP], ctx=inner)
            c.vcmp = k.sbuf("vcmp", [P, P], ctx=inner)
            copy_tiles(k, k.dram["w_in"], PROJ, proj, k.u)
            rope_tables(k, c, inner)
            rope(k, c, proj)
            compress(k, c, proj)
            vtok = k.sbuf("vtok", [P, 3, QT, P], ctx=inner)
            token_major(k, "values", [proj[:, t, b * P:(b + 1) * P] for t in (VSL, VWN, SVG) for b in range(QT)],
                        [vtok[:, n, b] for n in range(3) for b in range(QT)])
            with ExitStack() as deep:
                oa = k.sbuf("oa", [P, QT, 512], ctx=deep)
                ob = k.sbuf("ob", [P, QT, 512], ctx=deep)
                nsa(k, c, proj, vtok, oa)
                swa(k, c, proj, vtok, ob)
                token_major(k, "outputs",
                            [s[:, q, f * P:(f + 1) * P] for s in (oa, ob) for f in range(4) for q in range(QT)],
                            [d[:, f, q * P:(q + 1) * P] for d in (o_t[:, 0:4], o_t[:, 4:8]) for f in range(4) for q in range(QT)])
        gates = k.sbuf("branch_gates", [P, 2 * KD, T], ctx=ctx)
        copy_tiles(k, k.dram["w_in_gates"], 2 * KD, gates, k.u, sigmoid=True)
        split_tiles(k, "mixed_heads", o_t, k.u)
        branches(k, k.dram["w_branch"], gates, k.u, o_t)
        split_tiles(k, "merged", o_t, k.u)
        residual(k, k.dram["w_out"], KD, k.u, 1.0)


CHUNK = 16
NCH = T // CHUNK
HEADS2 = 4
LANES = HEADS2 * NCH
S5T = 16


def modulation(k):
    nc = k.nc
    with ExitStack() as tmp:
        cond = k.sbuf("cond", [P, KD], ctx=tmp)
        ready = Signal(tmp, nc, "cond_ready")
        read = [Signal(tmp, nc, f"ada_read{s}") for s in range(SLOTS)]
        added = [Signal(tmp, nc, f"ada_added{s}", 1) for s in range(SLOTS)]
        iters = 6 * KD // SLOTS
        with nc.Block() as block:
            @block.sync
            def _(sp):
                for s in range(SLOTS):
                    sp.dma_start(k.ring[:, s], k.dram["ada_w"][s]).then_inc(k.loaded[s].sem, 16)
                with sp.Fori(1, iters) as i:
                    for s in range(SLOTS):
                        src = k.dram["ada_w"][bass.ds(i * SLOTS + s, 1), :, :].rearrange("a p n -> p (a n)")
                        sp.wait_ge(read[s].sem, i)
                        sp.dma_start(k.ring[:, s], src).then_inc(k.loaded[s].sem, 16)

            @block.scalar
            def _(act):
                act.activation(cond[:], k.vec("c_2"), ACT.Silu).then_inc(ready.sem, 1)

            @block.tensor
            def _(pe):
                pe.wait_ge(ready.sem, 1)
                with pe.Fori(0, iters) as i:
                    for s in range(SLOTS):
                        pe.wait_ge(k.loaded[s].sem, i * 16 + k.loaded[s].at(16))
                        pe.wait_ge(added[s].sem, i + 1)
                        for x in range(KD):
                            mm = pe.matmul(k.ps[:, s, 0:1], k.ring[:, s, x * P:(x + 1) * P], cond[:, x:x + 1],
                                           start=x == 0, stop=x == KD - 1)
                        mm.then_inc(read[s].sem, 1)

            @block.vector
            def _(dve):
                for s in range(SLOTS):
                    dve.sem_inc(added[s].sem, 1)
                with dve.Fori(0, iters) as i:
                    for s in range(SLOTS):
                        dve.wait_ge(read[s].sem, i + 1)
                        dve.tensor_tensor(k.mod[:, bass.ds(i * SLOTS + s, 1)], k.ps[:, s, 0:1],
                                          k.vec("ada_b_2")[:, bass.ds(i * SLOTS + s, 1)], ALU.add)\
                           .then_inc(added[s].sem, 1)
        for s in range(SLOTS):
            k.loaded[s].passed(16 * iters)


def scaled_gain(k, name, scale, out):
    with k.nc.Block() as block:
        @block.vector
        def _(dve):
            dve.scalar_tensor_tensor(out, scale, 1.0, k.vec(name), ALU.add, ALU.mult)


def hgrn(k, proj, out):
    nc = k.nc
    Q, F, V, G = 0, 4, 8, 12
    lanes = lambda ap: ap.rearrange("p h (c j) -> p (h c) j", j=CHUNK)
    heads = lambda ap: ap.rearrange("p h (c j) -> p h c j", j=CHUNK)
    with ExitStack() as outer:
        f = k.sbuf("hg_f", [P, HEADS2, T], ctx=outer)
        key = k.sbuf("hg_key", [P, HEADS2, T], ctx=outer)
        start = k.sbuf("hg_start", [P, HEADS2, T], ctx=outer)
        q = proj[:, Q:Q + 4]
        with ExitStack() as tmp:
            lb = k.sbuf("hg_lb", [P, 3, HEADS2], ctx=tmp)
            lb_ready = Signal(tmp, nc, "hg_lb_ready")
            sig_ready = Signal(tmp, nc, "hg_sigmoid_ready")
            with nc.Block() as block:
                @block.scalar
                def _(act):
                    act.activation(q, q, ACT.Silu).then_inc(sig_ready.sem, 1)
                    act.activation(proj[:, G:G + 4], proj[:, G:G + 4], ACT.Silu).then_inc(sig_ready.sem, 1)
                    act.activation(f[:], proj[:, F:F + 4], ACT.Sigmoid).then_inc(sig_ready.sem, 1)
                    act.wait_ge(lb_ready.sem, 1)
                    act.activation(lb[:, 0:2], lb[:, 0:2], ACT.Exp).then_inc(sig_ready.sem, 1)

                @block.vector
                def _(dve):
                    step = lambda ins: k.dve_steps.then(dve, ins)
                    step(dve.tensor_tensor(lb[:, 2], k.vec("lb0"), k.vec("lb1"), ALU.max))
                    step(dve.tensor_tensor(lb[:, 0], k.vec("lb0"), lb[:, 2], ALU.subtract))
                    dve.tensor_tensor(lb[:, 1], k.vec("lb1"), lb[:, 2], ALU.subtract).then_inc(lb_ready.sem, 1)
                    dve.wait_ge(sig_ready.sem, 4)
                    step(dve.tensor_tensor(lb[:, 1], lb[:, 0], lb[:, 1], ALU.add))
                    step(dve.reciprocal(lb[:, 1], lb[:, 1]))
                    step(dve.tensor_tensor(lb[:, 0], lb[:, 0], lb[:, 1], ALU.mult))
                    step(dve.tensor_scalar(lb[:, 1], lb[:, 0], -1.0, 1.0, ALU.mult, ALU.add))
                    for h in range(HEADS2):
                        ins = dve.tensor_scalar(f[:, h], f[:, h], lb[:, 1, h:h + 1], lb[:, 0, h:h + 1],
                                                ALU.mult, ALU.add)
                    step(ins)
                    step(dve.tensor_scalar(key[:], f[:], -1.0, 1.0, ALU.mult, ALU.add))
                    step(dve.tensor_scalar(q, q, float(P) ** -0.5, None, ALU.mult))
                    sl, fl = lanes(start), lanes(f)
                    step(dve.tensor_copy(sl[:, :, 0:1], fl[:, :, 0:1]))
                    for j in range(1, CHUNK):
                        step(dve.tensor_tensor(sl[:, :, j:j + 1], sl[:, :, j - 1:j], fl[:, :, j:j + 1], ALU.mult))
        hgrn_within(k, lanes, heads, q, f, key, proj[:, V:V + 4], out)
        hgrn_across(k, lanes, q, f, key, start, proj[:, V:V + 4], out)
    hgrn_finish(k, proj[:, G:G + 4], out)


def hgrn_within(k, lanes, heads, q, f, key, v, out):
    nc = k.nc
    with ExitStack() as tmp:
        qf = k.sbuf("hg_qf", [P, LANES, CHUNK], ctx=tmp)
        qk = k.sbuf("hg_qk", [P, 2, LANES * CHUNK], ctx=tmp)
        sv = k.sbuf("hg_sv", [P, HEADS2 * NCH * CHUNK], ctx=tmp)
        decayed = Signal(tmp, nc, "hg_query_decayed")
        paired = Signal(tmp, nc, "hg_pairs_ready")
        scored = Signal(tmp, nc, "hg_lag_scored")
        with nc.Block() as block:
            @block.gpsimd
            def _(pool):
                fl = lanes(f)
                for lag in range(1, CHUNK):
                    if lag == 1:
                        ins = pool.tensor_tensor(qf[:, :, 1:], lanes(q)[:, :, 1:], fl[:, :, 1:], ALU.mult)
                    else:
                        pool.wait_ge(decayed.sem, lag - 1)
                        pool.wait_ge(paired.sem, lag)
                        ins = pool.tensor_tensor(qf[:, :, lag:], qf[:, :, lag:], fl[:, :, 1:CHUNK - lag + 1], ALU.mult)
                    ins.then_inc(decayed.sem, 1)

            @block.tensor
            def _(pe):
                for lag in range(CHUNK):
                    w = (CHUNK - lag) * NCH
                    pe.wait_ge(paired.sem, lag + 1)
                    for h in range(HEADS2):
                        mm = pe.matmul(k.ps[:, 4 * (lag % 2) + h, 0:w], k.ones[:],
                                       qk[:, lag % 2, h * w:(h + 1) * w], start=True, stop=True)
                    mm.then_inc(scored.sem, 1)

            @block.vector
            def _(dve):
                kl = lanes(key)

                def pairs(lag):
                    w = CHUNK - lag
                    dst = qk[:, lag % 2, 0:LANES * w].rearrange("p (l j) -> p l j", j=w)
                    if lag >= 1:
                        dve.wait_ge(decayed.sem, lag)
                    if lag >= 2:
                        dve.wait_ge(scored.sem, lag - 1)
                    source = lanes(q) if lag == 0 else qf[:, :, lag:]
                    dve.tensor_tensor(dst, source, kl[:, :, 0:w], ALU.mult).then_inc(paired.sem, 1)

                pairs(0)
                for lag in range(CHUNK):
                    w = CHUNK - lag
                    if lag + 1 < CHUNK:
                        pairs(lag + 1)
                    dve.wait_ge(scored.sem, lag + 1)
                    score = k.ps[:, 4 * (lag % 2):4 * (lag % 2) + 4, 0:NCH * w].rearrange("p h (c j) -> p h c j", j=w)
                    if lag == 0:
                        k.dve_steps.then(dve, dve.tensor_tensor(heads(out), score, heads(v), ALU.mult))
                        continue
                    part = sv[:, 0:HEADS2 * NCH * w].rearrange("p (h c j) -> p h c j", h=HEADS2, j=w)
                    k.dve_steps.then(dve, dve.tensor_tensor(part, score, heads(v)[:, :, :, 0:w], ALU.mult))
                    flat = sv[:, 0:LANES * w].rearrange("p (l j) -> p l j", j=w)
                    k.dve_steps.then(dve, dve.tensor_tensor(lanes(out)[:, :, lag:], lanes(out)[:, :, lag:], flat, ALU.add))


def hgrn_across(k, lanes, q, f, key, start, v, out):
    nc = k.nc
    per = T // (HEADS2 * CHUNK)
    with ExitStack() as tmp:
        rest = k.sbuf("hg_rest", [P, HEADS2, T], ctx=tmp)
        ktok = k.sbuf("hg_ktok", [CHUNK, 2, HEADS2 * P], ctx=tmp)
        vtok = k.sbuf("hg_vtok", [CHUNK, 2, HEADS2 * P], ctx=tmp)
        state = k.sbuf("hg_state", [P, 2, HEADS2, P], ctx=tmp)
        prepared = Signal(tmp, nc, "hg_prepared")
        turned = Signal(tmp, nc, "hg_turned")
        copied = Signal(tmp, nc, "hg_copied")
        multiplied = Signal(tmp, nc, "hg_outer_ready")
        stated = Signal(tmp, nc, "hg_state_ready")
        read = Signal(tmp, nc, "hg_state_read")
        gathered = Signal(tmp, nc, "hg_gathered")
        with nc.Block() as block:
            @block.tensor
            def _(pe):
                def turn(c):
                    if c >= 2:
                        pe.wait_ge(copied.sem, c - 1)
                    own = slice(c * CHUNK, (c + 1) * CHUNK)
                    for h in range(HEADS2):
                        pe.transpose(k.ps[0:CHUNK, c % 2, h * P:(h + 1) * P], key[:, h, own], k.ident[:])
                        tr = pe.transpose(k.ps[0:CHUNK, 2 + c % 2, h * P:(h + 1) * P], v[:, h, own], k.ident[:])
                    tr.then_inc(turned.sem, 1)

                def outer(c):
                    pe.wait_ge(copied.sem, c + 1)
                    if c >= 2:
                        pe.wait_ge(stated.sem, c - 1)
                    for h in range(HEADS2):
                        mm = pe.matmul(k.ps[:, 4 + c % 2, h * P:(h + 1) * P], ktok[:, c % 2, h * P:(h + 1) * P],
                                       vtok[:, c % 2, h * P:(h + 1) * P], start=True, stop=True)
                    mm.then_inc(multiplied.sem, 1)

                pe.wait_ge(prepared.sem, 1)
                turn(0)
                turn(1)
                outer(0)
                for c in range(NCH - 1):
                    if c + 2 < NCH - 1:
                        turn(c + 2)
                    if c + 1 < NCH - 1:
                        outer(c + 1)
                    n = c + 1
                    pe.wait_ge(stated.sem, n)
                    if n // per >= 2 and n % per == 0:
                        pe.wait_ge(gathered.sem, n // per - 1)
                    for h in range(HEADS2):
                        at = (h * per + n % per) * CHUNK
                        mm = pe.matmul(k.ps[:, 6 + (n // per) % 2, at:at + CHUNK], state[:, c % 2, h],
                                       q[:, h, n * CHUNK:(n + 1) * CHUNK], start=True, stop=True)
                    mm.then_inc(read.sem, 1)

            @block.scalar
            def _(act):
                for c in range(NCH - 1):
                    act.wait_ge(turned.sem, c + 1)
                    if c >= 2:
                        act.wait_ge(multiplied.sem, c - 1)
                    act.activation(ktok[:, c % 2], k.ps[0:CHUNK, c % 2], ACT.Copy)
                    act.activation(vtok[:, c % 2], k.ps[0:CHUNK, 2 + c % 2], ACT.Copy).then_inc(copied.sem, 1)

            @block.vector
            def _(dve):
                step = lambda ins: k.dve_steps.then(dve, ins)
                rl, fl = lanes(rest), lanes(f)
                step(dve.memset(rl[:, :, CHUNK - 1:], 1.0))
                for j in range(CHUNK - 2, -1, -1):
                    step(dve.tensor_tensor(rl[:, :, j:j + 1], rl[:, :, j + 1:j + 2], fl[:, :, j + 1:j + 2], ALU.mult))
                step(dve.tensor_tensor(key[:], key[:], rest[:], ALU.mult))
                dve.tensor_tensor(q, q, start[:], ALU.mult).then_inc(prepared.sem, 1)
                for c in range(NCH):
                    if c < NCH - 1:
                        dve.wait_ge(multiplied.sem, c + 1)
                        if c >= 2:
                            dve.wait_ge(read.sem, c - 1)
                        if c == 0:
                            ins = dve.tensor_copy(state[:, 0], k.ps[:, 4].rearrange("p (h n) -> p h n", h=HEADS2))
                        else:
                            for h in range(HEADS2):
                                last = (c + 1) * CHUNK - 1
                                ins = dve.scalar_tensor_tensor(state[:, c % 2, h], state[:, (c - 1) % 2, h],
                                                               start[:, h, last:last + 1],
                                                               k.ps[:, 4 + c % 2, h * P:(h + 1) * P], ALU.mult, ALU.add)
                        ins.then_inc(stated.sem, 1)
                        dve.wait_ge(stated.sem, c + 1)
                    if c % per == per - 1:
                        b = c // per
                        lo = 1 if b == 0 else 0
                        dve.wait_ge(read.sem, c)
                        mine = out[:, :, (b * per + lo) * CHUNK:(b + 1) * per * CHUNK]
                        got = k.ps[:, 6 + b % 2].rearrange("p (h n) -> p h n", h=HEADS2)[:, :, lo * CHUNK:]
                        dve.tensor_tensor(mine, mine, got, ALU.add).then_inc(gathered.sem, 1)


def hgrn_finish(k, gate, out):
    nc = k.nc
    with ExitStack() as tmp:
        sq = k.sbuf("hg_sq", [P, HEADS2, T], ctx=tmp)
        squared = Signal(tmp, nc, "hg_squared")
        summed = Signal(tmp, nc, "hg_squares_summed")
        mean = Signal(tmp, nc, "hg_mean_ready")
        root = Signal(tmp, nc, "hg_root_ready")
        with nc.Block() as block:
            @block.scalar
            def _(act):
                act.activation(sq[:], out, ACT.Square).then_inc(squared.sem, 1)
                act.wait_ge(mean.sem, 1)
                act.activation(sq[:], sq[:], ACT.Sqrt).then_inc(root.sem, 1)

            @block.tensor
            def _(pe):
                pe.wait_ge(squared.sem, 1)
                for h in range(HEADS2):
                    mm = pe.matmul(k.ps[:, h], k.ones[:], sq[:, h], start=True, stop=True)
                mm.then_inc(summed.sem, 1)

            @block.vector
            def _(dve):
                step = lambda ins: k.dve_steps.then(dve, ins)
                dve.wait_ge(summed.sem, 1)
                dve.tensor_scalar(sq[:], k.ps[:, 0:HEADS2], 1.0 / P, EPS, ALU.mult, ALU.add).then_inc(mean.sem, 1)
                dve.wait_ge(root.sem, 1)
                step(dve.reciprocal(sq[:], sq[:]))
                step(dve.tensor_tensor(sq[:], sq[:], gate, ALU.mult))
                step(dve.tensor_scalar(sq[:], sq[:], k.vec("gn"), None, ALU.mult))
                step(dve.tensor_tensor(out, out, sq[:], ALU.mult))


def spread(dve, src, dst, scale):
    to = dst.rearrange("p (a r) n -> p a r n", r=4)
    of = src.rearrange("p (a r) n -> p a r n", r=4)
    for r in range(4):
        for s in range(2):
            rows = slice(64 * s, 64 * (s + 1))
            at = 32 * r + 16 * s
            ins = dve.tensor_scalar(to[rows, :, r, at:at + 16], of[rows, :, r, :], scale, None, ALU.mult)
    return ins


def s5(k, u, out):
    nc = k.nc
    HALF = S5T // 2
    with ExitStack() as ctx:
        b_t = k.sbuf("s5_b_t", [P, 2, S5T, P], ctx=ctx)
        c_x = k.sbuf("s5_c_x", [P, 2, S5T, P], ctx=ctx)
        mag = k.sbuf("s5_mag", [P, S5T], ctx=ctx)
        unit = k.sbuf("s5_unit", [P, 2, S5T], ctx=ctx)
        with ExitStack() as tmp:
            load = k.sbuf("s5_load", [P, 4, S5T, 16], ctx=tmp)
            bb = k.sbuf("s5_bb", [P, 3, S5T, 16], ctx=tmp)
            s = k.sbuf("s5_small", [P, 10, S5T], ctx=tmp)
            loads = Signal(tmp, nc, "s5_loaded")
            handed = Signal(tmp, nc, "s5_to_act")
            acted = Signal(tmp, nc, "s5_act_done")
            with nc.Block() as block:
                @block.sync
                def _(sp):
                    for n, name in enumerate(("b_re", "b_im", "c_re", "c_im")):
                        sp.dma_start(load[:, n], k.dram["s5_" + name]).then_inc(loads.sem, 16)

                @block.scalar
                def _(act):
                    act.activation(s[:, 0], k.vec("log_dt"), ACT.Exp).then_inc(acted.sem, 1)
                    act.wait_ge(handed.sem, 1)
                    act.activation(mag[:], s[:, 1], ACT.Exp).then_inc(acted.sem, 1)
                    act.wait_ge(handed.sem, 2)
                    act.activation(unit[:, 0], s[:, 5], ACT.Sin).then_inc(acted.sem, 1)
                    act.activation(unit[:, 1], s[:, 4], ACT.Sin).then_inc(acted.sem, 1)

                @block.vector
                def _(dve):
                    step = lambda ins: k.dve_steps.then(dve, ins)
                    tt = lambda o, a, b, op: step(dve.tensor_tensor(o, a, b, op))
                    ar, ai = k.vec("a_re"), k.vec("a_im")
                    step(dve.memset(b_t[:], 0.0))
                    step(dve.memset(c_x[:], 0.0))
                    dve.wait_ge(acted.sem, 1)
                    dve.tensor_tensor(s[:, 1], ar, s[:, 0], ALU.mult).then_inc(handed.sem, 1)
                    tt(s[:, 2], ai, s[:, 0], ALU.mult)
                    reduce_angle(k, dve, s[:, 2], s[:, 3], s[:, 4], s[:, 5])
                    dve.sem_inc(handed.sem, 1)
                    dve.wait_ge(acted.sem, 4)
                    tt(s[:, 0], mag[:], unit[:, 0], ALU.mult)
                    step(dve.tensor_scalar(s[:, 0], s[:, 0], -1.0, None, ALU.add))
                    tt(s[:, 1], mag[:], unit[:, 1], ALU.mult)
                    tt(s[:, 2], ar, ar, ALU.mult)
                    tt(s[:, 3], ai, ai, ALU.mult)
                    tt(s[:, 2], s[:, 2], s[:, 3], ALU.add)
                    step(dve.reciprocal(s[:, 2], s[:, 2]))
                    tt(s[:, 3], s[:, 0], ar, ALU.mult)
                    tt(s[:, 4], s[:, 1], ai, ALU.mult)
                    tt(s[:, 3], s[:, 3], s[:, 4], ALU.add)
                    tt(s[:, 6], s[:, 3], s[:, 2], ALU.mult)
                    tt(s[:, 3], s[:, 1], ar, ALU.mult)
                    tt(s[:, 4], s[:, 0], ai, ALU.mult)
                    tt(s[:, 3], s[:, 3], s[:, 4], ALU.subtract)
                    tt(s[:, 7], s[:, 3], s[:, 2], ALU.mult)
                    dve.wait_ge(loads.sem, 64)
                    wide = lambda n: s[:, n].unsqueeze(2).to_broadcast((P, S5T, 16))
                    tt(bb[:, 0], load[:, 0], wide(6), ALU.mult)
                    tt(bb[:, 2], load[:, 1], wide(7), ALU.mult)
                    tt(bb[:, 0], bb[:, 0], bb[:, 2], ALU.subtract)
                    tt(bb[:, 1], load[:, 1], wide(6), ALU.mult)
                    tt(bb[:, 2], load[:, 0], wide(7), ALU.mult)
                    tt(bb[:, 1], bb[:, 1], bb[:, 2], ALU.add)
                    for n in range(2):
                        step(spread(dve, bb[:, n], b_t[:, n], 1.0))
                        step(spread(dve, load[:, 2 + n], c_x[:, n], 1.0 if n == 0 else -1.0))
        squares = [b_t[:, n, t] for n in range(2) for t in range(S5T)]
        token_major(k, "s5_b", squares, squares)
        y = k.sbuf("s5_y", [P, 4, T], ctx=ctx)
        with ExitStack() as tmp:
            turn = k.sbuf("s5_turn", [P, 2, HALF, T], ctx=tmp)
            s5_scan(k, u, y, turn, unit, mag, b_t, c_x)
        state = k.sbuf("s5_mixed", [P, 4, T], ctx=ctx)
        s5_glu(k, y, state)
        split_tiles(k, "s5_mixed", state, out, 4)


def s5_scan(k, u, y, turn, unit, mag, b_t, c_x):
    nc = k.nc
    HALF = S5T // 2
    with ExitStack() as tmp:
        part = k.sbuf("s5_part", [P, 2, T], ctx=tmp)
        w = k.sbuf("s5_w", [P, 2, 2, T], ctx=tmp)
        x = k.sbuf("s5_x", [P, 2, 2, T], ctx=tmp)
        ppart = k.sbuf("s5_pool_part", [P, T], ctx=tmp)
        dbl = k.sbuf("s5_double", [P, 2, 2, S5T], ctx=tmp)
        fed = Signal(tmp, nc, "s5_inputs_ready")
        rotated = Signal(tmp, nc, "s5_inputs_read")
        scanned = Signal(tmp, nc, "s5_scanned")
        real = Signal(tmp, nc, "s5_real_ready")
        imag = Signal(tmp, nc, "s5_imag_ready")
        done = Signal(tmp, nc, "s5_tile_multiplied")
        skipped = Signal(tmp, nc, "s5_skip_added")
        with nc.Block() as block:
            @block.tensor
            def _(pe):
                def feed(t):
                    if t >= 2:
                        pe.wait_ge(rotated.sem, t - 1)
                    for n in range(2):
                        mm = pe.matmul(k.ps[:, 2 * (t % 2) + n], b_t[:, n, t], u[:, t // 4], start=True, stop=True)
                    mm.then_inc(fed.sem, 1)

                feed(0)
                for t in range(S5T):
                    if t + 1 < S5T:
                        feed(t + 1)
                    bank = 4 + (t // 4) % 2
                    if t % 4 == 0 and t >= 8:
                        pe.wait_ge(skipped.sem, t // 4 - 1)
                    pe.wait_ge(real.sem, t + 1)
                    pe.matmul(k.ps[:, bank], c_x[:, 0, t], x[:, t % 2, 0], start=t % 4 == 0, stop=False)
                    pe.wait_ge(imag.sem, t + 1)
                    pe.matmul(k.ps[:, bank], c_x[:, 1, t], x[:, t % 2, 1], start=False, stop=t % 4 == 3)\
                      .then_inc(done.sem, 1)

            @block.gpsimd
            def _(pool):
                for t in range(S5T):
                    cos, sin = turn[:, 0, t % HALF], turn[:, 1, t % HALF]
                    pool.wait_ge(scanned.sem, t + 1)
                    if t >= 2:
                        pool.wait_ge(done.sem, t - 1)
                    pool.tensor_tensor(ppart[:], sin, w[:, t % 2, 1], ALU.mult)
                    k.pool_steps.then(pool, pool.tensor_tensor(x[:, t % 2, 0], cos, w[:, t % 2, 0], ALU.mult))
                    pool.tensor_tensor(x[:, t % 2, 0], x[:, t % 2, 0], ppart[:], ALU.subtract).then_inc(real.sem, 1)
                    pool.wait_ge(real.sem, t + 1)

            @block.vector
            def _(dve):
                step = lambda ins: k.dve_steps.then(dve, ins)
                tt = lambda o, a, b, op: step(dve.tensor_tensor(o, a, b, op))

                def tables(half):
                    own = slice(half * HALF, (half + 1) * HALF)
                    c, s = turn[:, 0], turn[:, 1]
                    dve.memset(c[:, :, 0:1], 1.0)
                    step(dve.memset(s[:, :, 0:1], 0.0))
                    step(dve.tensor_copy(dbl[:, 0, :, 0:HALF], unit[:, :, own]))
                    n, m = 1, 0
                    while n < T:
                        ca, sa = dbl[:, m, 0, 0:HALF], dbl[:, m, 1, 0:HALF]
                        cw, sw = (a.unsqueeze(2).to_broadcast((P, HALF, n)) for a in (ca, sa))
                        lo, hi = slice(0, n), slice(n, 2 * n)
                        cols = part[:].rearrange("p a t -> p (a t)")
                        done_ = 0
                        fit = min(HALF, 2 * T // n)
                        while done_ < HALF:
                            g = slice(done_, done_ + fit)
                            tmp_ = cols[:, 0:fit * n].rearrange("p (g t) -> p g t", t=n)
                            tt(tmp_, s[:, g, lo], sw[:, g], ALU.mult)
                            tt(c[:, g, hi], c[:, g, lo], cw[:, g], ALU.mult)
                            tt(c[:, g, hi], c[:, g, hi], tmp_, ALU.subtract)
                            tt(tmp_, c[:, g, lo], sw[:, g], ALU.mult)
                            tt(s[:, g, hi], s[:, g, lo], cw[:, g], ALU.mult)
                            tt(s[:, g, hi], s[:, g, hi], tmp_, ALU.add)
                            done_ += fit
                        c2, s2 = dbl[:, 1 - m, 0, 0:HALF], dbl[:, 1 - m, 1, 0:HALF]
                        tt(c2, ca, ca, ALU.mult)
                        tt(s2, sa, sa, ALU.mult)
                        tt(c2, c2, s2, ALU.subtract)
                        tt(s2, ca, sa, ALU.mult)
                        step(dve.tensor_scalar(s2, s2, 2.0, None, ALU.mult))
                        n, m = 2 * n, 1 - m

                for t in range(S5T):
                    if t % HALF == 0:
                        if t:
                            dve.wait_ge(real.sem, t)
                        tables(t // HALF)
                    cos, sin = turn[:, 0, t % HALF], turn[:, 1, t % HALF]
                    br, bi = k.ps[:, 2 * (t % 2)], k.ps[:, 2 * (t % 2) + 1]
                    wr, wi = w[:, t % 2, 0], w[:, t % 2, 1]
                    dve.wait_ge(fed.sem, t + 1)
                    if t >= 2:
                        dve.wait_ge(real.sem, t - 1)
                    dve.tensor_tensor(part[:, 0], br, cos, ALU.mult)
                    tt(part[:, 1], bi, sin, ALU.mult)
                    tt(wr, part[:, 0], part[:, 1], ALU.add)
                    dve.tensor_tensor(part[:, 0], bi, cos, ALU.mult)
                    dve.tensor_tensor(part[:, 1], br, sin, ALU.mult).then_inc(rotated.sem, 1)
                    dve.wait_ge(rotated.sem, t + 1)
                    tt(wi, part[:, 0], part[:, 1], ALU.subtract)
                    decay = mag[:, t:t + 1].to_broadcast((P, T))
                    dve.tensor_tensor_scan(wr, decay, wr, 0.0, ALU.mult, ALU.add)
                    dve.tensor_tensor_scan(wi, decay, wi, 0.0, ALU.mult, ALU.add).then_inc(scanned.sem, 1)
                    dve.wait_ge(scanned.sem, t + 1)
                    if t >= 2:
                        dve.wait_ge(done.sem, t - 1)
                    dve.tensor_tensor(part[:, 0], wi, cos, ALU.mult)
                    tt(part[:, 1], wr, sin, ALU.mult)
                    dve.tensor_tensor(x[:, t % 2, 1], part[:, 0], part[:, 1], ALU.add).then_inc(imag.sem, 1)
                    dve.wait_ge(imag.sem, t + 1)
                    if t % 4 == 3:
                        m = t // 4
                        dve.wait_ge(done.sem, t + 1)
                        dve.scalar_tensor_tensor(y[:, m], u[:, m], k.vec("d_skip")[:, m:m + 1], k.ps[:, 4 + m % 2],
                                                 ALU.mult, ALU.add).then_inc(skipped.sem, 1)


def s5_glu(k, y, out):
    nc = k.nc
    with ExitStack() as tmp:
        w = k.sbuf("glu_w", [P, 4, 512], ctx=tmp)
        loads = Signal(tmp, nc, "glu_loaded")
        acted = Signal(tmp, nc, "glu_gelu_ready")
        gated = Signal(tmp, nc, "glu_gate_ready")
        product = Signal(tmp, nc, "glu_product_ready")
        with nc.Block() as block:
            @block.sync
            def _(sp):
                sp.dma_start(w[:], k.dram["glu_w"]).then_inc(loads.sem, 16)

            @block.scalar
            def _(act):
                for m in range(4):
                    act.activation(y[:, m], y[:, m], ACT.Gelu).then_inc(acted.sem, 1)
                for m in range(4):
                    act.wait_ge(product.sem, m + 1)
                    act.activation(out[:, m], k.ps[:, m], ACT.Sigmoid, bias=k.vec("glu_b")[:, m:m + 1])\
                       .then_inc(gated.sem, 1)

            @block.tensor
            def _(pe):
                pe.wait_ge(loads.sem, 16)
                pe.wait_ge(acted.sem, 4)
                for m in range(4):
                    for x in range(4):
                        mm = pe.matmul(k.ps[:, m], w[:, x, m * P:(m + 1) * P], y[:, x], start=x == 0, stop=x == 3)
                    mm.then_inc(product.sem, 1)

            @block.vector
            def _(dve):
                for m in range(4):
                    dve.wait_ge(gated.sem, m + 1)
                    dve.tensor_tensor(out[:, m], out[:, m], y[:, m], ALU.mult)


def mixer2(k, gain):
    scaled_gain(k, "norm_mix_w_2", k.mod[:, KD:2 * KD], gain[:, 0])
    norm(k, gain[:, 0], k.u, k.mod[:, 0:KD])
    with ExitStack() as ctx:
        state_in = k.sbuf("s5_in", [P, 4, T], ctx=ctx)
        with ExitStack() as inner:
            proj = k.sbuf("proj2", [P, 16, T], ctx=inner)
            copy_tiles(k, k.dram["w_in_2"], 16, proj, k.u)
            copy_tiles(k, k.dram["w_in_2_state"], 4, state_in, k.u)
            mixed = k.sbuf("hg_mixed", [P, 4, T], ctx=inner)
            hgrn(k, proj, mixed[:])
            split_tiles(k, "hg_mixed", mixed, k.u)
        s5(k, state_in, k.u)
    residual(k, k.dram["w_out_2"], KD, k.u, k.mod[:, 2 * KD:3 * KD])


PH = 8
TOPK = 16
ROUNDS = 4
I1 = P // ROUNDS
LOW = -3.0e38


def top16(k, dve, src, work, values, index):
    step = lambda ins: k.dve_steps.then(dve, ins)
    step(dve.max(values[:, 0:8], src))
    dve.max_index(index[:, 0:8], values[:, 0:8], src)
    step(dve.match_replace(work, values[:, 0:8], src, LOW))
    step(dve.max(values[:, 8:16], work))
    return dve.max_index(index[:, 8:16], values[:, 8:16], work)


def route(k, by_choice):
    nc = k.nc
    with ExitStack() as ctx:
        q = k.sbuf("peer_q", [P, 2 * PH, T], ctx=ctx)
        keys = k.sbuf("peer_keys", [P, 2, P], ctx=ctx)
        copy_tiles(k, k.dram["peer_wq"], 2 * PH, q, k.u)
        work = k.sbuf("peer_work", [P, 2 * P], ctx=ctx)
        best = k.sbuf("peer_best", [P, PH, 2, TOPK], ctx=ctx)
        which = k.sbuf("peer_which", [P, PH, 2, TOPK], U32, ctx)
        whichf = k.sbuf("peer_whichf", [P, PH, 2, TOPK], ctx=ctx)
        cand = k.sbuf("peer_cand", [P, PH, TOPK, TOPK], ctx=ctx)
        top = k.sbuf("peer_top", [P, PH, TOPK], ctx=ctx)
        place = k.sbuf("peer_place", [P, PH, TOPK], U32, ctx)
        part = k.sbuf("peer_part", [P, 2, PH, TOPK], U32, ctx)
        partf = k.sbuf("peer_partf", [P, 2, PH * TOPK], ctx=ctx)
        hot = k.sbuf("peer_hot", [P, PH * TOPK, TOPK], ctx=ctx)
        chosen = k.sbuf("peer_chosen", [P, QT, 3, PH * TOPK], ctx=ctx)
        count = k.sbuf("peer_count", [P, TOPK], ctx=ctx)
        total = k.sbuf("peer_total", [P, PH], ctx=ctx)
        loads = Signal(ctx, nc, "peer_keys_loaded")
        counted = Signal(ctx, nc, "peer_count_ready")
        scored = Signal(ctx, nc, "peer_scored")
        ranked = Signal(ctx, nc, "peer_ranked")
        shifted = Signal(ctx, nc, "peer_shifted")
        exped = Signal(ctx, nc, "peer_exped")
        with nc.Block() as block:
            @block.sync
            def _(sp):
                sp.dma_start(keys[:], k.dram["peer_keys"]).then_inc(loads.sem, 16)

            @block.gpsimd
            def _(pool):
                pool.iota(count[:], pattern=[[1, TOPK]], base=0, channel_multiplier=0,
                          allow_small_or_imprecise_dtypes=True).then_inc(counted.sem, 1)

            @block.tensor
            def _(pe):
                pe.wait_ge(loads.sem, 16)
                for n in range(QT * 4):
                    qt, quad = n // 4, n % 4
                    if n >= BANKS:
                        pe.wait_ge(ranked.sem, n - BANKS + 1)
                    for m in range(4):
                        t = 4 * quad + m
                        mm = pe.matmul(k.ps[:, n % BANKS, m * P:(m + 1) * P], q[:, t, qt * P:(qt + 1) * P],
                                       keys[:, t % 2], start=True, stop=True)
                    mm.then_inc(scored.sem, 1)

            @block.scalar
            def _(act):
                for qt in range(QT):
                    act.wait_ge(shifted.sem, qt + 1)
                    gate = chosen[:, qt, 2]
                    act.activation(gate, gate, ACT.Exp).then_inc(exped.sem, 1)

            @block.vector
            def _(dve):
                step = lambda ins: k.dve_steps.then(dve, ins)
                tt = lambda o, a, b, op: step(dve.tensor_tensor(o, a, b, op))
                dve.wait_ge(counted.sem, 1)
                for qt in range(QT):
                    for quad in range(4):
                        n = qt * 4 + quad
                        dve.wait_ge(scored.sem, n + 1)
                        for m in range(4):
                            t = 4 * quad + m
                            ins = top16(k, dve, k.ps[:, n % BANKS, m * P:(m + 1) * P], work[:, 0:P],
                                        best[:, t // 2, t % 2], which[:, t // 2, t % 2])
                            step(ins)
                        dve.sem_inc(ranked.sem, 1)
                    step(dve.tensor_copy(whichf[:], which[:]))
                    first = best[:, :, 0].unsqueeze(3).to_broadcast((P, PH, TOPK, TOPK))
                    second = best[:, :, 1].unsqueeze(2).to_broadcast((P, PH, TOPK, TOPK))
                    tt(cand[:], first, second, ALU.add)
                    for h in range(PH):
                        step(top16(k, dve, cand[:, h].rearrange("p a b -> p (a b)"), work[:], top[:, h], place[:, h]))
                    gate = chosen[:, qt, 2].rearrange("p (h c) -> p h c", h=PH)
                    dve.tensor_tensor(gate, top[:], top[:, :, 0:1].to_broadcast((P, PH, TOPK)), ALU.subtract)\
                       .then_inc(shifted.sem, 1)
                    dve.tensor_scalar(part[:, 0], place[:], 4, None, ALU.logical_shift_right)
                    step(dve.tensor_scalar(part[:, 1], place[:], 15, None, ALU.bitwise_and))
                    step(dve.tensor_copy(partf[:], part[:].rearrange("p s h c -> p s (h c)")))
                    for s in range(2):
                        at = partf[:, s].unsqueeze(2).to_broadcast((P, PH * TOPK, TOPK))
                        tt(hot[:], at, count[:].unsqueeze(1).to_broadcast((P, PH * TOPK, TOPK)), ALU.is_equal)
                        names = whichf[:, :, s].unsqueeze(2).to_broadcast((P, PH, TOPK, TOPK))
                        view = hot[:].rearrange("p (h c) a -> p h c a", h=PH)
                        tt(view, view, names, ALU.mult)
                        step(dve.tensor_reduce(chosen[:, qt, s], hot[:], AX.X, ALU.add))
                    dve.wait_ge(exped.sem, qt + 1)
                    step(dve.tensor_reduce(total[:], gate, AX.X, ALU.add))
                    step(dve.reciprocal(total[:], total[:]))
                    tt(gate, gate, total[:].unsqueeze(2).to_broadcast((P, PH, TOPK)), ALU.mult)
        token_major(k, "choices", [chosen[:, qt, s] for s in range(3) for qt in range(QT)],
                    [by_choice[:, s, qt * P:(qt + 1) * P] for s in range(3) for qt in range(QT)])


TOK = T // I1
PIECES = 3


class Choices:

    def __init__(self, k, ctx):
        self.names = k.sbuf("choice_names", [P, 2, T], BF16, ctx)
        self.gates = k.sbuf("choice_gates", [P, PIECES, T], BF16, ctx)
        self.count = k.sbuf("expert_count", [P, P, TOK], BF16, ctx)


def split_choices(k, by_choice, choices):
    nc = k.nc
    with ExitStack() as tmp:
        rest = k.sbuf("gate_rest", [P, T], ctx=tmp)
        iota = k.sbuf("expert_iota", [P, P], ctx=tmp)
        counted = Signal(tmp, nc, "expert_iota_ready")
        with nc.Block() as block:
            @block.gpsimd
            def _(pool):
                pool.iota(iota[:], pattern=[[1, P]], base=0, channel_multiplier=0,
                          allow_small_or_imprecise_dtypes=True).then_inc(counted.sem, 1)

            @block.vector
            def _(dve):
                step = lambda ins: k.dve_steps.then(dve, ins)
                dve.tensor_copy(choices.names[:], by_choice[:, 0:2])
                step(dve.tensor_copy(choices.gates[:, 0], by_choice[:, 2]))
                step(dve.tensor_tensor(rest[:], by_choice[:, 2], choices.gates[:, 0], ALU.subtract))
                step(dve.tensor_copy(choices.gates[:, 1], rest[:]))
                step(dve.tensor_tensor(rest[:], rest[:], choices.gates[:, 1], ALU.subtract))
                dve.tensor_copy(choices.gates[:, 2], rest[:])
                dve.wait_ge(counted.sem, 1)
                dve.tensor_copy(choices.count[:], iota[:].unsqueeze(2).to_broadcast((P, P, TOK)))


def expert_weights(k, r, choices, weight, sig):
    nc = k.nc
    rows_ready, hot_ready, cols_ready, rest_ready, product, copied = sig
    iters = T // (2 * TOK)
    with ExitStack() as tmp:
        rows = k.sbuf("hot_i2", [P, 2, P, TOK], BF16, tmp)
        hot = k.sbuf("hot_i1", [P, 2, I1, TOK], BF16, tmp)
        cols = k.sbuf("gated_i1", [P, 2, PIECES, I1, TOK], BF16, tmp)

        def gated(eng, b, piece, tokens):
            gates = choices.gates[:, piece, tokens].unsqueeze(1).to_broadcast((P, I1, TOK))
            return eng.tensor_tensor(cols[:, b, piece], hot[:, b], gates, ALU.mult)

        with nc.Block() as block:
            @block.gpsimd
            def _(pool):
                with pool.Fori(0, iters) as i:
                    for b in range(2):
                        pool.wait_ge(hot_ready[b].sem, i + hot_ready[b].at(1))
                        gated(pool, b, 2, bass.ds(i * (2 * TOK) + b * TOK, TOK)).then_inc(rest_ready[b].sem, 1)

            @block.vector
            def _(dve):
                with dve.Fori(0, iters) as i:
                    for b in range(2):
                        tokens = bass.ds(i * (2 * TOK) + b * TOK, TOK)
                        dve.wait_ge(product[b].sem, i + product[b].at(0))
                        dve.tensor_tensor(hot[:, b], choices.names[:, 0, tokens].unsqueeze(1).to_broadcast((P, I1, TOK)),
                                          choices.count[:, r * I1:(r + 1) * I1], ALU.is_equal).then_inc(hot_ready[b].sem, 1)
                        dve.tensor_tensor(rows[:, b], choices.names[:, 1, tokens].unsqueeze(1).to_broadcast((P, P, TOK)),
                                          choices.count[:], ALU.is_equal).then_inc(rows_ready[b].sem, 1)
                        dve.wait_ge(hot_ready[b].sem, i + hot_ready[b].at(1))
                        for piece in range(2):
                            gated(dve, b, piece, tokens).then_inc(cols_ready[b].sem, 1)

            @block.tensor
            def _(pe):
                with pe.Fori(0, iters) as i:
                    for b in range(2):
                        pe.wait_ge(rows_ready[b].sem, i + rows_ready[b].at(1))
                        pe.wait_ge(cols_ready[b].sem, i * 2 + cols_ready[b].at(2))
                        pe.wait_ge(rest_ready[b].sem, i + rest_ready[b].at(1))
                        pe.wait_ge(copied[b].sem, i + copied[b].at(0))
                        for t in range(TOK):
                            for piece in range(PIECES):
                                mm = pe.matmul(k.ps[:, b, t * I1:(t + 1) * I1], rows[:, b, :, t], cols[:, b, piece, :, t],
                                               start=piece == 0, stop=piece == PIECES - 1)
                        mm.then_inc(product[b].sem, 1)

            @block.scalar
            def _(act):
                with act.Fori(0, iters) as i:
                    for b in range(2):
                        act.wait_ge(product[b].sem, i + product[b].at(1))
                        act.activation(weight[:, :, bass.ds(i * (2 * TOK) + b * TOK, TOK)].rearrange("p e t -> p t e"),
                                       k.ps[:, b].rearrange("p (t e) -> p t e", t=TOK), ACT.Copy)\
                           .then_inc(copied[b].sem, 1)
    for b in range(2):
        for s in (rows_ready, hot_ready, rest_ready, product, copied):
            s[b].passed(iters)
        cols_ready[b].passed(2 * iters)


def experts(k, r, weight, gate, sig):
    nc = k.nc
    gelu_ready, product_ready, high_ready, low_ready = sig
    with ExitStack() as tmp:
        acted = k.sbuf("expert_act", [P, 2, T], ctx=tmp)
        product = k.sbuf("expert_product", [P, 2, T], ctx=tmp)
        coef = Split(k, tmp, "expert_coef", 8)
        iters = I1 // 8
        base = r * I1

        def source(name, j):
            return lambda i: k.dram[name][bass.ds(i * 8 + (base + j), 1), :, :].rearrange("a p n -> p (a n)")

        def coef_is_ready(pe, i):
            pe.wait_ge(low_ready.sem, i * 8 + low_ready.at(8))

        chunks = [(source("peer_u", e), [(e % 4, k.ps[:, e % 4], [(x, k.u.high[:, x], k.u.low[:, x]) for x in range(KD)], True, True, None)])
                  for e in range(8)]
        chunks += [(source("peer_v", d), [(4 + d % 4, k.ps[:, 4 + d % 4], [(x, coef.high[:, x], coef.low[:, x]) for x in range(8)],
                                           True, True, coef_is_ready if d == 0 else None)]) for d in range(KD)]
        stream = Stream(k, iters, chunks)
        with nc.Block() as block:
            @block.sync
            def _(sp):
                stream.load(sp)

            @block.gpsimd
            def _(pool):
                stream.split_low(pool)

            @block.tensor
            def _(pe):
                stream.multiply(pe)

            @block.scalar
            def _(act):
                def epilogue(i, e):
                    if e < 8:
                        stream.wait_products(act, i, e)
                        act.wait_ge(product_ready.sem, i * 8 + product_ready.at(e - 1))
                        act.activation(acted[:, e % 2], k.ps[:, e % 4], ACT.Gelu).then_inc(gelu_ready.sem, 1)

                def after(i, e):
                    if e < 8:
                        act.wait_ge(product_ready.sem, i * 8 + product_ready.at(e + 1))
                        act.activation(coef.high[:, e], product[:, e % 2], ACT.Copy).then_inc(high_ready.sem, 1)

                stream.scalar(act, epilogue, after)

            @block.vector
            def _(dve):
                with dve.Fori(0, iters) as i:
                    for e in range(8):
                        dve.wait_ge(gelu_ready.sem, i * 8 + gelu_ready.at(e + 1))
                        dve.sem_inc(k.emptied[e % 4].sem, 1)
                        dve.wait_ge(low_ready.sem, i * 8 + low_ready.at(e - 1))
                        dve.tensor_tensor(product[:, e % 2], acted[:, e % 2], one(weight, i * 8 + e), ALU.mult)\
                           .then_inc(product_ready.sem, 1)
                        dve.wait_ge(high_ready.sem, i * 8 + high_ready.at(e + 1))
                        dve.tensor_tensor(coef.low[:, e], product[:, e % 2], coef.high[:, e].bitcast(F32),
                                          ALU.subtract).then_inc(low_ready.sem, 1)
                    for d in range(KD):
                        stream.wait_products(dve, i, 8 + d)
                        dve.scalar_tensor_tensor(k.h[:, d], k.ps[:, 4 + d % 4], gate[:, d:d + 1], k.h[:, d],
                                                 ALU.mult, ALU.add).then_inc(k.emptied[4 + d % 4].sem, 1)
        stream.finish()
    for s in (gelu_ready, product_ready, high_ready, low_ready):
        s.passed(8 * iters)


def peer(k, gain):
    nc = k.nc
    scaled_gain(k, "norm_ffn_w_2", k.mod[:, 4 * KD:5 * KD], gain[:, 1])
    norm(k, gain[:, 1], k.u, k.mod[:, 3 * KD:4 * KD])
    with ExitStack() as ctx:
        choices = Choices(k, ctx)
        with ExitStack() as tmp:
            by_choice = k.sbuf("by_choice", [P, 3, T], ctx=tmp)
            route(k, by_choice)
            split_choices(k, by_choice, choices)
        weight = k.sbuf("expert_weight", [P, I1, T], ctx=ctx)
        for r in range(ROUNDS):
            expert_weights(k, r, choices, weight, k.weight_signals)
            experts(k, r, weight, k.mod[:, 5 * KD:6 * KD], k.expert_signals)


def signals_of_loops(k):
    pair = lambda name, base=0: [k.new_sem(f"{name}{b}", base) for b in range(2)]
    k.ffn_signals = (pair("gated_ready"), pair("product_ready", 1), pair("hid_high_ready"), pair("hid_low_ready", 1))
    k.weight_signals = (pair("rows_ready"), pair("hot_ready"), pair("cols_ready"), pair("last_cols_ready"),
                        pair("weights_ready", 1), pair("weights_copied", 1))
    k.expert_signals = (k.new_sem("gelu_ready"), k.new_sem("expert_product_ready", 2), k.new_sem("coef_high_ready"),
                        k.new_sem("coef_low_ready", 2))
    with k.nc.Block() as block:
        @block.vector
        def _(dve):
            for b in range(2):
                dve.sem_inc(k.ffn_signals[1][b].sem, 1)
                dve.sem_inc(k.ffn_signals[3][b].sem, 1)
                dve.sem_inc(k.weight_signals[4][b].sem, 1)
                dve.sem_inc(k.weight_signals[5][b].sem, 1)
            dve.sem_inc(k.expert_signals[1].sem, 2)
            dve.sem_inc(k.expert_signals[3].sem, 2)


def store(k, y):
    stored = k.new_sem("stored")
    with k.nc.Block() as block:
        @block.sync
        def _(sp):
            sp.dma_start(k.dram["y"], y[:]).then_inc(stored.sem, 16)
            sp.wait_ge(stored.sem, 16)


def build(nc, dram):
    with ExitStack() as ctx:
        k = Kernel(nc, ctx, dram)
        gain = k.sbuf("gain", [P, 2, KD])
        setup(k)
        signals_of_loops(k)
        ffn(k, "ffn1", k.vec("norm_ffn1"), k.ffn_signals)
        mixer1(k)
        ffn(k, "ffn2", k.vec("norm_ffn2"), k.ffn_signals)
        norm(k, k.vec("norm_final"), None, plain=k.h)
        modulation(k)
        mixer2(k, gain)
        peer(k, gain)
        norm(k, k.vec("final_norm_w_2"), None, plain=k.h)
        store(k, k.h)



def tiles8(w):
    kin, n = w.shape
    return w.reshape(kin // P, P, n // P, P).transpose(2, 1, 0, 3).reshape(n // P, P, kin)


def down_chunks(w):
    c = np.zeros((KD, P, 3 * KD, P), w.dtype)
    c[:, :, :KF] = w.reshape(KF, P, KD, P).transpose(2, 1, 0, 3)
    return c.reshape(KD, P, 3, KD * P).transpose(0, 2, 1, 3).reshape(3 * KD, P, KD * P)


def features(v):
    return v.reshape(-1, P).T


def projection_columns():
    nq, kc, vc, ksl, vsl, kwn, vwn, ng, sq, sk, sv, ga, gb = np.cumsum(
        [0, 512, 128, 128, 128, 128, 128, 128, 24, 512, 64, 64, 1024])
    r = np.arange
    head = lambda base, a: r(base + HD * a, base + HD * (a + 1))
    tiles = [np.r_[head(nq, j), head(nq, 4 + j)] for j in range(4)]
    tiles += [r(ksl, ksl + P), r(kwn, kwn + P)]
    tiles += [np.r_[head(sq, j), head(sq, 4 + j)] for j in range(4)]
    tiles += [np.r_[head(sk, 0), head(sk, 0)]]
    tiles += [np.r_[head(kc, g), head(vc, g)] for g in range(2)]
    tiles += [r(vsl, vsl + P), r(vwn, vwn + P)]
    tiles += [np.r_[head(sv, 0), r(ng, ng + 24), np.full(P - HD - 24, -1)]]
    return np.concatenate(tiles + [r(ga, ga + D), r(gb, gb + D)])


def lay_out(a):
    g = {n: np.asarray(v) for n, v in a.items()}
    first = lambda n: g[n][0]
    out = {"x": g["x"][0].T.reshape(KD, P, T).transpose(1, 0, 2)}
    for n in (1, 2):
        gate, up = tiles8(first(f"ffn{n}_gate")), tiles8(first(f"ffn{n}_up"))
        out[f"ffn{n}_gu"] = np.stack([gate, up], 1).reshape(2 * KF, P, D)
        out[f"ffn{n}_down"] = down_chunks(first(f"ffn{n}_down"))
    w = first("w_in")
    w = np.concatenate([w, np.zeros((D, 1), w.dtype)], 1)[:, projection_columns()]
    tiles = tiles8(w)
    out["w_in"], out["w_in_gates"] = tiles[:PROJ], tiles[PROJ:]
    out["positions"] = g["positions"].astype(np.int32).reshape(1, T)
    w1 = np.concatenate([first(f"cmp_{n}_w1").reshape(32, HD, 256).transpose(1, 0, 2) for n in "kv"])
    out["cmp_w1"] = w1
    w2k, w2v = (first(f"cmp_{n}_w2").reshape(2, P, HD).transpose(1, 0, 2) for n in "kv")
    out["cmp_w2"] = np.concatenate([w2k, w2k, w2v], 2)
    out["cmp_pe"] = np.concatenate([first("cmp_pe_k").T, first("cmp_pe_v").T])
    ab = [first(n).reshape(4, P, KD, P).transpose(2, 1, 0, 3) for n in ("w_branch_a", "w_branch_b")]
    out["w_branch"] = np.concatenate(ab, 2).reshape(KD, P, D)
    out["w_out"] = tiles8(first("w_out"))
    out["ada_w"] = tiles8(first("ada_w_2"))
    tiles = tiles8(first("w_in_2"))
    out["w_in_2"], out["w_in_2_state"] = tiles[:16], tiles[16:]
    out["w_out_2"] = tiles8(first("w_out_2"))
    out["peer_wq"] = tiles8(first("peer_wq_2"))
    out["peer_keys"] = np.stack([first("peer_keys1_2").T, first("peer_keys2_2").T], 1)
    out["peer_u"] = first("peer_u_2").reshape(P, P, KD, P).transpose(0, 3, 2, 1).reshape(P, P, D)
    out["peer_v"] = first("peer_v_2").reshape(P // 8, 8, P, KD, P).transpose(0, 3, 2, 1, 4).reshape(P, P, D)
    for n in ("b_re", "b_im"):
        out["s5_" + n] = first(f"s5_{n}_2").reshape(16, P, 16).transpose(1, 0, 2)
    for n in ("c_re", "c_im"):
        out["s5_" + n] = first(f"s5_{n}_2").transpose(0, 2, 1).reshape(16, P, 16).transpose(1, 0, 2)
    out["glu_w"] = first("s5_glu_w_2").reshape(4, P, 512).transpose(1, 0, 2)
    half = HD // 2
    freq = (np.float32(10000.0) ** (-np.arange(half, dtype=np.float32) / np.float32(half))).astype(np.float32)
    vecs = {n: features(g[n].reshape(-1)) for n in
            ("norm_ffn1", "norm_mix", "norm_ffn2", "norm_final", "norm_mix_w_2", "norm_ffn_w_2",
             "final_norm_w_2", "c_2", "ada_b_2")}
    vecs["lb0"], vecs["lb1"] = (features(g["hg_lower_bounds_2"][i]) for i in range(2))
    vecs["gn"] = features(first("hg_gnorm_w_2"))
    vecs["a_re"], vecs["a_im"] = features(first("s5_a_re_2").reshape(-1)), features(first("s5_a_im_2").reshape(-1))
    vecs["log_dt"] = features(np.repeat(first("s5_log_dt_2"), 64))
    vecs["d_skip"], vecs["glu_b"] = features(first("s5_d_2")), features(first("s5_glu_b_2"))
    vecs["sinks"] = np.broadcast_to(first("swa_sinks"), (P, 8))
    vecs["freq"] = np.tile(freq, P // half).reshape(P, 1)
    out["vecs"] = np.concatenate([vecs[n] for n in VEC], 1)
    return {n: np.ascontiguousarray(v) for n, v in out.items()}


def kernel(**inputs):
    import concourse.bacc as bacc
    from concourse.bass_utils import run_bass_kernel_spmd

    nc = bacc.Bacc("TRN2", target_bir_lowering=False, num_devices=1)
    arrays = lay_out(inputs)
    dram = {n: nc.dram_tensor(f"in_{n}", a.shape, mybir.dt.from_np(a.dtype), kind="ExternalInput").ap()
            for n, a in arrays.items()}
    dram["y"] = nc.dram_tensor("out_y", (P, KD, T), F32, kind="ExternalOutput").ap()
    build(nc, dram)
    r = run_bass_kernel_spmd(nc, [{f"in_{n}": a for n, a in arrays.items()}], core_ids=[0])
    y = r.results[0]["out_y"]
    return np.ascontiguousarray(y.transpose(1, 0, 2).reshape(D, T).T).reshape(1, T, D)
```

```python
from contextlib import ExitStack

import numpy as np

import concourse.bass as bass
from concourse import mybir

F32 = mybir.dt.float32
F32R = mybir.dt.float32r
I32 = mybir.dt.int32
BF16 = mybir.dt.bfloat16
U32 = mybir.dt.uint32
ALU = mybir.AluOpType
ACT = mybir.ActivationFunctionType
AX = mybir.AxisListType

P = 128
T = 512
D = 1024
KD = D // P
FF = 2816
KF = FF // P
HD = 64
QT = T // P
CMP = 31
EPS = 1e-6
NEG = -1e30
SLOTS = 4
PARTS = 2
BANKS = 8
ROUNDS = 4
SCALE = HD ** -0.5
TWO_PI = 2.0 * np.pi

Q0, KSL, KWN, SQ0, SK, KCA, KCB, VSL, VWN, SVG = 0, 4, 5, 6, 10, 11, 12, 13, 14, 15
ROPED = 11
PROJ = 16

VEC = {}
_at = 0
for _name, _n in (("norm_ffn1", 8), ("norm_mix", 8), ("norm_ffn2", 8), ("norm_final", 8),
                  ("norm_mix_w_2", 8), ("norm_ffn_w_2", 8), ("final_norm_w_2", 8), ("c_2", 8),
                  ("ada_b_2", 48), ("lb0", 4), ("lb1", 4), ("gn", 1), ("a_re", 16), ("a_im", 16),
                  ("log_dt", 16), ("d_skip", 4), ("glu_b", 4), ("sinks", 8), ("freq", 1)):
    VEC[_name] = (_at, _n)
    _at += _n
NVEC = _at


class Signal:

    def __init__(self, ctx, nc, name, base=0):
        self.sem = ctx.enter_context(nc.semaphore(name))
        self.base = base

    def at(self, n):
        return self.base + n

    def passed(self, n):
        self.base += n


class Steps:

    def __init__(self, ctx, nc, name):
        self.sem = ctx.enter_context(nc.semaphore(name))
        self.n = 0

    def then(self, eng, ins):
        self.n += 1
        ins.then_inc(self.sem, 1)
        eng.wait_ge(self.sem, self.n)


def one(ap, i):
    return ap[:, bass.ds(i, 1), :].rearrange("p a n -> p (a n)")


def heads_of_streams(dram):
    names = ["ffn1_gu", "ffn1_down", "w_in", "w_in_gates", "w_branch", "w_out", "ffn2_gu", "ffn2_down",
             "w_in_2", "w_in_2_state", "w_out_2", "peer_wq"]
    return [[dram[n][j] for j in range(SLOTS)] for n in names] + \
           [[dram[n][j] for j in range(SLOTS)] for n in ("peer_u", "peer_v")] + \
           [[dram["peer_u"][r * (P // ROUNDS) + j] for j in range(SLOTS)] for r in range(1, ROUNDS)]


ADA_FFN = 3 * KD


class Ada:

    def __init__(self, k, ctx, part):
        self.k, self.part = k, part
        self.weights = k.sbuf("ada_weights", [P, 2, D], ctx=ctx)
        self.cond = k.sbuf("cond", [P, D], ctx=ctx)
        self.product = k.sbuf("ada_product", [P, 2], ctx=ctx)
        self.terms = k.sbuf("ada_terms", [P, D], ctx=ctx)

    def start(self, sp):
        k = self.k
        sp.dma_start(self.cond[:], k.dram["cond_rows"]).then_inc(k.cond_loaded.sem, 16)
        for s in range(2):
            sp.dma_start(self.weights[:, s], k.dram["ada_w"][self.part * ADA_FFN + s]).then_inc(k.ada_loaded[s].sem, 16)

    def silu(self, act):
        k = self.k
        act.wait_ge(k.cond_loaded.sem, k.cond_loaded.at(16))
        act.activation(self.cond[:], self.cond[:], ACT.Silu).then_inc(k.cond_ready.sem, 1)

    def load(self, sp, i):
        k = self.k
        for s in range(2):
            src = k.dram["ada_w"][bass.ds(i * 2 + (self.part * ADA_FFN + 2 + s), 1), :, :].rearrange("a p n -> p (a n)")
            sp.wait_ge(k.ada_summed[s].sem, i + k.ada_summed[s].at(1))
            sp.dma_start(self.weights[:, s], src).then_inc(k.ada_loaded[s].sem, 16)

    def sum(self, dve, i, s):
        k = self.k
        dve.wait_ge(k.ada_loaded[s].sem, i * 16 + k.ada_loaded[s].at(16))
        dve.wait_ge(k.ada_summed[1 - s].sem, i + k.ada_summed[1 - s].at(s))
        dve.tensor_tensor_reduce(out=self.terms[:], in0=self.weights[:, s], in1=self.cond[:], scale=1.0, scalar=0.0,
                                 op0=ALU.mult, op1=ALU.add,
                                 accum_out=self.product[:, s:s + 1]).then_inc(k.ada_reduced[s].sem, 1)
        dve.wait_ge(k.ada_reduced[s].sem, i + k.ada_reduced[s].at(1))
        at = bass.ds(i * 2 + (self.part * ADA_FFN + s), 1)
        dve.tensor_tensor(k.mod[:, at], self.product[:, s:s + 1], k.vec("ada_b_2")[:, at], ALU.add)\
            .then_inc(k.ada_summed[s].sem, 1)

    def finish(self):
        k = self.k
        k.cond_loaded.passed(16)
        k.cond_ready.passed(1)
        for s in range(2):
            k.ada_loaded[s].passed(16 * ADA_FFN // 2)
            k.ada_reduced[s].passed(ADA_FFN // 2)
            k.ada_summed[s].passed(ADA_FFN // 2)


class Kernel:

    def __init__(self, nc, ctx, dram):
        self.nc, self.ctx, self.dram = nc, ctx, dram
        self.heads = heads_of_streams(dram)
        self.names = {}
        self.h = self.sbuf("h", [P, KD, T])
        self.u = Split(self, ctx, "u", KD)
        self.ring = self.sbuf("ring", [P, SLOTS, KD * P])
        self.high = self.sbuf("ring_high", [P, PARTS, KD * P], F32R)
        self.low = self.sbuf("ring_low", [P, PARTS, KD * P], F32R)
        self.total = self.sbuf("squares_total", [P, T])
        self.vecs = self.sbuf("vecs", [P, NVEC])
        self.ident = self.sbuf("ident", [P, P])
        self.ones = self.sbuf("ones", [P, P])
        self.rs = self.sbuf("rs", [P, T])
        self.square = self.rs
        self.mod = self.sbuf("mod", [P, 6 * KD])
        self.ps = ctx.enter_context(nc.psum_tensor("ps", [P, BANKS, T], F32))
        self.dve_steps = Steps(ctx, nc, "dve_steps")
        self.act_steps = Steps(ctx, nc, "act_steps")
        self.pool_steps = Steps(ctx, nc, "pool_steps")
        self.loaded = [self.new_sem(f"slot{s}_loaded") for s in range(SLOTS)]
        self.high_ready = [self.new_sem(f"high{p}_ready") for p in range(PARTS)]
        self.low_ready = [self.new_sem(f"low{p}_ready", 2) for p in range(PARTS)]
        self.used = [self.new_sem(f"split{p}_used", 1) for p in range(PARTS)]
        self.emptied = [self.new_sem(f"bank{b}_emptied", 1) for b in range(BANKS)]
        self.cond_loaded = self.new_sem("cond_loaded")
        self.cond_ready = self.new_sem("cond_ready")
        self.ada_loaded = [self.new_sem(f"ada_loaded{s}") for s in range(2)]
        self.ada_reduced = [self.new_sem(f"ada_reduced{s}") for s in range(2)]
        self.ada_summed = [self.new_sem(f"ada_summed{s}", 1) for s in range(2)]
        self.first_ready = self.new_sem("first_ready")
        self.squares_ready = self.new_sem("squares_ready")
        self.tiles_rounded = self.new_sem("tiles_rounded")
        self.squares_turned = self.new_sem("squares_turned")
        self.squares_copied = self.new_sem("squares_copied")
        self.tile_squared = self.new_sem("tile_squared")
        self.tile_folded = self.new_sem("tile_folded", 1)
        self.folded_ready = self.new_sem("squares_folded")
        self.sumsq_ready = self.new_sem("sumsq_ready")
        self.mean_ready = self.new_sem("mean_ready")
        self.root_ready = self.new_sem("root_ready")
        self.scaled_ready = self.new_sem("scaled_ready")
        self.rounded_ready = self.new_sem("rounded_ready")

    def sbuf(self, name, shape, dtype=F32, ctx=None):
        self.names[name] = self.names.get(name, 0) + 1
        if self.names[name] > 1:
            name = f"{name}_{self.names[name]}"
        return (ctx or self.ctx).enter_context(self.nc.sbuf_tensor(name, shape, dtype))

    def new_sem(self, name, base=0):
        return Signal(self.ctx, self.nc, name, base)

    def vec(self, name):
        at, n = VEC[name]
        return self.vecs[:, at:at + n]


class Split:

    def __init__(self, k, ctx, name, tiles):
        self.high = k.sbuf(f"{name}_high", [P, tiles, T], F32R, ctx)
        self.low = k.sbuf(f"{name}_low", [P, tiles, T], F32R, ctx)


class Stream:

    def __init__(self, k, iters, chunks):
        self.k, self.iters, self.chunks = k, iters, chunks
        assert len(chunks) % SLOTS == 0
        self.then = k.heads.pop(0) if k.heads else []
        self.n = len(chunks)
        self.opened = [0] * BANKS
        for _, groups in chunks:
            for g in groups:
                self.opened[g[0]] += g[3]

    def load_chunk(self, sp, i, j, src):
        k = self.k
        s, p = j % SLOTS, j % PARTS
        sp.wait_ge(k.low_ready[p].sem, i * (self.n // PARTS) + k.low_ready[p].at(j // PARTS - 1))
        sp.dma_start(k.ring[:, s, 0:src.shape[-1]], src).then_inc(k.loaded[s].sem, 16)

    def load(self, sp, beside=None):
        if self.iters > 1:
            with sp.Fori(0, self.iters - 1) as i:
                for j in range(SLOTS, self.n):
                    self.load_chunk(sp, i, j, self.chunks[j][0](i))
                for j in range(SLOTS):
                    self.load_chunk(sp, i + 1, j, self.chunks[j][0](i + 1))
                if beside is not None:
                    beside(i)
        for j in range(SLOTS, self.n):
            self.load_chunk(sp, self.iters - 1, j, self.chunks[j][0](self.iters - 1))
        if beside is not None:
            beside(self.iters - 1)
        for j, src in enumerate(self.then):
            self.load_chunk(sp, self.iters, j, src)

    def split_high(self, act, i, j):
        k = self.k
        s, p = j % SLOTS, j % PARTS
        act.wait_ge(k.loaded[s].sem, i * (16 * self.n // SLOTS) + k.loaded[s].at(16 * (j // SLOTS + 1)))
        act.wait_ge(k.used[p].sem, i * (self.n // PARTS) + k.used[p].at(j // PARTS))
        act.activation(k.high[:, p], k.ring[:, s], ACT.Copy).then_inc(k.high_ready[p].sem, 1)

    def scalar(self, act, epilogue=None, after=None, unrolled=False):
        def turn(i, j, ahead):
            if epilogue is not None:
                epilogue(i, j)
            if ahead:
                if j + PARTS < self.n:
                    self.split_high(act, i, j + PARTS)
                else:
                    self.split_high(act, i + 1, j + PARTS - self.n)
            if after is not None:
                after(i, j)

        self.split_high(act, 0, 1)
        if unrolled:
            for i in range(self.iters - 1):
                for j in range(self.n):
                    turn(i, j, True)
        elif self.iters > 1:
            with act.Fori(0, self.iters - 1) as i:
                for j in range(self.n):
                    turn(i, j, True)
        for j in range(self.n):
            turn(self.iters - 1, j, j + PARTS < self.n or (j + PARTS == self.n and len(self.then) > 0))

    def low_chunk(self, pool, i, j):
        k = self.k
        s, p = j % SLOTS, j % PARTS
        pool.wait_ge(k.high_ready[p].sem, i * (self.n // PARTS) + k.high_ready[p].at(j // PARTS + 1))
        pool.tensor_tensor(k.low[:, p], k.ring[:, s], k.high[:, p].bitcast(F32), ALU.subtract)\
            .then_inc(k.low_ready[p].sem, 1)

    def split_low(self, pool, beside=None):
        if beside is not None:
            for i in range(self.iters - 1):
                for j in range(1, self.n):
                    self.low_chunk(pool, i, j)
                self.low_chunk(pool, i + 1, 0)
                beside(i)
        elif self.iters > 1:
            with pool.Fori(0, self.iters - 1) as i:
                for j in range(1, self.n):
                    self.low_chunk(pool, i, j)
                self.low_chunk(pool, i + 1, 0)
        for j in range(1, self.n):
            self.low_chunk(pool, self.iters - 1, j)
        if self.then:
            self.low_chunk(pool, self.iters, 0)
        if beside is not None:
            beside(self.iters - 1)

    def multiply(self, pe):
        with pe.Fori(0, self.iters) as i:
            self.multiply_once(pe, i)

    def multiply_once(self, pe, i):
        k = self.k
        seen = [0] * BANKS
        for j, (_, groups) in enumerate(self.chunks):
            p = j % PARTS
            pe.wait_ge(k.low_ready[p].sem, i * (self.n // PARTS) + k.low_ready[p].at(j // PARTS + 1))
            for bank, out, parts, opens, closes, before in groups:
                if opens:
                    pe.wait_ge(k.emptied[bank].sem, i * self.opened[bank] + k.emptied[bank].at(seen[bank]))
                    seen[bank] += 1
                for m, (tile, high, low) in enumerate(parts):
                    if before is not None:
                        before(pe, i, m)
                    w = slice(tile * P, (tile + 1) * P)
                    first, final = opens and m == 0, closes and m == len(parts) - 1
                    pe.matmul(out, k.high[:, p, w], high, start=first, stop=False)
                    pe.matmul(out, k.high[:, p, w], low, start=False, stop=False)
                    last = pe.matmul(out, k.low[:, p, w], high, start=False, stop=final)
            last.then_inc(k.used[p].sem, 1)

    def wait_products(self, eng, i, j):
        p = j % PARTS
        eng.wait_ge(self.k.used[p].sem, i * (self.n // PARTS) + self.k.used[p].at(j // PARTS + 1))

    def finish(self):
        for s in range(SLOTS):
            self.k.loaded[s].passed(16 * self.n // SLOTS * self.iters)
        for p in range(PARTS):
            for sem in (self.k.high_ready, self.k.low_ready, self.k.used):
                sem[p].passed(self.n // PARTS * self.iters)
        for b in range(BANKS):
            self.k.emptied[b].passed(self.opened[b] * self.iters)


def chunk_of(weights, per_iter, j):
    return lambda i: weights[bass.ds(i * per_iter + j, 1), :, :].rearrange("a p n -> p (a n)")


def plain_stream(k, weights, tiles, unroll, kin, moving):
    per = -(-kin // KD)
    chunks = []
    for t in range(unroll):
        for c in range(per):
            parts = [(x - c * KD, moving.high[:, x], moving.low[:, x]) for x in range(c * KD, min(kin, (c + 1) * KD))]
            chunks.append((chunk_of(weights, unroll * per, t * per + c),
                           [(t, k.ps[:, t], parts, c == 0, c == per - 1, None)]))
    return Stream(k, tiles // unroll, chunks)


def split_tiles(k, source, to, at=0):
    tiles = source.shape[1]
    rounded = k.tiles_rounded
    with k.nc.Block() as block:
        @block.scalar
        def _(act):
            for t in range(tiles):
                act.activation(to.high[:, at + t], source[:, t], ACT.Copy).then_inc(rounded.sem, 1)

        @block.vector
        def _(dve):
            for t in range(tiles):
                dve.wait_ge(rounded.sem, rounded.at(t + 1))
                dve.tensor_tensor(to.low[:, at + t], source[:, t], to.high[:, at + t].bitcast(F32), ALU.subtract)
    rounded.passed(tiles)


def setup(k):
    nc = k.nc
    h_in = k.dram["x"]
    first = k.heads.pop(0)
    with nc.Block() as block:
        @block.sync
        def _(sp):
            sp.dma_start(k.h[:], h_in).then_inc(k.first_ready.sem, 16)
            sp.dma_start(k.vecs[:], k.dram["vecs"]).then_inc(k.first_ready.sem, 16)
            for s, src in enumerate(first):
                sp.dma_start(k.ring[:, s], src).then_inc(k.loaded[s].sem, 16)
            sp.wait_ge(k.first_ready.sem, 32)

        @block.scalar
        def _(act):
            act.wait_ge(k.loaded[0].sem, 16)
            act.activation(k.high[:, 0], k.ring[:, 0], ACT.Copy).then_inc(k.high_ready[0].sem, 1)

        @block.tensor
        def _(pe):
            for p in range(PARTS):
                pe.sem_inc(k.used[p].sem, 1)

        @block.vector
        def _(dve):
            dve.memset(k.ones[:], 1.0)
            for b in range(BANKS):
                dve.sem_inc(k.emptied[b].sem, 1)
            for s in range(2):
                dve.sem_inc(k.ada_summed[s].sem, 1)
            dve.sem_inc(k.tile_folded.sem, 1)

        @block.gpsimd
        def _(pool):
            k.pool_steps.then(pool, pool.memset(k.ident[:], 0.0))
            k.pool_steps.then(pool, pool.affine_select(out=k.ident[:], in_=k.ident[:], compare_op=ALU.not_equal,
                                                       fill=1.0, base=0, pattern=[[-1, P]], channel_multiplier=1))
            for p in range(PARTS):
                pool.sem_inc(k.low_ready[p].sem, 2)
            pool.wait_ge(k.high_ready[0].sem, 1)
            pool.tensor_tensor(k.low[:, 0], k.ring[:, 0], k.high[:, 0].bitcast(F32), ALU.subtract)\
                .then_inc(k.low_ready[0].sem, 1)


def norm(k, gain, out, shift=None, plain=None, summed=False):
    nc = k.nc
    with ExitStack() as tmp:
        sq = k.sbuf("norm_squares", [P, KD, T], ctx=tmp)
        total = k.total
        scaled = sq if plain is None else plain

        def rest(eng, t):
            eng.wait_ge(k.rounded_ready.sem, k.rounded_ready.at(t + 1))
            eng.tensor_tensor(out.low[:, t], sq[:, t], out.high[:, t].bitcast(F32), ALU.subtract)

        with nc.Block() as block:
            @block.scalar
            def _(act):
                if not summed:
                    for t in range(KD):
                        act.activation(sq[:, t], k.h[:, t], ACT.Square).then_inc(k.squares_ready.sem, 1)
                act.wait_ge(k.mean_ready.sem, k.mean_ready.at(1))
                act.activation(k.rs[:], k.rs[:], ACT.Sqrt).then_inc(k.root_ready.sem, 1)
                if plain is None:
                    for t in range(KD):
                        act.wait_ge(k.scaled_ready.sem, k.scaled_ready.at(t + 1))
                        act.activation(out.high[:, t], sq[:, t], ACT.Copy).then_inc(k.rounded_ready.sem, 1)

            @block.tensor
            def _(pe):
                if not summed:
                    pe.wait_ge(k.folded_ready.sem, k.folded_ready.at(1))
                pe.matmul(k.ps[:, 0], k.ones[:], total[:], start=True, stop=True).then_inc(k.sumsq_ready.sem, 1)

            if plain is None:
                @block.gpsimd
                def _(pool):
                    for t in range(1, KD, 2):
                        rest(pool, t)

            @block.vector
            def _(dve):
                if not summed:
                    for t in range(1, KD):
                        dve.wait_ge(k.squares_ready.sem, k.squares_ready.at(t + 1))
                        ins = dve.tensor_tensor(total[:], sq[:, 0] if t == 1 else total[:], sq[:, t], ALU.add)
                        if t < KD - 1:
                            k.dve_steps.then(dve, ins)
                    ins.then_inc(k.folded_ready.sem, 1)
                dve.wait_ge(k.sumsq_ready.sem, k.sumsq_ready.at(1))
                dve.tensor_scalar(k.rs[:], k.ps[:, 0], 1.0 / D, EPS, ALU.mult, ALU.add).then_inc(k.mean_ready.sem, 1)
                dve.wait_ge(k.root_ready.sem, k.root_ready.at(1))
                k.dve_steps.then(dve, dve.reciprocal(k.rs[:], k.rs[:]))

                for t in range(KD):
                    ins = dve.scalar_tensor_tensor(scaled[:, t], k.h[:, t], gain[:, t:t + 1], k.rs[:],
                                                   ALU.mult, ALU.mult)
                    if shift is not None:
                        k.dve_steps.then(dve, ins)
                        ins = dve.tensor_scalar(scaled[:, t], scaled[:, t], shift[:, t:t + 1], None, ALU.add)
                    ins.then_inc(k.scaled_ready.sem, 1)
                    if plain is None and t % 2 == 1:
                        rest(dve, t - 1)
    if not summed:
        k.squares_ready.passed(KD)
        k.folded_ready.passed(1)
    k.scaled_ready.passed(KD)
    if plain is None:
        k.rounded_ready.passed(KD)
    for s in (k.sumsq_ready, k.mean_ready, k.root_ready):
        s.passed(1)


def residual(k, weights, kin, moving, scale):
    stream = plain_stream(k, weights, KD, 4, kin, moving)
    per = -(-kin // KD)
    with k.nc.Block() as block:
        @block.sync
        def _(sp):
            stream.load(sp)

        @block.gpsimd
        def _(pool):
            stream.split_low(pool)

        @block.scalar
        def _(act):
            def square(i, j):
                if j % per == per - 1:
                    t = j // per
                    act.wait_ge(k.emptied[t].sem, i + k.emptied[t].at(1))
                    act.wait_ge(k.tile_folded.sem, i * 4 + k.tile_folded.at(t))
                    act.activation(k.square[:], one(k.h, i * 4 + t), ACT.Square).then_inc(k.tile_squared.sem, 1)

            stream.scalar(act, after=square)

        @block.tensor
        def _(pe):
            stream.multiply(pe)

        @block.vector
        def _(dve):
            k.dve_steps.then(dve, dve.memset(k.total[:], 0.0))
            with dve.Fori(0, stream.iters) as i:
                for t in range(4):
                    stream.wait_products(dve, i, t * per + per - 1)
                    by = scale if isinstance(scale, float) else scale[:, bass.ds(i * 4 + t, 1)]
                    dve.scalar_tensor_tensor(one(k.h, i * 4 + t), k.ps[:, t], by, one(k.h, i * 4 + t),
                                             ALU.mult, ALU.add).then_inc(k.emptied[t].sem, 1)
                    dve.wait_ge(k.tile_squared.sem, i * 4 + k.tile_squared.at(t + 1))
                    dve.tensor_tensor(k.total[:], k.total[:], k.square[:], ALU.add).then_inc(k.tile_folded.sem, 1)
                    dve.wait_ge(k.tile_folded.sem, i * 4 + k.tile_folded.at(t + 1))
    stream.finish()
    k.tile_squared.passed(KD)
    k.tile_folded.passed(KD)


def ffn(k, name, part, gain, sig):
    nc = k.nc
    norm(k, gain, k.u, summed=part == 1)
    with ExitStack() as ctx:
        hid = Split(k, ctx, f"{name}_hid", KF)
        gated = k.sbuf(f"{name}_gated", [P, 2, T], ctx=ctx)
        product = k.sbuf(f"{name}_product", [P, 2, T], ctx=ctx)
        gated_ready, product_ready, high_ready, low_ready = sig
        stream = plain_stream(k, k.dram[f"{name}_gu"], 2 * KF, 4, KD, k.u)
        ada = Ada(k, ctx, part)
        with nc.Block() as block:
            @block.sync
            def _(sp):
                ada.start(sp)
                stream.load(sp, lambda i: ada.load(sp, i))

            @block.gpsimd
            def _(pool):
                stream.split_low(pool)

            @block.tensor
            def _(pe):
                stream.multiply(pe)

            @block.scalar
            def _(act):
                def epilogue(i, j):
                    if j % 2 == 0:
                        t = j // 2
                        stream.wait_products(act, i, j)
                        act.wait_ge(product_ready[t].sem, i + product_ready[t].at(0))
                        act.activation(gated[:, t], k.ps[:, j], ACT.Silu).then_inc(gated_ready[t].sem, 1)

                def after(i, j):
                    if j % 2 == 1:
                        t = j // 2
                        act.wait_ge(product_ready[t].sem, i + product_ready[t].at(1))
                        act.activation(one(hid.high, i * 2 + t), product[:, t], ACT.Copy)\
                           .then_inc(high_ready[t].sem, 1)

                ada.silu(act)
                stream.scalar(act, epilogue, after)

            @block.vector
            def _(dve):
                dve.wait_ge(k.cond_ready.sem, k.cond_ready.at(1))
                with dve.Fori(0, stream.iters) as i:
                    for t in range(2):
                        ada.sum(dve, i, t)
                        stream.wait_products(dve, i, 2 * t + 1)
                        dve.wait_ge(gated_ready[t].sem, i + gated_ready[t].at(1))
                        dve.wait_ge(low_ready[t].sem, i + low_ready[t].at(0))
                        dve.tensor_tensor(product[:, t], gated[:, t], k.ps[:, 2 * t + 1], ALU.mult)\
                           .then_inc(product_ready[t].sem, 1)
                        dve.wait_ge(product_ready[t].sem, i + product_ready[t].at(1))
                        dve.sem_inc(k.emptied[2 * t].sem, 1)
                        dve.sem_inc(k.emptied[2 * t + 1].sem, 1)
                        dve.wait_ge(high_ready[t].sem, i + high_ready[t].at(1))
                        dve.tensor_tensor(one(hid.low, i * 2 + t), product[:, t], one(hid.high, i * 2 + t).bitcast(F32),
                                          ALU.subtract).then_inc(low_ready[t].sem, 1)
                for t in range(2):
                    ada.sum(dve, stream.iters, t)
        stream.finish()
        ada.finish()
        for t in range(2):
            for s in (gated_ready, product_ready, high_ready, low_ready):
                s[t].passed(stream.iters)
        residual(k, k.dram[f"{name}_down"], KF, hid, 0.5)


def reduce_angle(k, dve, angle, turns, sine, cosine):
    magic = 1.5 * 2.0 ** 23
    c1 = 6.28125
    c2 = float(np.float32(TWO_PI - c1))
    c3 = float(np.float32(TWO_PI - c1 - c2))
    edge = 3.1415925
    step = lambda ins: k.dve_steps.then(dve, ins)
    step(dve.tensor_scalar(turns, angle, 1.0 / TWO_PI, None, ALU.mult))
    step(dve.tensor_scalar(turns, turns, magic, None, ALU.add))
    step(dve.tensor_scalar(turns, turns, magic, None, ALU.subtract))
    step(dve.scalar_tensor_tensor(sine, turns, -c1, angle, ALU.mult, ALU.add))
    step(dve.scalar_tensor_tensor(sine, turns, -c2, sine, ALU.mult, ALU.add))
    step(dve.scalar_tensor_tensor(sine, turns, -c3, sine, ALU.mult, ALU.add))
    step(dve.tensor_scalar(cosine, sine, np.pi / 2, None, ALU.add))
    step(dve.tensor_scalar(turns, cosine, edge, None, ALU.is_gt))
    step(dve.scalar_tensor_tensor(cosine, turns, -TWO_PI, cosine, ALU.mult, ALU.add))
    step(dve.tensor_scalar(cosine, cosine, edge, -edge, ALU.min, ALU.max))
    step(dve.tensor_scalar(sine, sine, edge, -edge, ALU.min, ALU.max))


def copy_tiles(k, weights, tiles, dst, moving, sigmoid=False):
    stream = plain_stream(k, weights, tiles, 4, KD, moving)
    with k.nc.Block() as block:
        @block.sync
        def _(sp):
            stream.load(sp)

        @block.gpsimd
        def _(pool):
            stream.split_low(pool)

        @block.tensor
        def _(pe):
            stream.multiply(pe)

        if sigmoid:
            @block.scalar
            def _(act):
                def epilogue(i, j):
                    stream.wait_products(act, i, j)
                    act.activation(one(dst, i * 4 + j), k.ps[:, j], ACT.Sigmoid).then_inc(k.emptied[j].sem, 1)

                stream.scalar(act, epilogue)
        else:
            @block.scalar
            def _(act):
                stream.scalar(act)

            @block.vector
            def _(dve):
                with dve.Fori(0, stream.iters) as i:
                    for t in range(4):
                        stream.wait_products(dve, i, t)
                        dve.tensor_copy(one(dst, i * 4 + t), k.ps[:, t]).then_inc(k.emptied[t].sem, 1)
    stream.finish()


def rope_tables(k, c, ctx):
    nc = k.nc
    with ExitStack() as tmp:
        raw = k.sbuf("pos_raw", [P, T], I32, tmp)
        turns = k.sbuf("turns", [P, T], ctx=tmp)
        posf = k.sbuf("posf", [P, T], ctx=tmp)
        loads = Signal(tmp, nc, "pos_loaded")
        reduced = Signal(tmp, nc, "angles_reduced")
        with nc.Block() as block:
            @block.sync
            def _(sp):
                sp.dma_start(raw[:], k.dram["positions"].to_broadcast((P, T))).then_inc(loads.sem, 16)
                sp.dma_start(c.cmp_pe[:], k.dram["cmp_pe"]).then_inc(c.cmp_loaded.sem, 16)
                sp.dma_start(c.cmp_w2[:], k.dram["cmp_w2"]).then_inc(c.cmp_loaded.sem, 16)
                sp.dma_start(c.cmp_w1[:], k.dram["cmp_w1"]).then_inc(c.cmp_loaded.sem, 16)

            @block.vector
            def _(dve):
                dve.wait_ge(loads.sem, 16)
                k.dve_steps.then(dve, dve.tensor_copy(posf[:], raw[:]))
                k.dve_steps.then(dve, dve.tensor_scalar(posf[:], posf[:], k.vec("freq"), None, ALU.mult))
                reduce_angle(k, dve, posf[:], turns[:], c.sin[:], c.cos[:])
                dve.sem_inc(reduced.sem, 1)

            @block.scalar
            def _(act):
                act.wait_ge(reduced.sem, 1)
                act.activation(c.sin[:], c.sin[:], ACT.Sin)
                act.activation(c.cos[:], c.cos[:], ACT.Sin)

            @block.gpsimd
            def _(pool):
                step = lambda ins: k.pool_steps.then(pool, ins)
                step(pool.memset(c.rot[:], 0.0))
                for b, fill in ((0, -1.0), (1, 1.0)):
                    view = c.rot[:].rearrange("p (a b c) -> p b a c", a=2, b=2)[:, b]
                    step(pool.affine_select(out=view, in_=view, compare_op=ALU.not_equal, fill=fill,
                                            base=-32 if b == 0 else 0, pattern=[[-64, 2], [-1, 32]],
                                            channel_multiplier=1))
                step(pool.memset(c.causal[:], 0.0))
                step(pool.memset(c.before[:], 0.0))
                step(pool.memset(c.seen[:], 0.0))
                step(pool.memset(c.some[:], 1.0))
                pool.affine_select(out=c.causal[:], in_=c.causal[:], compare_op=ALU.is_ge, fill=NEG, base=0,
                                   pattern=[[-1, P]], channel_multiplier=1)
                pool.affine_select(out=c.before[:], in_=c.before[:], compare_op=ALU.is_ge, fill=NEG, base=-1,
                                   pattern=[[1, P]], channel_multiplier=-1)
                pool.affine_select(out=c.seen[:], in_=c.seen[:], compare_op=ALU.is_ge, fill=NEG, base=-31,
                                   pattern=[[P, QT], [-16, CMP]], channel_multiplier=1)
                pool.affine_select(out=c.some[:], in_=c.some[:], compare_op=ALU.is_ge, fill=0.0, base=-31,
                                   pattern=[[P, QT]], channel_multiplier=1)


def rope(k, c, proj):
    nc = k.nc
    with ExitStack() as tmp:
        by_sin = k.sbuf("rope_by_sin", [P, 2, T], ctx=tmp)
        by_cos = k.sbuf("rope_by_cos", [P, 2, T], ctx=tmp)
        turned = Signal(tmp, nc, "halves_turned")
        sined = Signal(tmp, nc, "sine_products_ready")
        cosined = Signal(tmp, nc, "cosine_products_ready")
        roped = Signal(tmp, nc, "tile_roped")
        with nc.Block() as block:
            @block.tensor
            def _(pe):
                for t in range(ROPED):
                    if t >= 2:
                        pe.wait_ge(sined.sem, t - 1)
                    pe.matmul(k.ps[:, t % 2], c.rot[:], proj[:, t], start=True, stop=True).then_inc(turned.sem, 1)

            @block.gpsimd
            def _(pool):
                for t in range(ROPED):
                    if t >= 2:
                        pool.wait_ge(roped.sem, t - 1)
                    pool.tensor_tensor(by_cos[:, t % 2], proj[:, t], c.cos[:], ALU.mult).then_inc(cosined.sem, 1)

            @block.vector
            def _(dve):
                def add(t):
                    dve.wait_ge(sined.sem, t + 1)
                    dve.wait_ge(cosined.sem, t + 1)
                    dve.tensor_tensor(proj[:, t], by_sin[:, t % 2], by_cos[:, t % 2], ALU.add).then_inc(roped.sem, 1)

                for t in range(ROPED):
                    dve.wait_ge(turned.sem, t + 1)
                    if t >= 2:
                        dve.wait_ge(roped.sem, t - 1)
                    dve.tensor_tensor(by_sin[:, t % 2], k.ps[:, t % 2], c.sin[:], ALU.mult).then_inc(sined.sem, 1)
                    if t >= 1:
                        add(t - 1)
                add(ROPED - 1)


def compress(k, c, proj):
    nc = k.nc
    with ExitStack() as tmp:
        w1, w2, pe_k = c.cmp_w1, c.cmp_w2, c.cmp_pe
        blocks = k.sbuf("cmp_blocks", [P, 32, 2, CMP], ctx=tmp)
        hid = k.sbuf("cmp_hid", [P, 2, 2, 2 * CMP], ctx=tmp)
        part = k.sbuf("cmp_part", [P, 2, CMP], ctx=tmp)
        made = Signal(tmp, nc, "cmp_blocks_made")
        first = Signal(tmp, nc, "cmp_first_done")
        act_done = Signal(tmp, nc, "cmp_hid_ready")
        second = Signal(tmp, nc, "cmp_second_done")
        copied = Signal(tmp, nc, "cmp_keys_copied")
        turned = Signal(tmp, nc, "cmp_keys_turned")
        with nc.Block() as block:
            @block.tensor
            def _(pe):
                pe.wait_ge(c.cmp_loaded.sem, 48)
                pe.wait_ge(made.sem, 4)
                for kv in range(2):
                    rows = slice(HD * kv, HD * (kv + 1))
                    for t in range(2):
                        for l in range(32):
                            mm = pe.matmul(k.ps[:, 2 * kv + t, 0:2 * CMP], w1[rows, l, t * P:(t + 1) * P],
                                           blocks[rows, l].rearrange("p g c -> p (g c)"),
                                           start=l == 0, stop=l == 31)
                        mm.then_inc(first.sem, 1)
                pe.wait_ge(act_done.sem, 4)
                for t in range(2):
                    mm = pe.matmul(k.ps[:, 4, 0:2 * CMP], w2[:, t, 0:P], hid[:, 0, t], start=t == 0, stop=t == 1)
                mm.then_inc(second.sem, 1)
                for g in range(2):
                    for t in range(2):
                        mm = pe.matmul(k.ps[0:CMP, 5, g * HD:(g + 1) * HD], hid[:, 1, t, g * CMP:(g + 1) * CMP],
                                       w2[:, t, P:P + HD], start=t == 0, stop=t == 1)
                mm.then_inc(second.sem, 1)
                pe.wait_ge(copied.sem, 2)
                pe.matmul(k.ps[:, 6, 0:CMP], c.rot[:], c.kcmp[:], start=True, stop=True).then_inc(turned.sem, 1)

            @block.scalar
            def _(act):
                for n in range(4):
                    act.wait_ge(first.sem, n + 1)
                    act.activation(hid[:, n // 2, n % 2], k.ps[:, n, 0:2 * CMP], ACT.Gelu_apprx_tanh)\
                       .then_inc(act_done.sem, 1)

            @block.vector
            def _(dve):
                dve.wait_ge(c.cmp_loaded.sem, 48)
                for g in range(2):
                    strides = proj[:, KCA + g].rearrange("p (c l) -> p l c", l=16)
                    for half in range(2):
                        pos = pe_k[:, half * 16:(half + 1) * 16].unsqueeze(2).to_broadcast((P, 16, CMP))
                        dve.tensor_tensor(blocks[:, half * 16:(half + 1) * 16, g], strides[:, :, half:half + CMP],
                                          pos, ALU.add).then_inc(made.sem, 1)
                dve.wait_ge(second.sem, 2)
                for g in range(2):
                    rows = slice(HD * g, HD * (g + 1))
                    dve.tensor_copy(c.kcmp[rows], k.ps[rows, 4, g * CMP:(g + 1) * CMP]).then_inc(copied.sem, 1)
                dve.tensor_copy(c.vcmp[0:CMP], k.ps[0:CMP, 5, 0:P])
                dve.wait_ge(turned.sem, 1)
                last = slice(31, T, 16)
                dve.tensor_tensor(part[:, 0], k.ps[:, 6, 0:CMP], c.sin[:, last], ALU.mult)
                k.dve_steps.then(dve, dve.tensor_tensor(part[:, 1], c.kcmp[:], c.cos[:, last], ALU.mult))
                dve.tensor_tensor(c.kcmp[:], part[:, 0], part[:, 1], ALU.add)


def token_major(k, sources, dst):
    nc = k.nc
    n_banks = -(-len(sources) // 4)
    turned, copied = k.squares_turned, k.squares_copied
    with nc.Block() as block:
        @block.tensor
        def _(pe):
            for b in range(n_banks):
                if b >= BANKS:
                    pe.wait_ge(copied.sem, copied.at(b - BANKS + 1))
                for n in range(4 * b, min(4 * b + 4, len(sources))):
                    tr = pe.transpose(k.ps[:, b % BANKS, (n % 4) * P:(n % 4 + 1) * P], sources[n], k.ident[:])
                tr.then_inc(turned.sem, 1)

        @block.vector
        def _(dve):
            for b in range(n_banks):
                dve.wait_ge(turned.sem, turned.at(b + 1))
                for n in range(4 * b, min(4 * b + 4, len(sources))):
                    ins = dve.tensor_copy(dst[n], k.ps[:, b % BANKS, (n % 4) * P:(n % 4 + 1) * P])
                ins.then_inc(copied.sem, 1)
    for s in (turned, copied):
        s.passed(n_banks)


def nsa_compressed(k, c, proj, sigm, o):
    nc = k.nc
    heads = 8
    with ExitStack() as tmp:
        probs = k.sbuf("cmp_probs", [P, QT, heads, CMP], ctx=tmp)
        keyed = k.sbuf("cmp_keyed", [CMP, QT * heads, P], ctx=tmp)
        peak = k.sbuf("cmp_peak", [P, QT, heads], ctx=tmp)
        share = k.sbuf("cmp_share", [P, QT, heads], ctx=tmp)
        scored = Signal(tmp, nc, "cmp_scored")
        shifted = Signal(tmp, nc, "cmp_shifted")
        exped = Signal(tmp, nc, "cmp_exped")
        weighed = Signal(tmp, nc, "cmp_weighed")
        turned = Signal(tmp, nc, "cmp_turned")
        copied_a = Signal(tmp, nc, "cmp_copied_by_act")
        copied_v = Signal(tmp, nc, "cmp_copied_by_dve")
        mixed = Signal(tmp, nc, "cmp_mixed")
        group = lambda h: slice(HD * (h // 4), HD * (h // 4 + 1))
        four = lambda n: k.ps[0:CMP, n].rearrange("p (h q) -> p h q", h=4)
        with nc.Block() as block:
            @block.tensor
            def _(pe):
                for qt in range(QT):
                    for h in range(heads):
                        mm = pe.matmul(k.ps[:, 2 * qt + h // 4, (h % 4) * CMP:(h % 4 + 1) * CMP], proj[group(h), Q0 + h % 4, qt * P:(qt + 1) * P],
                                       c.kcmp[group(h)], start=True, stop=True)
                        if h % 4 == 3:
                            mm.then_inc(scored.sem, 1)
                pe.wait_ge(weighed.sem, 1)
                for n in range(2 * QT):
                    for h in range(4):
                        tr = pe.transpose(four(n)[:, h], probs[:, n // 2, 4 * (n % 2) + h], k.ident[:])
                    tr.then_inc(turned.sem, 1)
                for qt in range(QT):
                    pe.wait_ge(copied_a.sem, qt + 1)
                    pe.wait_ge(copied_v.sem, qt + 1)
                    for h in range(heads):
                        mm = pe.matmul(k.ps[:, qt, h * HD:(h + 1) * HD], keyed[:, qt * heads + h], c.vcmp[0:CMP, group(h)],
                                       start=True, stop=True)
                    mm.then_inc(mixed.sem, 1)

            @block.scalar
            def _(act):
                act.wait_ge(shifted.sem, 1)
                act.activation(probs[:], probs[:], ACT.Exp, scale=SCALE).then_inc(exped.sem, 1)
                for qt in range(QT):
                    act.wait_ge(turned.sem, 2 * qt + 1)
                    act.activation(keyed[:, qt * heads:qt * heads + 4], four(2 * qt), ACT.Copy).then_inc(copied_a.sem, 1)

            @block.vector
            def _(dve):
                step = lambda ins: k.dve_steps.then(dve, ins)
                every = lambda small: small[:].unsqueeze(3).to_broadcast((P, QT, heads, CMP))
                dve.wait_ge(scored.sem, 2 * QT)
                for g in range(2):
                    mine = k.ps[:, :, 0:4 * CMP].rearrange("p (q g) (h n) -> p q g h n", g=2, h=4)[:, :, g]
                    step(dve.tensor_tensor(probs[:, :, 4 * g:4 * g + 4], mine,
                                           c.seen[:].unsqueeze(2).to_broadcast((P, QT, 4, CMP)), ALU.add))
                step(dve.tensor_reduce(peak[:], probs[:], AX.X, ALU.max))
                dve.tensor_tensor(probs[:], probs[:], every(peak), ALU.subtract).then_inc(shifted.sem, 1)
                dve.wait_ge(exped.sem, 1)
                step(dve.tensor_reduce(share[:], probs[:], AX.X, ALU.add))
                step(dve.reciprocal(share[:], share[:]))
                step(dve.tensor_tensor(share[:], share[:], sigm[:, :, 0:heads], ALU.mult))
                step(dve.tensor_tensor(share[:], share[:], c.some[:].unsqueeze(2).to_broadcast((P, QT, heads)), ALU.mult))
                dve.tensor_tensor(probs[:], probs[:], every(share), ALU.mult).then_inc(weighed.sem, 1)
                for qt in range(QT):
                    dve.wait_ge(turned.sem, 2 * qt + 2)
                    dve.tensor_copy(keyed[:, qt * heads + 4:(qt + 1) * heads], four(2 * qt + 1)).then_inc(copied_v.sem, 1)
                for qt in range(QT):
                    dve.wait_ge(mixed.sem, qt + 1)
                    dve.tensor_copy(o[:, qt], k.ps[:, qt])


def nsa(k, c, proj, vtok, o):
    nc = k.nc
    units = [(qt, j, g) for qt in range(QT) for j in range(4) for g in range(2)]
    with ExitStack() as tmp:
        sigm = k.sbuf("nsa_gates", [P, QT, 24], ctx=tmp)
        with nc.Block() as block:
            @block.scalar
            def _(act):
                act.activation(sigm[:], vtok[:, 2, :, HD:HD + 24], ACT.Sigmoid)
        nsa_compressed(k, c, proj, sigm, o)
        probs = k.sbuf("nsa_probs", [P, 2, 2, T], ctx=tmp)
        keyed = k.sbuf("nsa_keyed", [P, 2, 8, P], ctx=tmp)
        peak = k.sbuf("nsa_peak", [P, 2, 2], ctx=tmp)
        sums = k.sbuf("nsa_sums", [P, 3, 2], ctx=tmp)
        share = k.sbuf("nsa_share", [P, 2], ctx=tmp)
        scored = Signal(tmp, nc, "nsa_scored")
        peaked = Signal(tmp, nc, "nsa_peaked")
        exped = Signal(tmp, nc, "nsa_exped")
        turned = Signal(tmp, nc, "nsa_turned")
        copied_a = Signal(tmp, nc, "nsa_copied_by_act")
        copied_v = Signal(tmp, nc, "nsa_copied_by_dve")
        mixed = Signal(tmp, nc, "nsa_mixed")
        summed = Signal(tmp, nc, "nsa_summed")
        with nc.Block() as block:
            @block.tensor
            def _(pe):
                def score(n):
                    qt, j, g = units[n]
                    rows, keys = slice(HD * g, HD * (g + 1)), (qt + 1) * P
                    q = proj[rows, Q0 + j, qt * P:(qt + 1) * P]
                    b = n % 2
                    if n >= 2:
                        pe.wait_ge(exped.sem, n - 1)
                    pe.matmul(k.ps[:, 2 * b, 0:keys], q, proj[rows, KSL, 0:keys], start=True, stop=True)
                    pe.matmul(k.ps[:, 2 * b + 1, 0:keys], q, proj[rows, KWN, 0:keys], start=True, stop=True)\
                      .then_inc(scored.sem, 1)

                score(0)
                score(1)
                for n, (qt, j, g) in enumerate(units):
                    b = n % 2
                    pe.wait_ge(exped.sem, n + 1)
                    if n >= 1:
                        pe.wait_ge(copied_a.sem, n)
                        pe.wait_ge(copied_v.sem, n)
                    for kind in range(2):
                        for kb in range(qt + 1):
                            tr = pe.transpose(k.ps[:, 4 + kind, kb * P:(kb + 1) * P],
                                              probs[:, b, kind, kb * P:(kb + 1) * P], k.ident[:])
                        tr.then_inc(turned.sem, 1)
                    if n + 2 < len(units):
                        score(n + 2)
                    if n >= 2:
                        pe.wait_ge(summed.sem, n - 1)
                    for kind, copied in enumerate((copied_a, copied_v)):
                        pe.wait_ge(copied.sem, n + 1)
                        for kb in range(qt + 1):
                            mm = pe.matmul(k.ps[:, 6 + b, kind * HD:(kind + 1) * HD], keyed[:, b, 4 * kind + kb],
                                           vtok[:, kind, kb, HD * g:HD * (g + 1)], start=kb == 0, stop=kb == qt)
                    mm.then_inc(mixed.sem, 1)

            @block.scalar
            def _(act):
                def weigh(n):
                    b, keys = n % 2, (units[n][0] + 1) * P
                    act.wait_ge(peaked.sem, n + 1)
                    if n >= 2:
                        act.wait_ge(turned.sem, 2 * (n - 1))
                    if n >= 3:
                        act.wait_ge(summed.sem, n - 2)
                    for kind in range(2):
                        ins = act.activation(probs[:, b, kind, 0:keys], k.ps[:, 2 * b + kind, 0:keys], ACT.Exp,
                                             bias=peak[:, b, kind:kind + 1], scale=SCALE,
                                             accum_out=sums[:, n % 3, kind:kind + 1])
                    ins.then_inc(exped.sem, 1)

                weigh(0)
                for n, (qt, j, g) in enumerate(units):
                    b = n % 2
                    act.wait_ge(turned.sem, 2 * n + 1)
                    if n >= 2:
                        act.wait_ge(mixed.sem, n - 1)
                    act.activation(keyed[:, b, 0:qt + 1], k.ps[:, 4, 0:(qt + 1) * P].rearrange("p (a n) -> p a n", n=P),
                                   ACT.Copy).then_inc(copied_a.sem, 1)
                    if n + 1 < len(units):
                        weigh(n + 1)

            @block.vector
            def _(dve):
                def peaks(n):
                    qt, b = units[n][0], n % 2
                    own, keys = slice(qt * P, (qt + 1) * P), (qt + 1) * P
                    dve.wait_ge(scored.sem, n + 1)
                    both = k.ps[:, 2 * b:2 * b + 2, own]
                    k.dve_steps.then(dve, dve.tensor_tensor(both, both, c.causal[:].unsqueeze(1).to_broadcast((P, 2, P)),
                                                            ALU.add))
                    if n >= 2:
                        dve.wait_ge(exped.sem, n - 1)
                    k.dve_steps.then(dve, dve.tensor_reduce(peak[:, b], k.ps[:, 2 * b:2 * b + 2, 0:keys], AX.X, ALU.max))
                    dve.tensor_scalar(peak[:, b], peak[:, b], -SCALE, None, ALU.mult).then_inc(peaked.sem, 1)

                def finish(n):
                    qt, j, g = units[n]
                    b, head = n % 2, 4 * g + j
                    k.dve_steps.then(dve, dve.reciprocal(share[:], sums[:, n % 3]))
                    gate = sigm[:, qt].rearrange("p (b h) -> p b h", b=3)
                    k.dve_steps.then(dve, dve.tensor_tensor(share[:], share[:], gate[:, 1:3, head], ALU.mult))
                    dve.wait_ge(mixed.sem, n + 1)
                    mine = o[:, qt, HD * head:HD * (head + 1)]
                    k.dve_steps.then(dve, dve.scalar_tensor_tensor(mine, k.ps[:, 6 + b, 0:HD], share[:, 0:1], mine,
                                                                   ALU.mult, ALU.add))
                    dve.scalar_tensor_tensor(mine, k.ps[:, 6 + b, HD:2 * HD], share[:, 1:2], mine,
                                             ALU.mult, ALU.add).then_inc(summed.sem, 1)
                    dve.wait_ge(summed.sem, n + 1)

                peaks(0)
                peaks(1)
                for n, (qt, j, g) in enumerate(units):
                    b = n % 2
                    dve.wait_ge(turned.sem, 2 * n + 2)
                    if n >= 2:
                        dve.wait_ge(mixed.sem, n - 1)
                    dve.tensor_copy(keyed[:, b, 4:5 + qt], k.ps[:, 5, 0:(qt + 1) * P].rearrange("p (a n) -> p a n", n=P))\
                       .then_inc(copied_v.sem, 1)
                    if n + 2 < len(units):
                        peaks(n + 2)
                    if n >= 1:
                        finish(n - 1)
                finish(len(units) - 1)


def swa(k, c, proj, vtok, o):
    nc = k.nc
    units = [(qt, j, g) for qt in range(QT) for j in range(4) for g in range(2)]
    with ExitStack() as tmp:
        probs = k.sbuf("swa_probs", [P, 2, 2 * P], ctx=tmp)
        keyed = k.sbuf("swa_keyed", [P, 2, 2, P], ctx=tmp)
        peak = k.sbuf("swa_peak", [P, 2], ctx=tmp)
        sums = k.sbuf("swa_sums", [P, 3, 2], ctx=tmp)
        share = k.sbuf("swa_share", [P, 1], ctx=tmp)
        scored = Signal(tmp, nc, "swa_scored")
        peaked = Signal(tmp, nc, "swa_peaked")
        exped = Signal(tmp, nc, "swa_exped")
        turned = Signal(tmp, nc, "swa_turned")
        copied = Signal(tmp, nc, "swa_copied")
        mixed = Signal(tmp, nc, "swa_mixed")
        summed = Signal(tmp, nc, "swa_summed")
        with nc.Block() as block:
            @block.tensor
            def _(pe):
                def score(n):
                    qt, j, g = units[n]
                    rows, lo = slice(HD * g, HD * (g + 1)), max(qt - 1, 0) * P
                    if n >= 2:
                        pe.wait_ge(exped.sem, n - 1)
                    pe.matmul(k.ps[:, n % 2, 0:(qt + 1) * P - lo], proj[rows, SQ0 + j, qt * P:(qt + 1) * P],
                              proj[rows, SK, lo:(qt + 1) * P], start=True, stop=True).then_inc(scored.sem, 1)

                score(0)
                score(1)
                for n, (qt, j, g) in enumerate(units):
                    b, blocks = n % 2, min(qt, 1) + 1
                    pe.wait_ge(exped.sem, n + 1)
                    if n >= 2:
                        pe.wait_ge(copied.sem, n - 1)
                    for m in range(blocks):
                        tr = pe.transpose(k.ps[:, 2 + b, m * P:(m + 1) * P], probs[:, b, m * P:(m + 1) * P], k.ident[:])
                    tr.then_inc(turned.sem, 1)
                    if n + 2 < len(units):
                        score(n + 2)
                    pe.wait_ge(copied.sem, n + 1)
                    if n >= 2:
                        pe.wait_ge(summed.sem, n - 1)
                    for m in range(blocks):
                        mm = pe.matmul(k.ps[:, 4 + b, 0:HD], keyed[:, b, m], vtok[:, 2, qt - blocks + 1 + m, 0:HD],
                                       start=m == 0, stop=m == blocks - 1)
                    mm.then_inc(mixed.sem, 1)

            @block.scalar
            def _(act):
                def weigh(n):
                    qt, j, g = units[n]
                    b, head, width = n % 2, 4 * g + j, (min(qt, 1) + 1) * P
                    act.wait_ge(peaked.sem, n + 1)
                    if n >= 2:
                        act.wait_ge(turned.sem, n - 1)
                    if n >= 3:
                        act.wait_ge(summed.sem, n - 2)
                    act.activation(probs[:, b, 0:width], k.ps[:, b, 0:width], ACT.Exp, bias=peak[:, b:b + 1],
                                   scale=SCALE, accum_out=sums[:, n % 3, 0:1])
                    act.activation(sums[:, n % 3, 1:2], k.vec("sinks")[:, head:head + 1], ACT.Exp,
                                   bias=peak[:, b:b + 1]).then_inc(exped.sem, 1)

                weigh(0)
                for n, (qt, j, g) in enumerate(units):
                    b, width = n % 2, (min(qt, 1) + 1) * P
                    act.wait_ge(turned.sem, n + 1)
                    if n >= 2:
                        act.wait_ge(mixed.sem, n - 1)
                    act.activation(keyed[:, b, 0:width // P], k.ps[:, 2 + b, 0:width].rearrange("p (a n) -> p a n", n=P),
                                   ACT.Copy).then_inc(copied.sem, 1)
                    if n + 1 < len(units):
                        weigh(n + 1)

            @block.vector
            def _(dve):
                def peaks(n):
                    qt, j, g = units[n]
                    b, head, blocks = n % 2, 4 * g + j, min(qt, 1) + 1
                    dve.wait_ge(scored.sem, n + 1)
                    if blocks == 2:
                        dve.tensor_tensor(k.ps[:, b, 0:P], k.ps[:, b, 0:P], c.before[:], ALU.add)
                    own = k.ps[:, b, (blocks - 1) * P:blocks * P]
                    k.dve_steps.then(dve, dve.tensor_tensor(own, own, c.causal[:], ALU.add))
                    if n >= 2:
                        dve.wait_ge(exped.sem, n - 1)
                    k.dve_steps.then(dve, dve.tensor_reduce(peak[:, b:b + 1], k.ps[:, b, 0:blocks * P], AX.X, ALU.max))
                    k.dve_steps.then(dve, dve.scalar_tensor_tensor(peak[:, b:b + 1], peak[:, b:b + 1], SCALE,
                                                                   k.vec("sinks")[:, head:head + 1], ALU.mult, ALU.max))
                    dve.tensor_scalar(peak[:, b:b + 1], peak[:, b:b + 1], -1.0, None, ALU.mult)\
                       .then_inc(peaked.sem, 1)

                def finish(n):
                    qt, j, g = units[n]
                    b, head, both = n % 2, 4 * g + j, sums[:, n % 3]
                    k.dve_steps.then(dve, dve.tensor_tensor(share[:], both[:, 0:1], both[:, 1:2], ALU.add))
                    k.dve_steps.then(dve, dve.reciprocal(share[:], share[:]))
                    dve.wait_ge(mixed.sem, n + 1)
                    dve.tensor_scalar(o[:, qt, HD * head:HD * (head + 1)], k.ps[:, 4 + b, 0:HD], share[:], None,
                                      ALU.mult).then_inc(summed.sem, 1)
                    dve.wait_ge(summed.sem, n + 1)

                peaks(0)
                peaks(1)
                for n in range(len(units)):
                    dve.wait_ge(exped.sem, n + 1)
                    if n + 2 < len(units):
                        peaks(n + 2)
                    if n >= 1:
                        finish(n - 1)
                finish(len(units) - 1)


def branches(k, weights, gates, o, merged):
    nc = k.nc
    chunks = []
    for t in range(4):
        groups = [(t, k.ps[:, t], [(x, o.high[:, x], o.low[:, x]) for x in range(4)], True, True, None),
                  (4 + t, k.ps[:, 4 + t], [(x, o.high[:, x], o.low[:, x]) for x in range(4, 8)], True, True, None)]
        chunks.append((chunk_of(weights, 4, t), groups))
    stream = Stream(k, KD // 4, chunks)
    with ExitStack() as tmp:
        part = k.sbuf("branch_part", [P, 2, T], ctx=tmp)
        added = Signal(tmp, nc, "branch_added")
        with nc.Block() as block:
            @block.sync
            def _(sp):
                stream.load(sp)

            @block.gpsimd
            def _(pool):
                stream.split_low(pool)

            @block.tensor
            def _(pe):
                stream.multiply(pe)

            @block.scalar
            def _(act):
                stream.scalar(act)

            @block.vector
            def _(dve):
                with dve.Fori(0, stream.iters) as i:
                    for t in range(4):
                        stream.wait_products(dve, i, t)
                        dve.tensor_tensor(part[:, 0], one(gates, i * 4 + t), k.ps[:, t], ALU.mult)\
                           .then_inc(k.emptied[t].sem, 1)
                        dve.tensor_tensor(part[:, 1], one(gates, i * 4 + (KD + t)), k.ps[:, 4 + t], ALU.mult)\
                           .then_inc(k.emptied[4 + t].sem, 1)
                        dve.wait_ge(k.emptied[t].sem, i + k.emptied[t].at(1))
                        dve.wait_ge(k.emptied[4 + t].sem, i + k.emptied[4 + t].at(1))
                        dve.tensor_tensor(one(merged, i * 4 + t), part[:, 0], part[:, 1], ALU.add)\
                           .then_inc(added.sem, 1)
                        dve.wait_ge(added.sem, i * 4 + (t + 1))
        stream.finish()


class Mixer1:
    pass


def mixer1(k):
    nc = k.nc
    norm(k, k.vec("norm_mix"), k.u, summed=True)
    with ExitStack() as ctx:
        c = Mixer1()
        o_t = k.sbuf("o_t", [P, KD, T], ctx=ctx)
        with ExitStack() as inner:
            proj = k.sbuf("proj", [P, PROJ, T], ctx=inner)
            c.cos = k.sbuf("cos", [P, T], ctx=inner)
            c.sin = k.sbuf("sin", [P, T], ctx=inner)
            c.rot = k.sbuf("rot", [P, P], ctx=inner)
            c.causal = k.sbuf("causal", [P, P], ctx=inner)
            c.before = k.sbuf("before", [P, P], ctx=inner)
            c.seen = k.sbuf("seen", [P, QT, CMP], ctx=inner)
            c.some = k.sbuf("some", [P, QT], ctx=inner)
            c.kcmp = k.sbuf("kcmp", [P, CMP], ctx=inner)
            c.vcmp = k.sbuf("vcmp", [P, P], ctx=inner)
            copy_tiles(k, k.dram["w_in"], PROJ, proj, k.u)
            with ExitStack() as early:
                c.cmp_w1 = k.sbuf("cmp_w1", [P, 32, 256], ctx=early)
                c.cmp_w2 = k.sbuf("cmp_w2", [P, 2, 192], ctx=early)
                c.cmp_pe = k.sbuf("cmp_pe", [P, 32], ctx=early)
                c.cmp_loaded = Signal(early, nc, "cmp_loaded")
                rope_tables(k, c, inner)
                rope(k, c, proj)
                compress(k, c, proj)
            vtok = k.sbuf("vtok", [P, 3, QT, P], ctx=inner)
            token_major(k, [proj[:, t, b * P:(b + 1) * P] for t in (VSL, VWN, SVG) for b in range(QT)],
                        [vtok[:, n, b] for n in range(3) for b in range(QT)])
            with ExitStack() as deep:
                oa = k.sbuf("oa", [P, QT, 512], ctx=deep)
                ob = k.sbuf("ob", [P, QT, 512], ctx=deep)
                nsa(k, c, proj, vtok, oa)
                swa(k, c, proj, vtok, ob)
                token_major(k,
                            [s[:, q, f * P:(f + 1) * P] for s in (oa, ob) for f in range(4) for q in range(QT)],
                            [d[:, f, q * P:(q + 1) * P] for d in (o_t[:, 0:4], o_t[:, 4:8]) for f in range(4) for q in range(QT)])
        gates = k.sbuf("branch_gates", [P, 2 * KD, T], ctx=ctx)
        copy_tiles(k, k.dram["w_in_gates"], 2 * KD, gates, k.u, sigmoid=True)
        split_tiles(k, o_t, k.u)
        branches(k, k.dram["w_branch"], gates, k.u, o_t)
        split_tiles(k, o_t, k.u)
        residual(k, k.dram["w_out"], KD, k.u, 1.0)


CHUNK = 16
NCH = T // CHUNK
HEADS2 = 4
LANES = HEADS2 * NCH
S5T = 16


def modulation(k, gain):
    with k.nc.Block() as block:
        @block.vector
        def _(dve):
            for n, (name, scale) in enumerate((("norm_mix_w_2", 1), ("norm_ffn_w_2", 4))):
                dve.scalar_tensor_tensor(gain[:, n], k.mod[:, scale * KD:(scale + 1) * KD], 1.0, k.vec(name), ALU.add, ALU.mult)


def hgrn(k, proj, out):
    nc = k.nc
    Q, F, V, G = 0, 4, 8, 12
    lanes = lambda ap: ap.rearrange("p h (c j) -> p (h c) j", j=CHUNK)
    heads = lambda ap: ap.rearrange("p h (c j) -> p h c j", j=CHUNK)
    with ExitStack() as outer:
        f = k.sbuf("hg_f", [P, HEADS2, T], ctx=outer)
        key = k.sbuf("hg_key", [P, HEADS2, T], ctx=outer)
        start = k.sbuf("hg_start", [P, HEADS2, T], ctx=outer)
        q = proj[:, Q:Q + 4]
        with ExitStack() as tmp:
            lb = k.sbuf("hg_lb", [P, 3, HEADS2], ctx=tmp)
            lb_ready = Signal(tmp, nc, "hg_lb_ready")
            sig_ready = Signal(tmp, nc, "hg_sigmoid_ready")
            with nc.Block() as block:
                @block.scalar
                def _(act):
                    act.activation(q, q, ACT.Silu).then_inc(sig_ready.sem, 1)
                    act.activation(proj[:, G:G + 4], proj[:, G:G + 4], ACT.Silu).then_inc(sig_ready.sem, 1)
                    act.activation(f[:], proj[:, F:F + 4], ACT.Sigmoid).then_inc(sig_ready.sem, 1)
                    act.wait_ge(lb_ready.sem, 1)
                    act.activation(lb[:, 0:2], lb[:, 0:2], ACT.Exp).then_inc(sig_ready.sem, 1)

                @block.vector
                def _(dve):
                    step = lambda ins: k.dve_steps.then(dve, ins)
                    step(dve.tensor_tensor(lb[:, 2], k.vec("lb0"), k.vec("lb1"), ALU.max))
                    step(dve.tensor_tensor(lb[:, 0], k.vec("lb0"), lb[:, 2], ALU.subtract))
                    dve.tensor_tensor(lb[:, 1], k.vec("lb1"), lb[:, 2], ALU.subtract).then_inc(lb_ready.sem, 1)
                    dve.wait_ge(sig_ready.sem, 4)
                    step(dve.tensor_tensor(lb[:, 1], lb[:, 0], lb[:, 1], ALU.add))
                    step(dve.reciprocal(lb[:, 1], lb[:, 1]))
                    step(dve.tensor_tensor(lb[:, 0], lb[:, 0], lb[:, 1], ALU.mult))
                    step(dve.tensor_scalar(lb[:, 1], lb[:, 0], -1.0, 1.0, ALU.mult, ALU.add))
                    for h in range(HEADS2):
                        ins = dve.tensor_scalar(f[:, h], f[:, h], lb[:, 1, h:h + 1], lb[:, 0, h:h + 1],
                                                ALU.mult, ALU.add)
                    step(ins)
                    step(dve.tensor_scalar(key[:], f[:], -1.0, 1.0, ALU.mult, ALU.add))
                    step(dve.tensor_scalar(q, q, float(P) ** -0.5, None, ALU.mult))
                    sl, fl = lanes(start), lanes(f)
                    step(dve.tensor_copy(sl[:, :, 0:1], fl[:, :, 0:1]))
                    for j in range(1, CHUNK):
                        step(dve.tensor_tensor(sl[:, :, j:j + 1], sl[:, :, j - 1:j], fl[:, :, j:j + 1], ALU.mult))
        hgrn_within(k, lanes, heads, q, f, key, proj[:, V:V + 4], out)
        hgrn_across(k, lanes, q, f, key, start, proj[:, V:V + 4], out)
    hgrn_finish(k, proj[:, G:G + 4], out)


def hgrn_within(k, lanes, heads, q, f, key, v, out):
    nc = k.nc
    with ExitStack() as tmp:
        qf = k.sbuf("hg_qf", [P, LANES, CHUNK], ctx=tmp)
        qk = k.sbuf("hg_qk", [P, 2, LANES * CHUNK], ctx=tmp)
        sv = k.sbuf("hg_sv", [P, HEADS2 * NCH * CHUNK], ctx=tmp)
        decayed = Signal(tmp, nc, "hg_query_decayed")
        paired = Signal(tmp, nc, "hg_pairs_ready")
        scored = Signal(tmp, nc, "hg_lag_scored")
        with nc.Block() as block:
            @block.gpsimd
            def _(pool):
                fl = lanes(f)
                for lag in range(1, CHUNK):
                    if lag == 1:
                        ins = pool.tensor_tensor(qf[:, :, 1:], lanes(q)[:, :, 1:], fl[:, :, 1:], ALU.mult)
                    else:
                        pool.wait_ge(decayed.sem, lag - 1)
                        pool.wait_ge(paired.sem, lag)
                        ins = pool.tensor_tensor(qf[:, :, lag:], qf[:, :, lag:], fl[:, :, 1:CHUNK - lag + 1], ALU.mult)
                    ins.then_inc(decayed.sem, 1)

            @block.tensor
            def _(pe):
                for lag in range(CHUNK):
                    w = (CHUNK - lag) * NCH
                    pe.wait_ge(paired.sem, lag + 1)
                    for h in range(HEADS2):
                        mm = pe.matmul(k.ps[:, 4 * (lag % 2) + h, 0:w], k.ones[:],
                                       qk[:, lag % 2, h * w:(h + 1) * w], start=True, stop=True)
                    mm.then_inc(scored.sem, 1)

            @block.vector
            def _(dve):
                kl = lanes(key)

                def pairs(lag):
                    w = CHUNK - lag
                    dst = qk[:, lag % 2, 0:LANES * w].rearrange("p (l j) -> p l j", j=w)
                    if lag >= 1:
                        dve.wait_ge(decayed.sem, lag)
                    if lag >= 2:
                        dve.wait_ge(scored.sem, lag - 1)
                    source = lanes(q) if lag == 0 else qf[:, :, lag:]
                    dve.tensor_tensor(dst, source, kl[:, :, 0:w], ALU.mult).then_inc(paired.sem, 1)

                pairs(0)
                for lag in range(CHUNK):
                    w = CHUNK - lag
                    if lag + 1 < CHUNK:
                        pairs(lag + 1)
                    dve.wait_ge(scored.sem, lag + 1)
                    score = k.ps[:, 4 * (lag % 2):4 * (lag % 2) + 4, 0:NCH * w].rearrange("p h (c j) -> p h c j", j=w)
                    if lag == 0:
                        k.dve_steps.then(dve, dve.tensor_tensor(heads(out), score, heads(v), ALU.mult))
                        continue
                    part = sv[:, 0:HEADS2 * NCH * w].rearrange("p (h c j) -> p h c j", h=HEADS2, j=w)
                    k.dve_steps.then(dve, dve.tensor_tensor(part, score, heads(v)[:, :, :, 0:w], ALU.mult))
                    flat = sv[:, 0:LANES * w].rearrange("p (l j) -> p l j", j=w)
                    k.dve_steps.then(dve, dve.tensor_tensor(lanes(out)[:, :, lag:], lanes(out)[:, :, lag:], flat, ALU.add))


def hgrn_across(k, lanes, q, f, key, start, v, out):
    nc = k.nc
    per = T // (HEADS2 * CHUNK)
    own = P // CHUNK
    with ExitStack() as tmp:
        rest = k.sbuf("hg_rest", [P, HEADS2, T], ctx=tmp)
        ktok = k.sbuf("hg_ktok", [P, 2, HEADS2 * P], ctx=tmp)
        vtok = k.sbuf("hg_vtok", [P, 2, HEADS2 * P], ctx=tmp)
        state = k.sbuf("hg_state", [P, 2, HEADS2, P], ctx=tmp)
        inside = k.sbuf("hg_inside", [P, own], ctx=tmp)
        marked = Signal(tmp, nc, "hg_marked")
        prepared = Signal(tmp, nc, "hg_prepared")
        turned = Signal(tmp, nc, "hg_turned")
        copied = Signal(tmp, nc, "hg_copied")
        multiplied = Signal(tmp, nc, "hg_outer_ready")
        stated = Signal(tmp, nc, "hg_state_ready")
        read = Signal(tmp, nc, "hg_state_read")
        gathered = Signal(tmp, nc, "hg_gathered")
        with nc.Block() as block:
            @block.gpsimd
            def _(pool):
                k.pool_steps.then(pool, pool.memset(inside[:], 1.0))
                k.pool_steps.then(pool, pool.affine_select(out=inside[:], in_=inside[:], compare_op=ALU.is_ge, fill=0.0,
                                                           base=0, pattern=[[-CHUNK, own]], channel_multiplier=1))
                pool.affine_select(out=inside[:], in_=inside[:], compare_op=ALU.is_ge, fill=0.0, base=CHUNK - 1,
                                   pattern=[[CHUNK, own]], channel_multiplier=-1).then_inc(marked.sem, 1)

            @block.tensor
            def _(pe):
                def turn(t):
                    if t >= 2:
                        pe.wait_ge(copied.sem, own * (t - 1))
                    mine = slice(t * P, (t + 1) * P)
                    for h in range(HEADS2):
                        pe.transpose(k.ps[:, t % 2, h * P:(h + 1) * P], key[:, h, mine], k.ident[:])
                        tr = pe.transpose(k.ps[:, 2 + t % 2, h * P:(h + 1) * P], v[:, h, mine], k.ident[:])
                    tr.then_inc(turned.sem, 1)

                def outer(c):
                    pe.wait_ge(copied.sem, c + 1)
                    if c >= 2:
                        pe.wait_ge(stated.sem, c - 1)
                    for h in range(HEADS2):
                        mm = pe.matmul(k.ps[:, 4 + c % 2, h * P:(h + 1) * P], ktok[:, c % 2, h * P:(h + 1) * P],
                                       vtok[:, c // own % 2, h * P:(h + 1) * P], start=True, stop=True)
                    mm.then_inc(multiplied.sem, 1)

                pe.wait_ge(prepared.sem, 1)
                turn(0)
                outer(0)
                for c in range(NCH - 1):
                    if c % own == own // 2 and c // own + 1 < QT:
                        turn(c // own + 1)
                    if c + 1 < NCH - 1:
                        outer(c + 1)
                    n = c + 1
                    pe.wait_ge(stated.sem, n)
                    if n // per >= 2 and n % per == 0:
                        pe.wait_ge(gathered.sem, n // per - 1)
                    for h in range(HEADS2):
                        at = (h * per + n % per) * CHUNK
                        mm = pe.matmul(k.ps[:, 6 + (n // per) % 2, at:at + CHUNK], state[:, c % 2, h],
                                       q[:, h, n * CHUNK:(n + 1) * CHUNK], start=True, stop=True)
                    mm.then_inc(read.sem, 1)

            @block.scalar
            def _(act):
                act.wait_ge(marked.sem, 1)
                for c in range(NCH - 1):
                    t = c // own
                    if c % own == 0:
                        act.wait_ge(turned.sem, t + 1)
                        if t >= 2:
                            act.wait_ge(multiplied.sem, own * (t - 1))
                        act.activation(vtok[:, t % 2], k.ps[:, 2 + t % 2], ACT.Copy)
                    if c >= 2:
                        act.wait_ge(multiplied.sem, c - 1)
                    act.activation(ktok[:, c % 2], k.ps[:, t % 2], ACT.Copy, scale=inside[:, c % own:c % own + 1])\
                       .then_inc(copied.sem, 1)

            @block.vector
            def _(dve):
                step = lambda ins: k.dve_steps.then(dve, ins)
                rl, fl = lanes(rest), lanes(f)
                step(dve.memset(rl[:, :, CHUNK - 1:], 1.0))
                for j in range(CHUNK - 2, -1, -1):
                    step(dve.tensor_tensor(rl[:, :, j:j + 1], rl[:, :, j + 1:j + 2], fl[:, :, j + 1:j + 2], ALU.mult))
                step(dve.tensor_tensor(key[:], key[:], rest[:], ALU.mult))
                dve.tensor_tensor(q, q, start[:], ALU.mult).then_inc(prepared.sem, 1)
                for c in range(NCH):
                    if c < NCH - 1:
                        dve.wait_ge(multiplied.sem, c + 1)
                        if c >= 2:
                            dve.wait_ge(read.sem, c - 1)
                        if c == 0:
                            ins = dve.tensor_copy(state[:, 0], k.ps[:, 4].rearrange("p (h n) -> p h n", h=HEADS2))
                        else:
                            for h in range(HEADS2):
                                last = (c + 1) * CHUNK - 1
                                ins = dve.scalar_tensor_tensor(state[:, c % 2, h], state[:, (c - 1) % 2, h],
                                                               start[:, h, last:last + 1],
                                                               k.ps[:, 4 + c % 2, h * P:(h + 1) * P], ALU.mult, ALU.add)
                        ins.then_inc(stated.sem, 1)
                        dve.wait_ge(stated.sem, c + 1)
                    if c % per == per - 1:
                        b = c // per
                        lo = 1 if b == 0 else 0
                        dve.wait_ge(read.sem, c)
                        mine = out[:, :, (b * per + lo) * CHUNK:(b + 1) * per * CHUNK]
                        got = k.ps[:, 6 + b % 2].rearrange("p (h n) -> p h n", h=HEADS2)[:, :, lo * CHUNK:]
                        dve.tensor_tensor(mine, mine, got, ALU.add).then_inc(gathered.sem, 1)


def hgrn_finish(k, gate, out):
    nc = k.nc
    with ExitStack() as tmp:
        sq = k.sbuf("hg_sq", [P, HEADS2, T], ctx=tmp)
        squared = Signal(tmp, nc, "hg_squared")
        summed = Signal(tmp, nc, "hg_squares_summed")
        mean = Signal(tmp, nc, "hg_mean_ready")
        root = Signal(tmp, nc, "hg_root_ready")
        with nc.Block() as block:
            @block.scalar
            def _(act):
                act.activation(sq[:], out, ACT.Square).then_inc(squared.sem, 1)
                act.wait_ge(mean.sem, 1)
                act.activation(sq[:], sq[:], ACT.Sqrt).then_inc(root.sem, 1)

            @block.tensor
            def _(pe):
                pe.wait_ge(squared.sem, 1)
                for h in range(HEADS2):
                    mm = pe.matmul(k.ps[:, h], k.ones[:], sq[:, h], start=True, stop=True)
                mm.then_inc(summed.sem, 1)

            @block.vector
            def _(dve):
                step = lambda ins: k.dve_steps.then(dve, ins)
                dve.wait_ge(summed.sem, 1)
                dve.tensor_scalar(sq[:], k.ps[:, 0:HEADS2], 1.0 / P, EPS, ALU.mult, ALU.add).then_inc(mean.sem, 1)
                dve.wait_ge(root.sem, 1)
                step(dve.reciprocal(sq[:], sq[:]))
                step(dve.tensor_tensor(sq[:], sq[:], gate, ALU.mult))
                step(dve.tensor_scalar(sq[:], sq[:], k.vec("gn"), None, ALU.mult))
                step(dve.tensor_tensor(out, out, sq[:], ALU.mult))


def spread(dve, src, dst, scale):
    to = dst.rearrange("p (a r) n -> p a r n", r=4)
    of = src.rearrange("p (a r) n -> p a r n", r=4)
    for r in range(4):
        for s in range(2):
            rows = slice(64 * s, 64 * (s + 1))
            at = 32 * r + 16 * s
            ins = dve.tensor_scalar(to[rows, :, r, at:at + 16], of[rows, :, r, :], scale, None, ALU.mult)
    return ins


def s5(k, u, out):
    nc = k.nc
    HALF = S5T // 2
    with ExitStack() as ctx:
        b_t = k.sbuf("s5_b_t", [P, 2, S5T, P], ctx=ctx)
        c_x = k.sbuf("s5_c_x", [P, 2, S5T, P], ctx=ctx)
        mag = k.sbuf("s5_mag", [P, S5T], ctx=ctx)
        unit = k.sbuf("s5_unit", [P, 2, S5T], ctx=ctx)
        with ExitStack() as tmp:
            load = k.sbuf("s5_load", [P, 4, S5T, 16], ctx=tmp)
            bb = k.sbuf("s5_bb", [P, 3, S5T, 16], ctx=tmp)
            s = k.sbuf("s5_small", [P, 10, S5T], ctx=tmp)
            loads = Signal(tmp, nc, "s5_loaded")
            handed = Signal(tmp, nc, "s5_to_act")
            acted = Signal(tmp, nc, "s5_act_done")
            with nc.Block() as block:
                @block.sync
                def _(sp):
                    for n, name in enumerate(("b_re", "b_im", "c_re", "c_im")):
                        sp.dma_start(load[:, n], k.dram["s5_" + name]).then_inc(loads.sem, 16)

                @block.scalar
                def _(act):
                    act.activation(s[:, 0], k.vec("log_dt"), ACT.Exp).then_inc(acted.sem, 1)
                    act.wait_ge(handed.sem, 1)
                    act.activation(mag[:], s[:, 1], ACT.Exp).then_inc(acted.sem, 1)
                    act.wait_ge(handed.sem, 2)
                    act.activation(unit[:, 0], s[:, 5], ACT.Sin).then_inc(acted.sem, 1)
                    act.activation(unit[:, 1], s[:, 4], ACT.Sin).then_inc(acted.sem, 1)

                @block.vector
                def _(dve):
                    step = lambda ins: k.dve_steps.then(dve, ins)
                    tt = lambda o, a, b, op: step(dve.tensor_tensor(o, a, b, op))
                    ar, ai = k.vec("a_re"), k.vec("a_im")
                    step(dve.memset(b_t[:], 0.0))
                    step(dve.memset(c_x[:], 0.0))
                    dve.wait_ge(acted.sem, 1)
                    dve.tensor_tensor(s[:, 1], ar, s[:, 0], ALU.mult).then_inc(handed.sem, 1)
                    tt(s[:, 2], ai, s[:, 0], ALU.mult)
                    reduce_angle(k, dve, s[:, 2], s[:, 3], s[:, 4], s[:, 5])
                    dve.sem_inc(handed.sem, 1)
                    dve.wait_ge(acted.sem, 4)
                    tt(s[:, 0], mag[:], unit[:, 0], ALU.mult)
                    step(dve.tensor_scalar(s[:, 0], s[:, 0], -1.0, None, ALU.add))
                    tt(s[:, 1], mag[:], unit[:, 1], ALU.mult)
                    tt(s[:, 2], ar, ar, ALU.mult)
                    tt(s[:, 3], ai, ai, ALU.mult)
                    tt(s[:, 2], s[:, 2], s[:, 3], ALU.add)
                    step(dve.reciprocal(s[:, 2], s[:, 2]))
                    tt(s[:, 3], s[:, 0], ar, ALU.mult)
                    tt(s[:, 4], s[:, 1], ai, ALU.mult)
                    tt(s[:, 3], s[:, 3], s[:, 4], ALU.add)
                    tt(s[:, 6], s[:, 3], s[:, 2], ALU.mult)
                    tt(s[:, 3], s[:, 1], ar, ALU.mult)
                    tt(s[:, 4], s[:, 0], ai, ALU.mult)
                    tt(s[:, 3], s[:, 3], s[:, 4], ALU.subtract)
                    tt(s[:, 7], s[:, 3], s[:, 2], ALU.mult)
                    dve.wait_ge(loads.sem, 64)
                    wide = lambda n: s[:, n].unsqueeze(2).to_broadcast((P, S5T, 16))
                    tt(bb[:, 0], load[:, 0], wide(6), ALU.mult)
                    tt(bb[:, 2], load[:, 1], wide(7), ALU.mult)
                    tt(bb[:, 0], bb[:, 0], bb[:, 2], ALU.subtract)
                    tt(bb[:, 1], load[:, 1], wide(6), ALU.mult)
                    tt(bb[:, 2], load[:, 0], wide(7), ALU.mult)
                    tt(bb[:, 1], bb[:, 1], bb[:, 2], ALU.add)
                    for n in range(2):
                        step(spread(dve, bb[:, n], b_t[:, n], 1.0))
                        step(spread(dve, load[:, 2 + n], c_x[:, n], 1.0 if n == 0 else -1.0))
        squares = [b_t[:, n, t] for n in range(2) for t in range(S5T)]
        token_major(k, squares, squares)
        y = k.sbuf("s5_y", [P, 4, T], ctx=ctx)
        glu_w = k.sbuf("glu_w", [P, 4, 512], ctx=ctx)
        glu_loaded = Signal(ctx, k.nc, "glu_loaded")
        with ExitStack() as tmp:
            turn = k.sbuf("s5_turn", [P, 2, HALF, T], ctx=tmp)
            s5_scan(k, u, y, turn, unit, mag, b_t, c_x, glu_w, glu_loaded)
        state = k.sbuf("s5_mixed", [P, 4, T], ctx=ctx)
        s5_glu(k, y, glu_w, glu_loaded, state)
        split_tiles(k, state, out, 4)


def s5_scan(k, u, y, turn, unit, mag, b_t, c_x, glu_w, glu_loaded):
    nc = k.nc
    HALF = S5T // 2
    with ExitStack() as tmp:
        part = k.sbuf("s5_part", [P, 2, 2, T], ctx=tmp)
        ipart = k.sbuf("s5_imag_part", [P, 2, T], ctx=tmp)
        w = k.sbuf("s5_w", [P, 2, 2, T], ctx=tmp)
        x = k.sbuf("s5_x", [P, 2, 2, T], ctx=tmp)
        ppart = k.sbuf("s5_pool_part", [P, T], ctx=tmp)
        dbl = k.sbuf("s5_double", [P, 2, 2, S5T // 2], ctx=tmp)
        cross = k.sbuf("s5_cross", [P, S5T // 2], ctx=tmp)
        fed = Signal(tmp, nc, "s5_inputs_ready")
        rotated = Signal(tmp, nc, "s5_inputs_read")
        scanned = Signal(tmp, nc, "s5_scanned")
        real = Signal(tmp, nc, "s5_real_ready")
        imag = Signal(tmp, nc, "s5_imag_ready")
        done = Signal(tmp, nc, "s5_tile_multiplied")
        skipped = Signal(tmp, nc, "s5_skip_added")
        with nc.Block() as block:
            @block.sync
            def _(sp):
                sp.dma_start(glu_w[:], k.dram["glu_w"]).then_inc(glu_loaded.sem, 16)

            @block.tensor
            def _(pe):
                def feed(t):
                    if t >= 2:
                        pe.wait_ge(rotated.sem, t - 1)
                    for n in range(2):
                        mm = pe.matmul(k.ps[:, 2 * (t % 2) + n], b_t[:, n, t], u[:, t // 4], start=True, stop=True)
                    mm.then_inc(fed.sem, 1)

                feed(0)
                for t in range(S5T):
                    if t + 1 < S5T:
                        feed(t + 1)
                    bank = 4 + (t // 4) % 2
                    if t % 4 == 0 and t >= 8:
                        pe.wait_ge(skipped.sem, t // 4 - 1)
                    pe.wait_ge(real.sem, t + 1)
                    pe.matmul(k.ps[:, bank], c_x[:, 0, t], x[:, t % 2, 0], start=t % 4 == 0, stop=False)
                    pe.wait_ge(imag.sem, t + 1)
                    pe.matmul(k.ps[:, bank], c_x[:, 1, t], x[:, t % 2, 1], start=False, stop=t % 4 == 3)\
                      .then_inc(done.sem, 1)

            @block.gpsimd
            def _(pool):
                for t in range(S5T):
                    cos, sin = turn[:, 0, t % HALF], turn[:, 1, t % HALF]
                    pool.wait_ge(scanned.sem, t + 1)
                    if t >= 2:
                        pool.wait_ge(done.sem, t - 1)
                    pool.tensor_tensor(ppart[:], sin, w[:, t % 2, 1], ALU.mult)
                    k.pool_steps.then(pool, pool.tensor_tensor(x[:, t % 2, 0], cos, w[:, t % 2, 0], ALU.mult))
                    pool.tensor_tensor(x[:, t % 2, 0], x[:, t % 2, 0], ppart[:], ALU.subtract).then_inc(real.sem, 1)
                    pool.wait_ge(real.sem, t + 1)

            @block.vector
            def _(dve):
                step = lambda ins: k.dve_steps.then(dve, ins)
                tt = lambda o, a, b, op: step(dve.tensor_tensor(o, a, b, op))

                def tables(half):
                    own = slice(half * HALF, (half + 1) * HALF)
                    c, s = turn[:, 0], turn[:, 1]
                    dve.memset(c[:, :, 0:1], 1.0)
                    dve.memset(s[:, :, 0:1], 0.0)
                    step(dve.tensor_copy(dbl[:, 0], unit[:, :, own]))
                    n, m = 1, 0
                    while n < T:
                        ca, sa = dbl[:, m, 0], dbl[:, m, 1]
                        fit = min(HALF, 2 * T // n)
                        cols = part[:].rearrange("p a b t -> p a (b t)")[:, :, 0:fit * n].rearrange("p a (g t) -> p a g t", t=n)
                        for first in range(0, HALF, fit):
                            g = slice(first, first + fit)
                            by = lambda small: small[:, g].unsqueeze(1).unsqueeze(3).to_broadcast((P, 2, fit, n))
                            lo, hi = turn[:, :, g, 0:n], turn[:, :, g, n:2 * n]
                            dve.tensor_tensor(cols, lo, by(sa), ALU.mult)
                            tt(hi, lo, by(ca), ALU.mult)
                            dve.tensor_tensor(hi[:, 0], hi[:, 0], cols[:, 1], ALU.subtract)
                            ins = dve.tensor_tensor(hi[:, 1], hi[:, 1], cols[:, 0], ALU.add)
                            if first + fit < HALF:
                                step(ins)
                        c2, s2 = dbl[:, 1 - m, 0], dbl[:, 1 - m, 1]
                        dve.tensor_tensor(c2, ca, ca, ALU.mult)
                        dve.tensor_tensor(s2, ca, sa, ALU.mult)
                        tt(cross[:], sa, sa, ALU.mult)
                        dve.tensor_tensor(c2, c2, cross[:], ALU.subtract)
                        step(dve.tensor_scalar(s2, s2, 2.0, None, ALU.mult))
                        n, m = 2 * n, 1 - m

                def imaginary(t):
                    cos, sin = turn[:, 0, t % HALF], turn[:, 1, t % HALF]
                    if t >= 2:
                        dve.wait_ge(done.sem, t - 1)
                    dve.tensor_tensor(ipart[:, 0], w[:, t % 2, 1], cos, ALU.mult)
                    tt(ipart[:, 1], w[:, t % 2, 0], sin, ALU.mult)
                    dve.tensor_tensor(x[:, t % 2, 1], ipart[:, 0], ipart[:, 1], ALU.add).then_inc(imag.sem, 1)

                def skip(m):
                    dve.wait_ge(done.sem, 4 * m + 4)
                    dve.scalar_tensor_tensor(y[:, m], u[:, m], k.vec("d_skip")[:, m:m + 1], k.ps[:, 4 + m % 2],
                                             ALU.mult, ALU.add).then_inc(skipped.sem, 1)

                for t in range(S5T):
                    if t % HALF == 0:
                        if t:
                            dve.wait_ge(real.sem, t)
                        tables(t // HALF)
                    wr, wi = w[:, t % 2, 0], w[:, t % 2, 1]
                    dve.wait_ge(fed.sem, t + 1)
                    both = k.ps[:, 2 * (t % 2):2 * (t % 2) + 2]
                    for n in range(2):
                        by = turn[:, n, t % HALF].unsqueeze(1).to_broadcast((P, 2, T))
                        ins = dve.tensor_tensor(part[:, n], both, by, ALU.mult)
                    ins.then_inc(rotated.sem, 1)
                    dve.wait_ge(rotated.sem, t + 1)
                    if t >= 2:
                        dve.wait_ge(real.sem, t - 1)
                        dve.wait_ge(imag.sem, t - 1)
                    dve.tensor_tensor(wr, part[:, 0, 0], part[:, 1, 1], ALU.add)
                    tt(wi, part[:, 0, 1], part[:, 1, 0], ALU.subtract)
                    decay = mag[:, t:t + 1].to_broadcast((P, T))
                    dve.tensor_tensor_scan(wr, decay, wr, 0.0, ALU.mult, ALU.add)
                    dve.tensor_tensor_scan(wi, decay, wi, 0.0, ALU.mult, ALU.add).then_inc(scanned.sem, 1)
                    dve.wait_ge(scanned.sem, t + 1)
                    imaginary(t)
                    if t % 4 == 0 and t:
                        skip(t // 4 - 1)
                    dve.wait_ge(imag.sem, t + 1)
                skip(S5T // 4 - 1)


def s5_glu(k, y, w, loads, out):
    nc = k.nc
    with ExitStack() as tmp:
        acted = Signal(tmp, nc, "glu_gelu_ready")
        gated = Signal(tmp, nc, "glu_gate_ready")
        product = Signal(tmp, nc, "glu_product_ready")
        with nc.Block() as block:
            @block.scalar
            def _(act):
                for m in range(4):
                    act.activation(y[:, m], y[:, m], ACT.Gelu).then_inc(acted.sem, 1)
                for m in range(4):
                    act.wait_ge(product.sem, m + 1)
                    act.activation(out[:, m], k.ps[:, m], ACT.Sigmoid, bias=k.vec("glu_b")[:, m:m + 1])\
                       .then_inc(gated.sem, 1)

            @block.tensor
            def _(pe):
                pe.wait_ge(loads.sem, 16)
                pe.wait_ge(acted.sem, 4)
                for m in range(4):
                    for x in range(4):
                        mm = pe.matmul(k.ps[:, m], w[:, x, m * P:(m + 1) * P], y[:, x], start=x == 0, stop=x == 3)
                    mm.then_inc(product.sem, 1)

            @block.vector
            def _(dve):
                for m in range(4):
                    dve.wait_ge(gated.sem, m + 1)
                    dve.tensor_tensor(out[:, m], out[:, m], y[:, m], ALU.mult)


def mixer2(k, gain):
    modulation(k, gain)
    norm(k, gain[:, 0], k.u, k.mod[:, 0:KD])
    with ExitStack() as ctx:
        state_in = k.sbuf("s5_in", [P, 4, T], ctx=ctx)
        with ExitStack() as inner:
            proj = k.sbuf("proj2", [P, 16, T], ctx=inner)
            copy_tiles(k, k.dram["w_in_2"], 16, proj, k.u)
            copy_tiles(k, k.dram["w_in_2_state"], 4, state_in, k.u)
            mixed = k.sbuf("hg_mixed", [P, 4, T], ctx=inner)
            hgrn(k, proj, mixed[:])
            split_tiles(k, mixed, k.u)
        s5(k, state_in, k.u)
    residual(k, k.dram["w_out_2"], KD, k.u, k.mod[:, 2 * KD:3 * KD])


PH = 8
TOPK = 16
I1 = P // ROUNDS
LOW = -3.0e38


def top16(k, dve, tables):
    step = lambda ins: k.dve_steps.then(dve, ins)
    for src, work, values, index in tables:
        ins = dve.max(values[:, 0:8], src)
    step(ins)
    for src, work, values, index in tables:
        dve.max_index(index[:, 0:8], values[:, 0:8], src)
        ins = dve.match_replace(work, values[:, 0:8], src, LOW)
    step(ins)
    for src, work, values, index in tables:
        ins = dve.max(values[:, 8:16], work)
    step(ins)
    for src, work, values, index in tables:
        ins = dve.max_index(index[:, 8:16], values[:, 8:16], work)
    return ins


def early_stream(k):
    chunks = [(chunk_of(k.dram["peer_u"], 8, e),
               [(4 + e % 4, k.ps[:, 4 + e % 4], [(x, k.u.high[:, x], k.u.low[:, x]) for x in range(KD)], True, True, None)])
              for e in range(8)]
    return Stream(k, I1 // 8, chunks)


def route(k, by_choice):
    nc = k.nc
    with ExitStack() as ctx:
        q = k.sbuf("peer_q", [P, 2 * PH, T], ctx=ctx)
        keys = k.sbuf("peer_keys", [P, 2, P], ctx=ctx)
        copy_tiles(k, k.dram["peer_wq"], 2 * PH, q, k.u)
        work = k.sbuf("peer_work", [P, 4, P], ctx=ctx)
        cand_work = k.sbuf("peer_cand_work", [P, PH, TOPK * TOPK], ctx=ctx)
        best = k.sbuf("peer_best", [P, PH, 2, TOPK], ctx=ctx)
        which = k.sbuf("peer_which", [P, PH, 2, TOPK], U32, ctx)
        whichf = k.sbuf("peer_whichf", [P, 2, PH, 2, TOPK], ctx=ctx)
        cand = k.sbuf("peer_cand", [P, PH, TOPK, TOPK], ctx=ctx)
        top = k.sbuf("peer_top", [P, PH, TOPK], ctx=ctx)
        place = k.sbuf("peer_place", [P, PH, TOPK], U32, ctx)
        part = k.sbuf("peer_part", [P, 2, PH, TOPK], U32, ctx)
        partf = k.sbuf("peer_partf", [P, 2, PH * TOPK], ctx=ctx)
        hot = k.sbuf("peer_hot", [P, 2, PH * TOPK, TOPK], ctx=ctx)
        chosen = k.sbuf("peer_chosen", [P, QT, 3, PH * TOPK], ctx=ctx)
        count = k.sbuf("peer_count", [P, TOPK], ctx=ctx)
        total = k.sbuf("peer_total", [P, QT, PH], ctx=ctx)
        loads = Signal(ctx, nc, "peer_keys_loaded")
        counted = Signal(ctx, nc, "peer_count_ready")
        scored = Signal(ctx, nc, "peer_scored")
        ranked = Signal(ctx, nc, "peer_ranked")
        shifted = Signal(ctx, nc, "peer_shifted")
        exped = Signal(ctx, nc, "peer_exped")
        placed = Signal(ctx, nc, "peer_placed")
        named = Signal(ctx, nc, "peer_named")
        early = k.sbuf("early_act", [P, 4, T], ctx=ctx)
        stored = k.early_moved[:4]
        stream = early_stream(k)
        assert stream.iters == QT
        with nc.Block() as block:
            @block.sync
            def _(sp):
                sp.dma_start(keys[:], k.dram["peer_keys"]).then_inc(loads.sem, 16)
                stream.load(sp)

            @block.gpsimd
            def _(pool):
                pool.iota(count[:], pattern=[[1, TOPK]], base=0, channel_multiplier=0,
                          allow_small_or_imprecise_dtypes=True).then_inc(counted.sem, 1)

                def name(qt):
                    for s in range(2):
                        pool.wait_ge(placed.sem, 2 * qt + s + 1)
                        names = whichf[:, qt % 2, :, s].unsqueeze(2).to_broadcast((P, PH, TOPK, TOPK))
                        view = hot[:, s].rearrange("p (h c) a -> p h c a", h=PH)
                        pool.tensor_tensor(view, view, names, ALU.mult).then_inc(named.sem, 1)

                def beside(i):
                    if i >= 1:
                        name(i - 1)

                stream.split_low(pool, beside)
                name(QT - 1)

            @block.tensor
            def _(pe):
                pe.wait_ge(loads.sem, 16)
                for qt in range(QT):
                    for quad in range(4):
                        if qt >= 1:
                            pe.wait_ge(ranked.sem, (qt - 1) * 4 + quad + 1)
                        for m in range(4):
                            t = 4 * quad + m
                            mm = pe.matmul(k.ps[:, quad, m * P:(m + 1) * P], q[:, t, qt * P:(qt + 1) * P],
                                           keys[:, t % 2], start=True, stop=True)
                        mm.then_inc(scored.sem, 1)
                    stream.multiply_once(pe, qt)

            @block.scalar
            def _(act):
                def epilogue(i, e):
                    n = i * 8 + e
                    stream.wait_products(act, i, e)
                    if n >= 4:
                        act.wait_ge(stored[n % 4].sem, 16 * (n // 4))
                    act.activation(early[:, n % 4], k.ps[:, 4 + n % 4], ACT.Gelu).then_inc(k.emptied[4 + n % 4].sem, 1)

                def after(i, e):
                    n = i * 8 + e
                    act.wait_ge(k.emptied[4 + n % 4].sem, k.emptied[4 + n % 4].at(n // 4 + 1))
                    act.dma_start(k.dram["early_act"][n], early[:, n % 4]).then_inc(stored[n % 4].sem, 16)

                stream.scalar(act, epilogue, after, unrolled=True)
                act.wait_ge(shifted.sem, QT)
                act.activation(chosen[:, :, 2], chosen[:, :, 2], ACT.Exp).then_inc(exped.sem, 1)
                for s in range(4):
                    act.wait_ge(stored[s].sem, 16 * (I1 // 4))

            @block.vector
            def _(dve):
                step = lambda ins: k.dve_steps.then(dve, ins)
                tt = lambda o, a, b, op: step(dve.tensor_tensor(o, a, b, op))

                def gather(qt):
                    for s in range(2):
                        dve.wait_ge(named.sem, 2 * qt + s + 1)
                        ins = dve.tensor_reduce(chosen[:, qt, s], hot[:, s], AX.X, ALU.add)
                    step(ins)

                dve.wait_ge(counted.sem, 1)
                for qt in range(QT):
                    gate = chosen[:, qt, 2].rearrange("p (h c) -> p h c", h=PH)
                    for quad in range(4):
                        n = qt * 4 + quad
                        dve.wait_ge(scored.sem, n + 1)
                        tables = [(4 * quad + m, m) for m in range(4)]
                        step(top16(k, dve, [(k.ps[:, quad, m * P:(m + 1) * P], work[:, m], best[:, t // 2, t % 2],
                                             which[:, t // 2, t % 2]) for t, m in tables]))
                        dve.sem_inc(ranked.sem, 1)
                    dve.tensor_copy(whichf[:, qt % 2], which[:])
                    first = best[:, :, 0].unsqueeze(3).to_broadcast((P, PH, TOPK, TOPK))
                    second = best[:, :, 1].unsqueeze(2).to_broadcast((P, PH, TOPK, TOPK))
                    tt(cand[:], first, second, ALU.add)
                    step(top16(k, dve, [(cand[:, h].rearrange("p a b -> p (a b)"), cand_work[:, h], top[:, h], place[:, h])
                                        for h in range(PH)]))
                    dve.tensor_tensor(gate, top[:], top[:, :, 0:1].to_broadcast((P, PH, TOPK)), ALU.subtract)\
                       .then_inc(shifted.sem, 1)
                    dve.tensor_scalar(part[:, 0], place[:], 4, None, ALU.logical_shift_right)
                    step(dve.tensor_scalar(part[:, 1], place[:], 15, None, ALU.bitwise_and))
                    step(dve.tensor_copy(partf[:], part[:].rearrange("p s h c -> p s (h c)")))
                    if qt >= 1:
                        gather(qt - 1)
                    for s in range(2):
                        at = partf[:, s].unsqueeze(2).to_broadcast((P, PH * TOPK, TOPK))
                        dve.tensor_tensor(hot[:, s], at, count[:].unsqueeze(1).to_broadcast((P, PH * TOPK, TOPK)),
                                          ALU.is_equal).then_inc(placed.sem, 1)
                gates = chosen[:, :, 2].rearrange("p q (h c) -> p q h c", h=PH)
                dve.wait_ge(exped.sem, 1)
                step(dve.tensor_reduce(total[:], gates, AX.X, ALU.add))
                step(dve.reciprocal(total[:], total[:]))
                tt(gates, gates, total[:].unsqueeze(3).to_broadcast((P, QT, PH, TOPK)), ALU.mult)
                gather(QT - 1)
        stream.finish()
        for s in range(4):
            stored[s].passed(16 * (I1 // 4))
        token_major(k, [chosen[:, qt, s] for s in range(3) for qt in range(QT)],
                    [by_choice[:, s, qt * P:(qt + 1) * P] for s in range(3) for qt in range(QT)])


TOK = T // I1
PIECES = 3


class Choices:

    def __init__(self, k, ctx):
        self.names = k.sbuf("choice_names", [P, 2, T], BF16, ctx)
        self.gates = k.sbuf("choice_gates", [P, PIECES, T], BF16, ctx)
        self.count = k.sbuf("expert_count", [P, P, TOK], BF16, ctx)


def split_choices(k, by_choice, choices):
    nc = k.nc
    with ExitStack() as tmp:
        rest = k.sbuf("gate_rest", [P, T], ctx=tmp)
        iota = k.sbuf("expert_iota", [P, P], ctx=tmp)
        counted = Signal(tmp, nc, "expert_iota_ready")
        with nc.Block() as block:
            @block.gpsimd
            def _(pool):
                pool.iota(iota[:], pattern=[[1, P]], base=0, channel_multiplier=0,
                          allow_small_or_imprecise_dtypes=True).then_inc(counted.sem, 1)

            @block.vector
            def _(dve):
                step = lambda ins: k.dve_steps.then(dve, ins)
                dve.tensor_copy(choices.names[:], by_choice[:, 0:2])
                step(dve.tensor_copy(choices.gates[:, 0], by_choice[:, 2]))
                step(dve.tensor_tensor(rest[:], by_choice[:, 2], choices.gates[:, 0], ALU.subtract))
                step(dve.tensor_copy(choices.gates[:, 1], rest[:]))
                step(dve.tensor_tensor(rest[:], rest[:], choices.gates[:, 1], ALU.subtract))
                dve.tensor_copy(choices.gates[:, 2], rest[:])
                dve.wait_ge(counted.sem, 1)
                dve.tensor_copy(choices.count[:], iota[:].unsqueeze(2).to_broadcast((P, P, TOK)))


def expert_weights(k, r, choices, weight, sig):
    nc = k.nc
    rows_ready, hot_ready, cols_ready, rest_ready, product, copied = sig
    iters = T // (2 * TOK)
    with ExitStack() as tmp:
        rows = k.sbuf("hot_i2", [P, 2, P, TOK], BF16, tmp)
        hot = k.sbuf("hot_i1", [P, 2, I1, TOK], BF16, tmp)
        cols = k.sbuf("gated_i1", [P, 2, PIECES, I1, TOK], BF16, tmp)

        def gated(eng, b, piece, tokens):
            gates = choices.gates[:, piece, tokens].unsqueeze(1).to_broadcast((P, I1, TOK))
            return eng.tensor_tensor(cols[:, b, piece], hot[:, b], gates, ALU.mult)

        with nc.Block() as block:
            @block.gpsimd
            def _(pool):
                with pool.Fori(0, iters) as i:
                    for b in range(2):
                        pool.wait_ge(hot_ready[b].sem, i + hot_ready[b].at(1))
                        gated(pool, b, 2, bass.ds(i * (2 * TOK) + b * TOK, TOK)).then_inc(rest_ready[b].sem, 1)

            @block.vector
            def _(dve):
                with dve.Fori(0, iters) as i:
                    for b in range(2):
                        tokens = bass.ds(i * (2 * TOK) + b * TOK, TOK)
                        dve.wait_ge(product[b].sem, i + product[b].at(0))
                        dve.tensor_tensor(hot[:, b], choices.names[:, 0, tokens].unsqueeze(1).to_broadcast((P, I1, TOK)),
                                          choices.count[:, r * I1:(r + 1) * I1], ALU.is_equal).then_inc(hot_ready[b].sem, 1)
                        dve.tensor_tensor(rows[:, b], choices.names[:, 1, tokens].unsqueeze(1).to_broadcast((P, P, TOK)),
                                          choices.count[:], ALU.is_equal).then_inc(rows_ready[b].sem, 1)
                        dve.wait_ge(hot_ready[b].sem, i + hot_ready[b].at(1))
                        for piece in range(2):
                            gated(dve, b, piece, tokens).then_inc(cols_ready[b].sem, 1)

            @block.tensor
            def _(pe):
                with pe.Fori(0, iters) as i:
                    for b in range(2):
                        pe.wait_ge(rows_ready[b].sem, i + rows_ready[b].at(1))
                        pe.wait_ge(cols_ready[b].sem, i * 2 + cols_ready[b].at(2))
                        pe.wait_ge(rest_ready[b].sem, i + rest_ready[b].at(1))
                        pe.wait_ge(copied[b].sem, i + copied[b].at(0))
                        for t in range(TOK):
                            for piece in range(PIECES):
                                mm = pe.matmul(k.ps[:, b, t * I1:(t + 1) * I1], rows[:, b, :, t], cols[:, b, piece, :, t],
                                               start=piece == 0, stop=piece == PIECES - 1)
                        mm.then_inc(product[b].sem, 1)

            @block.scalar
            def _(act):
                with act.Fori(0, iters) as i:
                    for b in range(2):
                        act.wait_ge(product[b].sem, i + product[b].at(1))
                        act.activation(weight[:, :, bass.ds(i * (2 * TOK) + b * TOK, TOK)].rearrange("p e t -> p t e"),
                                       k.ps[:, b].rearrange("p (t e) -> p t e", t=TOK), ACT.Copy)\
                           .then_inc(copied[b].sem, 1)
    for b in range(2):
        for s in (rows_ready, hot_ready, rest_ready, product, copied):
            s[b].passed(iters)
        cols_ready[b].passed(2 * iters)


def experts_first(k, weight, gate):
    nc = k.nc
    with ExitStack() as tmp:
        product = k.sbuf("early_product", [P, 8, T], ctx=tmp)
        coef = Split(k, tmp, "early_coef", 8)
        loaded = k.early_moved
        _, product_ready, high_ready, low_ready = k.expert_signals

        def coef_is_ready(pe, i, e):
            pe.wait_ge(low_ready.sem, i * 8 + low_ready.at(e + 1))

        chunks = [(chunk_of(k.dram["peer_v"], 8, d),
                   [(4 + d % 4, k.ps[:, 4 + d % 4], [(x, coef.high[:, x], coef.low[:, x]) for x in range(8)], True, True,
                     coef_is_ready if d == 0 else None)]) for d in range(KD)]
        stream = Stream(k, I1 // 8, chunks)
        with nc.Block() as block:
            @block.sync
            def _(sp):
                for e in range(8):
                    sp.dma_start(product[:, e], k.dram["early_act"][e]).then_inc(loaded[e].sem, 16)

                def next_acts(i):
                    if isinstance(i, int):
                        return
                    for e in range(8):
                        src = k.dram["early_act"][bass.ds(i * 8 + (8 + e), 1), :, :].rearrange("a p n -> p (a n)")
                        sp.wait_ge(low_ready.sem, i * 8 + low_ready.at(e + 1))
                        sp.dma_start(product[:, e], src).then_inc(loaded[e].sem, 16)

                stream.load(sp, next_acts)

            @block.gpsimd
            def _(pool):
                stream.split_low(pool)

            @block.tensor
            def _(pe):
                stream.multiply(pe)

            @block.scalar
            def _(act):
                def epilogue(i, d):
                    if d == 0:
                        for e in range(8):
                            act.wait_ge(product_ready.sem, i * 8 + product_ready.at(e + 1))
                            act.activation(coef.high[:, e], product[:, e], ACT.Copy).then_inc(high_ready.sem, 1)

                stream.scalar(act, epilogue)

            @block.vector
            def _(dve):
                with dve.Fori(0, stream.iters) as i:
                    def low(e):
                        dve.wait_ge(high_ready.sem, i * 8 + high_ready.at(e + 1))
                        dve.tensor_tensor(coef.low[:, e], product[:, e], coef.high[:, e].bitcast(F32),
                                          ALU.subtract).then_inc(low_ready.sem, 1)

                    for e in range(8):
                        dve.wait_ge(loaded[e].sem, i * 16 + loaded[e].at(16))
                        dve.tensor_tensor(product[:, e], product[:, e], one(weight, i * 8 + e), ALU.mult)\
                           .then_inc(product_ready.sem, 1)
                        if e >= 1:
                            low(e - 1)
                    low(7)
                    for d in range(KD):
                        stream.wait_products(dve, i, d)
                        dve.scalar_tensor_tensor(k.h[:, d], k.ps[:, 4 + d % 4], gate[:, d:d + 1], k.h[:, d],
                                                 ALU.mult, ALU.add).then_inc(k.emptied[4 + d % 4].sem, 1)
        stream.finish()
    for e in range(8):
        loaded[e].passed(16 * (I1 // 8))
    for s in (product_ready, high_ready, low_ready):
        s.passed(I1)


def experts(k, r, weight, gate, sig):
    nc = k.nc
    gelu_ready, product_ready, high_ready, low_ready = sig
    with ExitStack() as tmp:
        acted = k.sbuf("expert_act", [P, 2, T], ctx=tmp)
        product = k.sbuf("expert_product", [P, 2, T], ctx=tmp)
        coef = Split(k, tmp, "expert_coef", 8)
        iters = I1 // 8
        base = r * I1

        def source(name, j):
            return lambda i: k.dram[name][bass.ds(i * 8 + (base + j), 1), :, :].rearrange("a p n -> p (a n)")

        def coef_is_ready(pe, i, e):
            pe.wait_ge(low_ready.sem, i * 8 + low_ready.at(e + 1))

        chunks = [(source("peer_u", e), [(e % 4, k.ps[:, e % 4], [(x, k.u.high[:, x], k.u.low[:, x]) for x in range(KD)], True, True, None)])
                  for e in range(8)]
        chunks += [(source("peer_v", d), [(4 + d % 4, k.ps[:, 4 + d % 4], [(x, coef.high[:, x], coef.low[:, x]) for x in range(8)],
                                           True, True, coef_is_ready if d == 0 else None)]) for d in range(KD)]
        stream = Stream(k, iters, chunks)
        with nc.Block() as block:
            @block.sync
            def _(sp):
                stream.load(sp)

            @block.gpsimd
            def _(pool):
                stream.split_low(pool)

            @block.tensor
            def _(pe):
                stream.multiply(pe)

            @block.scalar
            def _(act):
                def epilogue(i, e):
                    if e < 8:
                        stream.wait_products(act, i, e)
                        act.wait_ge(product_ready.sem, i * 8 + product_ready.at(e - 1))
                        act.activation(acted[:, e % 2], k.ps[:, e % 4], ACT.Gelu).then_inc(gelu_ready.sem, 1)

                def after(i, e):
                    if e < 8:
                        act.wait_ge(product_ready.sem, i * 8 + product_ready.at(e + 1))
                        act.activation(coef.high[:, e], product[:, e % 2], ACT.Copy).then_inc(high_ready.sem, 1)

                stream.scalar(act, epilogue, after)

            @block.vector
            def _(dve):
                with dve.Fori(0, iters) as i:
                    for e in range(8):
                        dve.wait_ge(gelu_ready.sem, i * 8 + gelu_ready.at(e + 1))
                        dve.sem_inc(k.emptied[e % 4].sem, 1)
                        dve.wait_ge(low_ready.sem, i * 8 + low_ready.at(e - 1))
                        dve.tensor_tensor(product[:, e % 2], acted[:, e % 2], one(weight, i * 8 + e), ALU.mult)\
                           .then_inc(product_ready.sem, 1)
                        dve.wait_ge(high_ready.sem, i * 8 + high_ready.at(e + 1))
                        dve.tensor_tensor(coef.low[:, e], product[:, e % 2], coef.high[:, e].bitcast(F32),
                                          ALU.subtract).then_inc(low_ready.sem, 1)
                    for d in range(KD):
                        stream.wait_products(dve, i, 8 + d)
                        dve.scalar_tensor_tensor(k.h[:, d], k.ps[:, 4 + d % 4], gate[:, d:d + 1], k.h[:, d],
                                                 ALU.mult, ALU.add).then_inc(k.emptied[4 + d % 4].sem, 1)
        stream.finish()
    for s in (gelu_ready, product_ready, high_ready, low_ready):
        s.passed(8 * iters)


def peer(k, gain):
    nc = k.nc
    norm(k, gain[:, 1], k.u, k.mod[:, 3 * KD:4 * KD], summed=True)
    with ExitStack() as ctx:
        choices = Choices(k, ctx)
        with ExitStack() as tmp:
            by_choice = k.sbuf("by_choice", [P, 3, T], ctx=tmp)
            route(k, by_choice)
            split_choices(k, by_choice, choices)
        weight = k.sbuf("expert_weight", [P, I1, T], ctx=ctx)
        for r in range(ROUNDS):
            expert_weights(k, r, choices, weight, k.weight_signals)
            if r == 0:
                experts_first(k, weight, k.mod[:, 5 * KD:6 * KD])
            else:
                experts(k, r, weight, k.mod[:, 5 * KD:6 * KD], k.expert_signals)


def signals_of_loops(k):
    pair = lambda name, base=0: [k.new_sem(f"{name}{b}", base) for b in range(2)]
    k.ffn_signals = (pair("gated_ready"), pair("product_ready", 1), pair("hid_high_ready"), pair("hid_low_ready", 1))
    k.weight_signals = (pair("rows_ready"), pair("hot_ready"), pair("cols_ready"), pair("last_cols_ready"),
                        pair("weights_ready", 1), pair("weights_copied", 1))
    k.expert_signals = (k.new_sem("gelu_ready"), k.new_sem("expert_product_ready", 2), k.new_sem("coef_high_ready"),
                        k.new_sem("coef_low_ready", 2))
    k.early_moved = [k.new_sem(f"early_act_moved{e}") for e in range(8)]
    with k.nc.Block() as block:
        @block.vector
        def _(dve):
            for b in range(2):
                dve.sem_inc(k.ffn_signals[1][b].sem, 1)
                dve.sem_inc(k.ffn_signals[3][b].sem, 1)
                dve.sem_inc(k.weight_signals[4][b].sem, 1)
                dve.sem_inc(k.weight_signals[5][b].sem, 1)
            dve.sem_inc(k.expert_signals[1].sem, 2)
            dve.sem_inc(k.expert_signals[3].sem, 2)


def store(k, y):
    stored = k.new_sem("stored")
    with k.nc.Block() as block:
        @block.sync
        def _(sp):
            sp.dma_start(k.dram["y"], y[:]).then_inc(stored.sem, 16)
            sp.wait_ge(stored.sem, 16)


def build(nc, dram):
    with ExitStack() as ctx:
        dram = dict(dram, early_act=nc.dram_tensor("early_act_dram", (I1, P, T), F32, kind="Internal").ap())
        k = Kernel(nc, ctx, dram)
        gain = k.sbuf("gain", [P, 2, KD])
        setup(k)
        signals_of_loops(k)
        ffn(k, "ffn1", 0, k.vec("norm_ffn1"), k.ffn_signals)
        mixer1(k)
        ffn(k, "ffn2", 1, k.vec("norm_ffn2"), k.ffn_signals)
        norm(k, k.vec("norm_final"), None, plain=k.h, summed=True)
        mixer2(k, gain)
        peer(k, gain)
        norm(k, k.vec("final_norm_w_2"), None, plain=k.h)
        store(k, k.h)



def tiles8(w):
    kin, n = w.shape
    return w.reshape(kin // P, P, n // P, P).transpose(2, 1, 0, 3).reshape(n // P, P, kin)


def down_chunks(w):
    c = np.zeros((KD, P, 3 * KD, P), w.dtype)
    c[:, :, :KF] = w.reshape(KF, P, KD, P).transpose(2, 1, 0, 3)
    return c.reshape(KD, P, 3, KD * P).transpose(0, 2, 1, 3).reshape(3 * KD, P, KD * P)


def features(v):
    return v.reshape(-1, P).T


def projection_columns():
    nq, kc, vc, ksl, vsl, kwn, vwn, ng, sq, sk, sv, ga, gb = np.cumsum(
        [0, 512, 128, 128, 128, 128, 128, 128, 24, 512, 64, 64, 1024])
    r = np.arange
    head = lambda base, a: r(base + HD * a, base + HD * (a + 1))
    tiles = [np.r_[head(nq, j), head(nq, 4 + j)] for j in range(4)]
    tiles += [r(ksl, ksl + P), r(kwn, kwn + P)]
    tiles += [np.r_[head(sq, j), head(sq, 4 + j)] for j in range(4)]
    tiles += [np.r_[head(sk, 0), head(sk, 0)]]
    tiles += [np.r_[head(kc, g), head(vc, g)] for g in range(2)]
    tiles += [r(vsl, vsl + P), r(vwn, vwn + P)]
    tiles += [np.r_[head(sv, 0), r(ng, ng + 24), np.full(P - HD - 24, -1)]]
    return np.concatenate(tiles + [r(ga, ga + D), r(gb, gb + D)])


def lay_out(a):
    g = {n: np.asarray(v) for n, v in a.items()}
    first = lambda n: g[n][0]
    out = {"x": g["x"][0].T.reshape(KD, P, T).transpose(1, 0, 2)}
    for n in (1, 2):
        gate, up = tiles8(first(f"ffn{n}_gate")), tiles8(first(f"ffn{n}_up"))
        out[f"ffn{n}_gu"] = np.stack([gate, up], 1).reshape(2 * KF, P, D)
        out[f"ffn{n}_down"] = down_chunks(first(f"ffn{n}_down"))
    w = first("w_in")
    w = np.concatenate([w, np.zeros((D, 1), w.dtype)], 1)[:, projection_columns()]
    tiles = tiles8(w)
    out["w_in"], out["w_in_gates"] = tiles[:PROJ], tiles[PROJ:]
    out["positions"] = g["positions"].astype(np.int32).reshape(1, T)
    w1 = np.concatenate([first(f"cmp_{n}_w1").reshape(32, HD, 256).transpose(1, 0, 2) for n in "kv"])
    out["cmp_w1"] = w1
    w2k, w2v = (first(f"cmp_{n}_w2").reshape(2, P, HD).transpose(1, 0, 2) for n in "kv")
    out["cmp_w2"] = np.concatenate([w2k, w2k, w2v], 2)
    out["cmp_pe"] = np.concatenate([first("cmp_pe_k").T, first("cmp_pe_v").T])
    ab = [first(n).reshape(4, P, KD, P).transpose(2, 1, 0, 3) for n in ("w_branch_a", "w_branch_b")]
    out["w_branch"] = np.concatenate(ab, 2).reshape(KD, P, D)
    out["w_out"] = tiles8(first("w_out"))
    out["ada_w"] = first("ada_w_2").T.reshape(6 * KD, P, D)
    out["cond_rows"] = np.broadcast_to(g["c_2"].reshape(1, D), (P, D))
    tiles = tiles8(first("w_in_2"))
    out["w_in_2"], out["w_in_2_state"] = tiles[:16], tiles[16:]
    out["w_out_2"] = tiles8(first("w_out_2"))
    out["peer_wq"] = tiles8(first("peer_wq_2"))
    out["peer_keys"] = np.stack([first("peer_keys1_2").T, first("peer_keys2_2").T], 1)
    out["peer_u"] = first("peer_u_2").reshape(P, P, KD, P).transpose(0, 3, 2, 1).reshape(P, P, D)
    out["peer_v"] = first("peer_v_2").reshape(P // 8, 8, P, KD, P).transpose(0, 3, 2, 1, 4).reshape(P, P, D)
    for n in ("b_re", "b_im"):
        out["s5_" + n] = first(f"s5_{n}_2").reshape(16, P, 16).transpose(1, 0, 2)
    for n in ("c_re", "c_im"):
        out["s5_" + n] = first(f"s5_{n}_2").transpose(0, 2, 1).reshape(16, P, 16).transpose(1, 0, 2)
    out["glu_w"] = first("s5_glu_w_2").reshape(4, P, 512).transpose(1, 0, 2)
    half = HD // 2
    freq = (np.float32(10000.0) ** (-np.arange(half, dtype=np.float32) / np.float32(half))).astype(np.float32)
    vecs = {n: features(g[n].reshape(-1)) for n in
            ("norm_ffn1", "norm_mix", "norm_ffn2", "norm_final", "norm_mix_w_2", "norm_ffn_w_2",
             "final_norm_w_2", "c_2", "ada_b_2")}
    vecs["lb0"], vecs["lb1"] = (features(g["hg_lower_bounds_2"][i]) for i in range(2))
    vecs["gn"] = features(first("hg_gnorm_w_2"))
    vecs["a_re"], vecs["a_im"] = features(first("s5_a_re_2").reshape(-1)), features(first("s5_a_im_2").reshape(-1))
    vecs["log_dt"] = features(np.repeat(first("s5_log_dt_2"), 64))
    vecs["d_skip"], vecs["glu_b"] = features(first("s5_d_2")), features(first("s5_glu_b_2"))
    vecs["sinks"] = np.broadcast_to(first("swa_sinks"), (P, 8))
    vecs["freq"] = np.tile(freq, P // half).reshape(P, 1)
    out["vecs"] = np.concatenate([vecs[n] for n in VEC], 1)
    return {n: np.ascontiguousarray(v) for n, v in out.items()}


def kernel(**inputs):
    import concourse.bacc as bacc
    from concourse.bass_utils import run_bass_kernel_spmd

    nc = bacc.Bacc("TRN2", target_bir_lowering=False, num_devices=1)
    arrays = lay_out(inputs)
    dram = {n: nc.dram_tensor(f"in_{n}", a.shape, mybir.dt.from_np(a.dtype), kind="ExternalInput").ap()
            for n, a in arrays.items()}
    dram["y"] = nc.dram_tensor("out_y", (P, KD, T), F32, kind="ExternalOutput").ap()
    build(nc, dram)
    r = run_bass_kernel_spmd(nc, [{f"in_{n}": a for n, a in arrays.items()}], core_ids=[0])
    y = r.results[0]["out_y"]
    return np.ascontiguousarray(y.transpose(1, 0, 2).reshape(D, T).T).reshape(1, T, D)
```
